# Optimizing a Trainium2 kernel written in Bass

```python
import math, functools
import jax, jax.numpy as jnp
from jax import lax
import numpy as np
import math

D_MODEL = 1024
BATCH = 1
SEQ = 512
DEPTH = 2

PLE_DIM = 256
N_EVEN = (DEPTH + 1) // 2
N_ODD = DEPTH // 2
A_WIDTH = D_MODEL // 2
A_GROUPS = 4
A_GROUP_DIM = A_WIDTH // A_GROUPS
A_CHUNK = 128
B_HEADS = 4
B_HEAD_DIM = (D_MODEL // 2) // B_HEADS
B_WIDTH = B_HEADS * B_HEAD_DIM
B_CONV = 4
B_CHUNK = 64
C_HEADS = 8
C_HEAD_DIM = D_MODEL // (2 * C_HEADS)
C_VALUE_DIM = 2 * C_HEAD_DIM
Q_BLOCK = 128
D_FF = 4 * D_MODEL
EVEN_IN = 2 * A_WIDTH + 4 * B_WIDTH + 2 * B_HEADS
NORM_EPS = 1e-6
RES_SCALE = 0.5


def rms_norm(x, gain):
    xf = x.astype(jnp.float32)
    y = xf * lax.rsqrt(jnp.mean(xf * xf, axis=-1, keepdims=True) + NORM_EPS)
    return (y * gain.astype(jnp.float32)).astype(x.dtype)

def layer_norm(x, gain):
    xf = x.astype(jnp.float32)
    xc = xf - jnp.mean(xf, axis=-1, keepdims=True)
    y = xc * lax.rsqrt(jnp.mean(xc * xc, axis=-1, keepdims=True) + NORM_EPS)
    return (y * gain.astype(jnp.float32)).astype(x.dtype)

def l2_normalize(x):
    xf = x.astype(jnp.float32)
    return xf * lax.rsqrt(jnp.sum(xf * xf, axis=-1, keepdims=True) + NORM_EPS)

def causal_depthwise_conv(x, w):
    k_len, ch = w.shape
    return lax.conv_general_dilated(
        x, w[:, None, :].astype(x.dtype), window_strides=(1,), padding=[(k_len - 1, 0)],
        dimension_numbers=('NWC', 'WIO', 'NWC'), feature_group_count=ch)

def gmlp_spatial_gate(uv, v_gain, w_s, b_s):
    bsz, seq, _ = uv.shape
    u, v = jnp.split(uv, 2, axis=-1)
    v = v.reshape(bsz, seq // A_CHUNK, A_CHUNK, A_GROUPS, A_GROUP_DIM)
    v = layer_norm(v, v_gain.reshape(A_GROUPS, A_GROUP_DIM))
    causal = jnp.tril(jnp.ones((A_CHUNK, A_CHUNK), dtype=bool))
    w = jnp.where(causal, w_s, 0.0)
    s = jnp.einsum('gts,bnsgc->bntgc', w, v) + b_s.T[None, None, :, :, None]
    return u * s.reshape(bsz, seq, A_WIDTH)

def chunk_gated_delta_rule(q, k, v, g, beta):
    bsz, seq, heads, dk = q.shape
    dv = v.shape[-1]
    c = B_CHUNK
    n = seq // c
    f32 = jnp.float32

    def chunks(t):
        t = t.astype(f32).reshape((bsz, n, c, heads) + t.shape[3:])
        return jnp.moveaxis(t, 3, 1)

    q, k, v, g, beta = chunks(q), chunks(k), chunks(v), chunks(g), chunks(beta)
    gc = jnp.cumsum(g, axis=-1)
    causal = jnp.tril(jnp.ones((c, c), dtype=bool))
    strict = jnp.tril(jnp.ones((c, c), dtype=bool), k=-1)
    diff = gc[..., :, None] - gc[..., None, :]
    decay = jnp.where(causal, jnp.exp(jnp.where(causal, diff, 0.0)), 0.0)
    k_beta = k * beta[..., None]
    v_beta = v * beta[..., None]
    a = jnp.where(strict, jnp.einsum('bhnid,bhnjd->bhnij', k_beta, k) * decay, 0.0)
    t_mat = a + jnp.eye(c, dtype=f32)
    solve = functools.partial(lax.linalg.triangular_solve, left_side=True, lower=True,
                              unit_diagonal=True)
    u = solve(t_mat, v_beta)
    w = solve(t_mat, k_beta * jnp.exp(gc)[..., None])
    qk = jnp.einsum('bhnid,bhnjd->bhnij', q, k) * decay
    q_dec = q * jnp.exp(gc)[..., None]
    k_dec = k * jnp.exp(gc[..., -1:] - gc)[..., None]
    g_last = jnp.exp(gc[..., -1])
    xs = tuple(jnp.moveaxis(t, 2, 0) for t in (q_dec, k_dec, u, w, qk, g_last))

    def step(state, inp):
        q_c, k_c, u_c, w_c, qk_c, gl_c = inp
        v_new = u_c - jnp.einsum('bhck,bhkv->bhcv', w_c, state)
        o_c = (jnp.einsum('bhck,bhkv->bhcv', q_c, state)
               + jnp.einsum('bhij,bhjv->bhiv', qk_c, v_new))
        state = state * gl_c[..., None, None] + jnp.einsum('bhck,bhcv->bhkv', k_c, v_new)
        return state, o_c

    state0 = jnp.zeros((bsz, heads, dk, dv), f32)
    _, o = lax.scan(step, state0, xs)
    return jnp.transpose(o, (1, 0, 3, 2, 4)).reshape(bsz, seq, heads, dv)

def gated_deltanet(qkv, z, beta_logit, a_logit, conv_w, a_log, dt_bias, out_gain):
    bsz, seq, _ = qkv.shape
    qkv = jax.nn.silu(causal_depthwise_conv(qkv, conv_w))
    q, k, v = jnp.split(qkv, 3, axis=-1)
    shp = (bsz, seq, B_HEADS, B_HEAD_DIM)
    q = l2_normalize(q.reshape(shp)) * (B_HEAD_DIM ** -0.5)
    k = l2_normalize(k.reshape(shp))
    v = v.reshape(shp)
    beta = jax.nn.sigmoid(beta_logit.astype(jnp.float32))
    g = -jnp.exp(a_log.astype(jnp.float32)) * jax.nn.softplus(
        a_logit.astype(jnp.float32) + dt_bias.astype(jnp.float32))
    o = chunk_gated_delta_rule(q, k, v, g, beta).astype(qkv.dtype)
    o = rms_norm(o, out_gain) * jax.nn.silu(z.reshape(shp))
    return o.reshape(bsz, seq, B_WIDTH)

def alibi_slopes(heads):
    return 2.0 ** (-8.0 * jnp.arange(1, heads + 1, dtype=jnp.float32) / heads)

def diff_attention(qkv, q_gain, k_gain, lam_params, sub_gain, lam_init):
    bsz, seq, _ = qkv.shape
    q, k, v = jnp.split(qkv, 3, axis=-1)
    q = rms_norm(q.reshape(bsz, seq, C_HEADS, 2, C_HEAD_DIM), q_gain) * (C_HEAD_DIM ** -0.5)
    k = rms_norm(k.reshape(bsz, seq, C_HEADS, 2, C_HEAD_DIM), k_gain)
    v = v.reshape(bsz, seq, C_HEADS, C_VALUE_DIM)
    lp = lam_params.astype(jnp.float32)
    lam = jnp.exp(jnp.sum(lp[0] * lp[1])) - jnp.exp(jnp.sum(lp[2] * lp[3])) + lam_init
    slopes = alibi_slopes(C_HEADS)[None, :, None, None, None]
    nblk = seq // Q_BLOCK
    qb = jnp.moveaxis(q.reshape(bsz, nblk, Q_BLOCK, C_HEADS, 2, C_HEAD_DIM), 1, 0)
    kpos = jnp.arange(seq)

    def attend(args):
        q_blk, blk = args
        qpos = blk * Q_BLOCK + jnp.arange(Q_BLOCK)
        dist = (qpos[:, None] - kpos[None, :]).astype(jnp.float32)
        logits = jnp.einsum('bqhrd,bkhrd->bhrqk', q_blk, k).astype(jnp.float32) - slopes * dist
        logits = jnp.where(dist >= 0, logits, -jnp.inf)
        probs = jax.nn.softmax(logits, axis=-1)
        attn = probs[:, :, 0] - lam * probs[:, :, 1]
        return jnp.einsum('bhqk,bkhe->bqhe', attn.astype(v.dtype), v)

    o = lax.map(attend, (qb, jnp.arange(nblk)))
    o = jnp.moveaxis(o, 0, 1).reshape(bsz, seq, C_HEADS, C_VALUE_DIM)
    o = rms_norm(o, sub_gain) * (1.0 - lam_init)
    return o.reshape(bsz, seq, C_HEADS * C_VALUE_DIM)

def first_inputs(seed: int = 0) -> dict:
    key = jax.random.key(seed)
    ks = jax.random.split(key, 32)
    f32 = jnp.float32

    def normal(k, shape, scale):
        return jax.random.normal(k, shape, f32) * scale

    def gain(k, shape):
        return 1.0 + 0.1 * jax.random.normal(k, shape, f32)

    dt = jnp.exp(jax.random.uniform(ks[9], (N_EVEN, B_HEADS), f32,
                                    minval=math.log(1e-3), maxval=math.log(1e-1)))
    return {
        'x': normal(ks[0], (BATCH, SEQ, D_MODEL), 1.0),
        'p': normal(ks[1], (DEPTH, BATCH, SEQ, PLE_DIM), 1.0),
        'ln_mix_e': gain(ks[2], (N_EVEN, D_MODEL)),
        'w_in_e': normal(ks[3], (N_EVEN, D_MODEL, EVEN_IN), D_MODEL ** -0.5),
        'gmlp_v_gain': gain(ks[4], (N_EVEN, A_WIDTH)),
        'gmlp_ws': normal(ks[5], (N_EVEN, A_GROUPS, A_CHUNK, A_CHUNK), A_CHUNK ** -0.5),
        'gmlp_bs': gain(ks[6], (N_EVEN, A_GROUPS, A_CHUNK)),
        'gdn_conv': normal(ks[7], (N_EVEN, B_CONV, 3 * B_WIDTH), B_CONV ** -0.5),
        'gdn_a_log': jnp.log(jax.random.uniform(ks[8], (N_EVEN, B_HEADS), f32, minval=1.0, maxval=16.0)),
        'gdn_dt_bias': dt + jnp.log(-jnp.expm1(-dt)),
        'gdn_out_gain': gain(ks[10], (N_EVEN, B_HEAD_DIM)),
        'w_out_e': normal(ks[11], (N_EVEN, A_WIDTH + B_WIDTH, D_MODEL), (A_WIDTH + B_WIDTH) ** -0.5 * RES_SCALE),
        'ln_mix_o': gain(ks[12], (N_ODD, D_MODEL)),
        'w_qkv_o': normal(ks[13], (N_ODD, D_MODEL, 3 * C_HEADS * C_VALUE_DIM), D_MODEL ** -0.5),
        'attn_q_gain': gain(ks[14], (N_ODD, C_HEAD_DIM)),
        'attn_k_gain': gain(ks[15], (N_ODD, C_HEAD_DIM)),
        'diff_lambda': normal(ks[16], (N_ODD, 4, C_HEAD_DIM), 0.1),
        'attn_sub_gain': gain(ks[17], (N_ODD, C_VALUE_DIM)),
        'w_out_o': normal(ks[18], (N_ODD, C_HEADS * C_VALUE_DIM, D_MODEL), (C_HEADS * C_VALUE_DIM) ** -0.5 * RES_SCALE),
        'ln_mlp': gain(ks[19], (DEPTH, D_MODEL)),
        'w_mlp1': normal(ks[20], (DEPTH, D_MODEL, D_FF), D_MODEL ** -0.5),
        'w_mlp2': normal(ks[21], (DEPTH, D_FF, D_MODEL), D_FF ** -0.5 * RES_SCALE),
        'ln_ple': gain(ks[22], (DEPTH, D_MODEL)),
        'w_ple_gate': normal(ks[23], (DEPTH, D_MODEL, D_MODEL), D_MODEL ** -0.5),
        'w_ple_proj': normal(ks[24], (DEPTH, PLE_DIM, D_MODEL), PLE_DIM ** -0.5 * RES_SCALE),
    }

def first_block(x, p, ln_mix_e, w_in_e, gmlp_v_gain, gmlp_ws, gmlp_bs, gdn_conv, gdn_a_log,
              gdn_dt_bias, gdn_out_gain, w_out_e, ln_mix_o, w_qkv_o, attn_q_gain, attn_k_gain,
              diff_lambda, attn_sub_gain, w_out_o, ln_mlp, w_mlp1, w_mlp2, ln_ple, w_ple_gate,
              w_ple_proj):
    split_at = [2 * A_WIDTH, 2 * A_WIDTH + 3 * B_WIDTH, 2 * A_WIDTH + 4 * B_WIDTH,
                2 * A_WIDTH + 4 * B_WIDTH + B_HEADS]
    h = x
    for layer in range(DEPTH):
        i = layer // 2
        if layer % 2 == 0:
            hn = rms_norm(h, ln_mix_e[i])
            proj = hn @ w_in_e[i]
            a_uv, b_qkv, b_z, b_beta, b_a = jnp.split(proj, split_at, axis=-1)
            a_out = gmlp_spatial_gate(jax.nn.gelu(a_uv), gmlp_v_gain[i], gmlp_ws[i], gmlp_bs[i])
            b_out = gated_deltanet(b_qkv, b_z, b_beta, b_a, gdn_conv[i], gdn_a_log[i],
                                   gdn_dt_bias[i], gdn_out_gain[i])
            h = h + jnp.concatenate([a_out, b_out], axis=-1) @ w_out_e[i]
        else:
            hn = rms_norm(h, ln_mix_o[i])
            lam_init = 0.8 - 0.6 * math.exp(-0.3 * layer)
            o = diff_attention(hn @ w_qkv_o[i], attn_q_gain[i], attn_k_gain[i], diff_lambda[i],
                               attn_sub_gain[i], lam_init)
            h = h + o @ w_out_o[i]
        hn = rms_norm(h, ln_mlp[layer])
        h = h + jnp.square(jax.nn.relu(hn @ w_mlp1[layer])) @ w_mlp2[layer]
        gate = jax.nn.sigmoid(rms_norm(h, ln_ple[layer]) @ w_ple_gate[layer])
        h = h + (p[layer] @ w_ple_proj[layer]) * gate
    return h


CHUNK = 64
CONV_DIM = D_MODEL // 2
CONV_WIDTH = 3
HG_HEADS = 4
HG_DK = 128
HG_DV = (D_MODEL // 2) // HG_HEADS
HG_FDIM = HG_HEADS * HG_DK
HG_WIDTH = HG_HEADS * HG_DV
SB_HEADS = 16
SB_HEAD_DIM = D_MODEL // SB_HEADS
SB_WIDTH = SB_HEADS * SB_HEAD_DIM
D_FF_2 = 4 * D_MODEL
N_EVEN_2 = (DEPTH + 1) // 2
N_ODD_2 = DEPTH // 2
AB_IN = 3 * CONV_DIM + 2 * HG_FDIM + 2 * HG_WIDTH
AB_MIX = CONV_DIM + HG_WIDTH
AB_SPLITS = [CONV_DIM, 2 * CONV_DIM, 3 * CONV_DIM,
             3 * CONV_DIM + HG_FDIM, 3 * CONV_DIM + 2 * HG_FDIM,
             3 * CONV_DIM + 2 * HG_FDIM + HG_WIDTH]
EPS = 1e-6


def rms_norm_2(x, g):
    xf = x.astype(jnp.float32)
    y = xf * lax.rsqrt(jnp.mean(xf * xf, axis=-1, keepdims=True) + EPS)
    return (y * g.astype(jnp.float32)).astype(x.dtype)

def causal_depthwise_conv_2(u, w):
    width, ch = w.shape
    return lax.conv_general_dilated(
        u, w[:, None, :], window_strides=(1,), padding=[(width - 1, 0)],
        dimension_numbers=('NWC', 'WIO', 'NWC'), feature_group_count=ch)

def hgrn2_chunkwise(q, k, v, log_f):
    B, S, H, Dk = q.shape
    Dv = v.shape[-1]
    n = S // CHUNK

    def to_chunks(t):
        return t.reshape(B, n, CHUNK, H, t.shape[-1]).transpose(1, 0, 3, 2, 4)

    qc, kc, vc, gc = to_chunks(q), to_chunks(k), to_chunks(v), to_chunks(log_f)
    bc = jnp.cumsum(gc, axis=3)
    causal = jnp.tril(jnp.ones((CHUNK, CHUNK), dtype=bool))

    def step(state, inp):
        q_, k_, v_, b_ = inp
        inter = jnp.einsum('bhtk,bhkv->bhtv', q_ * jnp.exp(b_), state)
        diff = jnp.where(causal[None, None, :, :, None],
                         b_[:, :, :, None, :] - b_[:, :, None, :, :], -jnp.inf)
        decay = jnp.exp(diff)
        scores = jnp.einsum('bhtk,bhsk,bhtsk->bhts', q_, k_, decay)
        intra = jnp.einsum('bhts,bhsv->bhtv', scores, v_)
        b_last = b_[:, :, -1:, :]
        new_state = (jnp.exp(b_last[:, :, 0, :])[..., None] * state
                     + jnp.einsum('bhsk,bhsv->bhkv', k_ * jnp.exp(b_last - b_), v_))
        return new_state, inter + intra

    init = jnp.zeros((B, H, Dk, Dv), jnp.float32)
    _, out = lax.scan(step, init, (qc, kc, vc, bc))
    return out.transpose(1, 0, 3, 2, 4).reshape(B, S, H, Dv)

def stick_breaking_attention(q, k, v):
    S = q.shape[2]
    scale = SB_HEAD_DIM ** -0.5
    outs = []
    for blk in range(S // Q_BLOCK):
        q0 = blk * Q_BLOCK
        end = q0 + Q_BLOCK
        qb = q[:, :, q0:end]
        kb = k[:, :, :end]
        vb = v[:, :, :end]
        z = jnp.einsum('bhqd,bhkd->bhqk', qb, kb) * scale
        qpos = q0 + jnp.arange(Q_BLOCK)
        kpos = jnp.arange(end)
        mask = (kpos[None, :] < qpos[:, None])[None, None]
        log_beta = jax.nn.log_sigmoid(z)
        log_one_minus = jnp.where(mask, log_beta - z, 0.0)
        later = lax.cumsum(log_one_minus, axis=3, reverse=True) - log_one_minus
        w = jnp.where(mask, jnp.exp(log_beta + later), 0.0)
        outs.append(jnp.einsum('bhqk,bhkd->bhqd', w, vb))
    return jnp.concatenate(outs, axis=2)

def mixer_conv_hgrn(h, w_in, conv_w, hg_norm, lower_bound, w_out):
    B, S, _ = h.shape
    u = h @ w_in
    a_b, a_c, a_h, hq, hf, hi, hg = jnp.split(u, AB_SPLITS, axis=-1)
    y_a = a_b * causal_depthwise_conv_2(a_c * a_h, conv_w)
    f = lower_bound + (1.0 - lower_bound) * jax.nn.sigmoid(hf.astype(jnp.float32))
    log_f = jnp.log(f)
    k_in = 1.0 - f
    heads_k = lambda t: t.reshape(B, S, HG_HEADS, HG_DK)
    o = hgrn2_chunkwise(heads_k(hq.astype(jnp.float32)), heads_k(k_in), 
                        hi.astype(jnp.float32).reshape(B, S, HG_HEADS, HG_DV), heads_k(log_f))
    o = rms_norm_2(o, hg_norm.reshape(HG_HEADS, HG_DV))
    y_b = (o.reshape(B, S, HG_WIDTH) * jax.nn.silu(hg.astype(jnp.float32))).astype(h.dtype)
    return jnp.concatenate([y_a, y_b], axis=-1) @ w_out

def mixer_stick_breaking(h, w_qkv, q_norm, k_norm, w_out):
    B, S, _ = h.shape
    qkv = (h @ w_qkv).reshape(B, S, 3, SB_HEADS, SB_HEAD_DIM)
    q = rms_norm_2(qkv[:, :, 0], q_norm)
    k = rms_norm_2(qkv[:, :, 1], k_norm)
    v = qkv[:, :, 2]
    to_bhsd = lambda t: t.astype(jnp.float32).transpose(0, 2, 1, 3)
    o = stick_breaking_attention(to_bhsd(q), to_bhsd(k), to_bhsd(v))
    o = o.transpose(0, 2, 1, 3).reshape(B, S, SB_WIDTH).astype(h.dtype)
    return o @ w_out

def second_inputs(seed: int = 0) -> dict:
    key = jax.random.key(seed)
    ks = jax.random.split(key, 20)
    nrm = lambda k, shape, s: jax.random.normal(k, shape, jnp.float32) * s
    gain = lambda k, shape: 1.0 + 0.02 * jax.random.normal(k, shape, jnp.float32)
    return {
        "x": nrm(ks[0], (BATCH, SEQ, D_MODEL), 1.0),
        "c": nrm(ks[1], (BATCH, D_MODEL), 1.0),
        "ada_w": nrm(ks[2], (DEPTH, D_MODEL, 6 * D_MODEL), 0.5 * D_MODEL ** -0.5),
        "ada_b": nrm(ks[3], (DEPTH, 6 * D_MODEL), 0.02),
        "norm_mix": gain(ks[4], (DEPTH, D_MODEL)),
        "norm_mlp": gain(ks[5], (DEPTH, D_MODEL)),
        "w_in_ab": nrm(ks[6], (N_EVEN_2, D_MODEL, AB_IN), D_MODEL ** -0.5),
        "conv_w": nrm(ks[7], (N_EVEN_2, CONV_WIDTH, CONV_DIM), CONV_WIDTH ** -0.5),
        "hg_norm": gain(ks[8], (N_EVEN_2, HG_WIDTH)),
        "lb_logits": nrm(ks[9], (DEPTH + 1, HG_FDIM), 0.1),
        "w_out_ab": nrm(ks[10], (N_EVEN_2, AB_MIX, D_MODEL), AB_MIX ** -0.5),
        "w_qkv": nrm(ks[11], (N_ODD_2, D_MODEL, 3 * SB_WIDTH), D_MODEL ** -0.5),
        "q_norm": gain(ks[12], (N_ODD_2, SB_HEAD_DIM)),
        "k_norm": gain(ks[13], (N_ODD_2, SB_HEAD_DIM)),
        "w_out_c": nrm(ks[14], (N_ODD_2, SB_WIDTH, D_MODEL), SB_WIDTH ** -0.5),
        "mlp_w1": nrm(ks[15], (DEPTH, D_MODEL, D_FF_2), D_MODEL ** -0.5),
        "mlp_w2": nrm(ks[16], (DEPTH, D_FF_2, D_MODEL), D_FF_2 ** -0.5),
    }

def second_block(x, c, ada_w, ada_b, norm_mix, norm_mlp, w_in_ab, conv_w, hg_norm,
              lb_logits, w_out_ab, w_qkv, q_norm, k_norm, w_out_c, mlp_w1, mlp_w2):
    c_act = jax.nn.silu(c)
    lower_bounds = jnp.cumsum(jax.nn.softmax(lb_logits.astype(jnp.float32), axis=0), axis=0)
    for layer in range(DEPTH):
        mod = c_act @ ada_w[layer] + ada_b[layer]
        shift1, scale1, gate1, shift2, scale2, gate2 = jnp.split(mod[:, None, :], 6, axis=-1)
        h = rms_norm_2(x, norm_mix[layer]) * (1.0 + scale1) + shift1
        j = layer // 2
        if layer % 2 == 0:
            y = mixer_conv_hgrn(h, w_in_ab[j], conv_w[j], hg_norm[j],
                                lower_bounds[layer], w_out_ab[j])
        else:
            y = mixer_stick_breaking(h, w_qkv[j], q_norm[j], k_norm[j], w_out_c[j])
        x = x + gate1 * y
        h = rms_norm_2(x, norm_mlp[layer]) * (1.0 + scale2) + shift2
        x = x + gate2 * (jnp.square(jax.nn.relu(h @ mlp_w1[layer])) @ mlp_w2[layer])
    return x


def setup_inputs(seed=0):
    out = dict(first_inputs(seed))
    for name, value in second_inputs(seed + 1).items():
        if name != "x":
            out[name + "_2"] = value
    return out


def reference(
    x, p, ln_mix_e, w_in_e, gmlp_v_gain, gmlp_ws, gmlp_bs, gdn_conv, gdn_a_log, gdn_dt_bias,
    gdn_out_gain, w_out_e, ln_mix_o, w_qkv_o, attn_q_gain, attn_k_gain, diff_lambda,
    attn_sub_gain, w_out_o, ln_mlp, w_mlp1, w_mlp2, ln_ple, w_ple_gate, w_ple_proj, c_2,
    ada_w_2, ada_b_2, norm_mix_2, norm_mlp_2, w_in_ab_2, conv_w_2, hg_norm_2, lb_logits_2,
    w_out_ab_2, w_qkv_2, q_norm_2, k_norm_2, w_out_c_2, mlp_w1_2, mlp_w2_2,
):
    x = first_block(
        x, p, ln_mix_e, w_in_e, gmlp_v_gain, gmlp_ws, gmlp_bs, gdn_conv, gdn_a_log, gdn_dt_bias,
        gdn_out_gain, w_out_e, ln_mix_o, w_qkv_o, attn_q_gain, attn_k_gain, diff_lambda,
        attn_sub_gain, w_out_o, ln_mlp, w_mlp1, w_mlp2, ln_ple, w_ple_gate, w_ple_proj,
    )
    return second_block(
        x, c_2, ada_w_2, ada_b_2, norm_mix_2, norm_mlp_2, w_in_ab_2, conv_w_2, hg_norm_2,
        lb_logits_2, w_out_ab_2, w_qkv_2, q_norm_2, k_norm_2, w_out_c_2, mlp_w1_2, mlp_w2_2,
    )


_drawn_inputs = setup_inputs


def setup_inputs(seed=0):
    import zlib

    import numpy as np

    out = dict(_drawn_inputs(seed))
    spreads = {}
    factors = {'gmlp_v_gain': 3.249,
     'attn_q_gain': 2.854,
     'attn_k_gain': 3.046,
     'ln_ple': 4.688,
     'norm_mix_2': 6.713,
     'norm_mlp_2': 46.01,
     'hg_norm_2': 200.0,
     'lb_logits_2': 8.0,
     'q_norm_2': 200.0,
     'k_norm_2': 200.0,
     'w_qkv_2': 8.0,
     'w_out_c_2': 8.0}
    for name, (base, spread) in spreads.items():
        noise = np.random.default_rng([zlib.crc32(name.encode()), seed]).standard_normal(out[name].shape)
        drawn = base * np.exp(spread * noise) if base else spread * noise
        out[name] = __import__('jax').numpy.asarray(drawn.astype(out[name].dtype))
    for name, factor in factors.items():
        out[name] = (out[name] * factor).astype(out[name].dtype)
    return out
```

```python
import math
from contextlib import ExitStack

import concourse.bass as bass
from concourse import mybir

F32 = mybir.dt.float32
F32R = mybir.dt.float32r
I32 = mybir.dt.int32
U32 = mybir.dt.uint32
ALU = mybir.AluOpType
ACT = mybir.ActivationFunctionType
AX_X = mybir.AxisListType.X

P = 128
T = 512
NT = T // P
D = 1024
ND = D // P
DFF = 4096
EPS = 1e-6
BIG = 1e34
LAM_INIT = 0.8 - 0.6 * math.exp(-0.3)
LEVELS = 7


class Steps:

    def __init__(self, sem, names):
        self.sem, self.names, self.n = sem, list(names), 0
        assert len(set(self.names)) == len(self.names)

    def __call__(self, name):
        assert self.names[self.n % len(self.names)] == name, (self.names[self.n % len(self.names)], name)
        self.n += 1
        return self.sem, 1

    def at(self, unit, name):
        return self.sem, unit * len(self.names) + self.names.index(name) + 1

    def before(self, unit):
        return self.sem, unit * len(self.names)


def vector_rows():
    rows, at = [], 0
    index = {}
    for name, count in [("ln_mix_e", ND), ("ln_mix_o", ND), ("ln_mlp", 2 * ND), ("ln_ple", 2 * ND),
                        ("gmlp_v_gain", 4), ("gdn_out_gain", 1), ("gdn_conv", 48), ("attn_sub_gain", 1),
                        ("attn_q_gain", 1), ("attn_k_gain", 1),
                        ("norm_mix_2", 2 * ND), ("norm_mlp_2", 2 * ND), ("c_2", ND), ("hg_norm_2", 4),
                        ("conv_w_2", 12), ("lb_logits_2", 12), ("q_norm_2", 1), ("k_norm_2", 1),
                        ("ada_b_2", 96)]:
        if at % P + count > P:
            at += P - at % P
        index[name] = at
        rows.append((name, at, count))
        at += count
    return rows, index, -(-at // P)


def program(nc: bass.Bass, dram, out, upto="end"):
    rows, col, n_tables = vector_rows()
    ctx = ExitStack()
    with ctx:
        def sb(name, shape, dt=F32):
            return ctx.enter_context(nc.sbuf_tensor(name, shape, dt))

        def sem(name):
            return ctx.enter_context(nc.semaphore(name))

        h = sb("h", [P, ND, T])
        x_hi = sb("x_hi", [P, ND, T], F32R)
        x_lo = sb("x_lo", [P, ND, T], F32R)
        m_hi = sb("m_hi", [P, ND, T], F32R)
        m_lo = sb("m_lo", [P, ND, T], F32R)
        w_raw = sb("w_raw", [P, 4, ND, P])
        w_hi = sb("w_hi", [P, 4, ND, P], F32R)
        w_lo = sb("w_lo", [P, 4, ND, P], F32R)
        sq = sb("sq", [P, 2, T])
        rb = sb("rb", [P, 2, T])
        tt = sb("tt", [P, 3, T])
        ident = sb("ident", [P, P])
        ones = sb("ones", [P, P])
        ones64 = sb("ones64", [P, P])
        upper = sb("upper", [P, P])
        upper_s = sb("upper_s", [P, P])
        lower_s = sb("lower_s", [P, P])
        level = sb("level", [P, LEVELS, P])
        level0_low = sb("level0_low", [P, P])
        vt = sb("vt", [P, n_tables * P])
        idx = sb("idx", [P, P])
        small = sb("small", [P, 96])
        mod = sb("mod", [P, 96])
        mod_gain = sb("mod_gain", [P, 4 * ND])
        beta_nat = sb("beta_nat", [P, NT, 4])
        g_nat = sb("g_nat", [P, NT, 4])
        gc_nat = sb("gc_nat", [P, NT, 4])
        ps = [ctx.enter_context(nc.psum_tensor(f"ps{i}", [P, T], F32)) for i in range(8)]

        w_load = [sem(f"w_load{s}") for s in range(4)]
        w_cut_hi = sem("w_cut_hi")
        w_ready = sem("w_ready")
        mm_done = sem("mm_done")
        bank_free = [sem(f"bank_free{b}") for b in range(2)]
        phase_end = {e: sem(f"phase_end_{e}") for e in ("pe", "act", "dve")}

        def loaded(q, j):
            return w_load[j], 16 * q + 16

        def ready(q, j):
            return w_ready, 4 * q + j + 1

        def done(q, j):
            return mm_done, 4 * q + j + 1

        def freed(q, j):
            return bank_free[j % 2], 2 * q + j // 2 + 1

        class Phases:

            def __init__(self, eng, me):
                self.eng, self.me, self.n = eng, me, 0

            def enter(self):
                if self.n:
                    for e, s in phase_end.items():
                        if e != self.me:
                            self.eng.wait_ge(s, self.n)

            def leave(self):
                self.n += 1
                self.eng.drain().then_inc(phase_end[self.me], 1)

        quads, n_quads = {}, 0
        for name, count in [("gmlp", 2), ("delta", 4), ("out_e", 2), ("mlp0", 16), ("ple0", 2),
                            ("attn", 6), ("out_o", 2), ("mlp1", 16), ("ple1", 2),
                            ("conv", 3), ("hgrn", 4), ("out_ab", 2), ("mlp2", 16),
                            ("stick", 6), ("out_c", 2), ("mlp3", 16)]:
            quads[name] = n_quads
            n_quads += count
            if name == upto:
                break
        names = list(quads)

        def has(name):
            return name in quads

        mlp_w = [(dram["w_mlp1"][0], dram["w_mlp2"][0]), (dram["w_mlp1"][1], dram["w_mlp2"][1]),
                 (dram["mlp_w1_2"][0], dram["mlp_w2_2"][0]), (dram["mlp_w1_2"][1], dram["mlp_w2_2"][1])]
        proj_w = {"out_e": dram["w_out_e"][0], "out_o": dram["w_out_o"][0], "out_ab": dram["w_out_ab_2"][0],
                  "out_c": dram["w_out_c_2"][0], "ple0": dram["w_ple_gate"][0], "ple1": dram["w_ple_gate"][1]}

        gates_w = sb("gates_w", [P, ND, 8])
        gates_b = sb("gates_b", [P, 8])
        x_load, small_load, iota_done = sem("x_load"), sem("small_load"), sem("iota_done")
        ple_load = sem("ple_load")
        ada_load = [sem(f"ada_load{i}") for i in range(4)]
        out_sent = sem("out_sent")

        lam = small[:, 0:1]
        neg_lam = small[:, 1:2]
        q_gain_o = small[:, 2:3]
        sub_gain = small[:, 3:4]
        q_gain_s = small[:, 4:5]
        lb = small[:, 8:12]
        one_minus_lb = small[:, 12:16]
        neg_exp_a = small[:, 16:20]
        c_silu = small[:, 24:32]
        eps_col = small[:, 32:33]

        scratch_size = 26 * T
        arena = sb("arena", [P, scratch_size])
        arena_at = [0]

        def take(shape):
            n = int(math.prod(shape))
            a = arena[:, arena_at[0]:arena_at[0] + n]
            arena_at[0] += n
            assert arena_at[0] <= scratch_size, arena_at
            if len(shape) == 2:
                a = a.rearrange("p (a b) -> p a b", b=shape[1])
            if len(shape) == 3:
                a = a.rearrange("p (a b c) -> p a b c", b=shape[1], c=shape[2])
            return a

        def blocks(a):
            return a.rearrange("p (b t) -> p b t", t=P)

        def over_blocks(mask):
            return mask.unsqueeze(1).to_broadcast([P, NT, P])

        x_in = take([NT, D])
        ada_w = take([4, D])
        ada_acc = take([2, D])
        table_in = take([n_tables, P])
        lam_in = take([4, 64])
        s_idx = take([P]).bitcast(I32)
        t_idx = take([P]).bitcast(I32)
        s_xor_t = take([P])
        arena_at[0] = scratch_size - 3 * T
        gmlp_ws = take([4, P])
        gmlp_wt = take([4, P])
        gmlp_bs = take([4, P])

        def transposed_rows(name):
            return dram[name].rearrange("l (n p) -> (l n) p", p=P)

        row_views = {
            "ln_mix_e": transposed_rows("ln_mix_e"), "ln_mix_o": transposed_rows("ln_mix_o"),
            "ln_mlp": transposed_rows("ln_mlp"), "ln_ple": transposed_rows("ln_ple"),
            "gmlp_v_gain": transposed_rows("gmlp_v_gain"), "gdn_out_gain": dram["gdn_out_gain"],
            "gdn_conv": dram["gdn_conv"].rearrange("l t (n p) -> (l t n) p", p=P),
            "attn_sub_gain": dram["attn_sub_gain"],
            "norm_mix_2": transposed_rows("norm_mix_2"), "norm_mlp_2": transposed_rows("norm_mlp_2"),
            "c_2": transposed_rows("c_2"), "hg_norm_2": transposed_rows("hg_norm_2"),
            "conv_w_2": dram["conv_w_2"].rearrange("l t (n p) -> (l t n) p", p=P),
            "lb_logits_2": transposed_rows("lb_logits_2"),
            "ada_b_2": transposed_rows("ada_b_2"),
        }
        doubled = {"attn_q_gain": "attn_q_gain", "attn_k_gain": "attn_k_gain",
                   "q_norm_2": "q_norm_2", "k_norm_2": "k_norm_2"}

        def weight_chunk(sp, q, j, src):
            if not (isinstance(q, int) and q == 0):
                sp.wait_ge(*ready(q - 1, j))
            sp.dma_start(w_raw[:, j, :, :], src.rearrange("(k p) n -> p k n", p=P)).then_inc(w_load[j], 16)

        def stream(sp):
            sp_square(sp, "gmlp", lambda c: dram["w_in_e"][0][:, bass.ds((c % 2) * 512 + (c // 2) * P, P)], 8)
            if has("delta"):
                with sp.Fori(0, 4) as head:
                    for j in range(4):
                        weight_chunk(sp, quads["delta"] + head, j,
                                     dram["w_in_e"][0][:, bass.ds(head * P + (1024 + 512 * j), P)])
            for name in names:
                if name in proj_w:
                    with sp.Fori(0, 2) as i:
                        for j in range(4):
                            weight_chunk(sp, quads[name] + i, j, proj_w[name][:, bass.ds(i * 512 + j * P, P)])
                elif name.startswith("mlp"):
                    w1, w2 = mlp_w[int(name[3])]
                    with sp.Fori(0, 4) as i:
                        for n in range(8):
                            weight_chunk(sp, quads[name] + 4 * i + n // 4, n % 4,
                                         w1[:, bass.ds(i * 1024 + n * P, P)])
                        for n in range(8):
                            weight_chunk(sp, quads[name] + 4 * i + 2 + n // 4, n % 4,
                                         w2[bass.ds(i * 1024, 1024), n * P:(n + 1) * P])
                elif name in ("attn", "stick"):
                    w = dram["w_qkv_o"][0] if name == "attn" else dram["w_qkv_2"][0]
                    with sp.Fori(0, 2) as i:
                        for c in range(12):
                            weight_chunk(sp, quads[name] + 3 * i + c // 4, c % 4,
                                         w[:, bass.ds(i * 512 + (c // 3) * P + (c % 3) * 1024, P)])
                elif name == "conv":
                    sp_square(sp, "conv", lambda c: dram["w_in_ab_2"][0][:, bass.ds((c % 3) * 512 + (c // 3) * P, P)], 12)
                elif name == "hgrn":
                    with sp.Fori(0, 4) as head:
                        for j in range(4):
                            weight_chunk(sp, quads["hgrn"] + head, j,
                                         dram["w_in_ab_2"][0][:, bass.ds(head * P + (1536 + 512 * j), P)])

        def sp_square(sp, name, src, count):
            for c in range(count):
                weight_chunk(sp, quads[name] + c // 4, c % 4, src(c))

        def cut_hi(q, j):
            nc.gpsimd.tensor_copy(w_hi[:, j, :, :], w_raw[:, j, :, :]).then_inc(w_cut_hi, 1)

        def cut_lo(pool, q, j):
            pool.wait_ge(w_cut_hi, 4 * q + j + 1)
            nc.gpsimd.tensor_tensor(w_lo[:, j, :, :], w_raw[:, j, :, :], w_hi[:, j, :, :].bitcast(F32),
                                    ALU.subtract).then_inc(w_ready, 1)

        def cut_stream(pool):
            for j in range(4):
                pool.wait_ge(*loaded(0, j))
                if j:
                    cut_lo(pool, 0, j - 1)
                cut_hi(0, j)
            with pool.Fori(1, n_quads) as q:
                for j in range(4):
                    pool.wait_ge(*loaded(q, j))
                    pool.wait_ge(*done(q - 1, j))
                    if j:
                        cut_lo(pool, q, j - 1)
                    else:
                        cut_lo(pool, q - 1, 3)
                    cut_hi(q, j)
            cut_lo(pool, n_quads - 1, 3)

        def dense(pe, q, j, hi, lo, rhs_ready=None):
            pe.wait_ge(*ready(q, j))
            if not (isinstance(q, int) and q == 0 and j < 2):
                pe.wait_ge(bank_free[j % 2], 2 * q + j // 2)
            bank = ps[j % 2]
            for k in range(ND):
                if rhs_ready is not None:
                    pe.wait_ge(*rhs_ready(k))
                nc.tensor.matmul(bank[:, :], w_hi[:, j, k, :], hi[:, k, :], start=(k == 0), stop=False)
                nc.tensor.matmul(bank[:, :], w_hi[:, j, k, :], lo[:, k, :], start=False, stop=False)
                last = nc.tensor.matmul(bank[:, :], w_lo[:, j, k, :], hi[:, k, :], start=False, stop=(k == ND - 1))
            last.then_inc(mm_done, 1)

        setup_dve = sem("setup_dve")
        consts_ready = sem("consts_ready")
        x_turned, x_copied = sem("x_turned"), sem("x_copied")
        table_turned, table_copied = sem("table_turned"), sem("table_copied")
        ws_turned, ws_copied = sem("ws_turned"), sem("ws_copied")
        acted = sem("setup_acted")
        for_act = sem("setup_for_act")
        ada_summed, ada_turned = sem("ada_summed"), sem("ada_turned")
        ada_read = sem("ada_read")
        ada_parts = [(layer, part) for layer in range(2) for part in range(6)]

        def setup_sync(sp):
            for b in range(NT):
                sp.dma_start(x_in[:, b, :], dram["x"][0][b * P:(b + 1) * P, :]).then_inc(x_load, 16)

        def setup_loads(act):
            n = 0

            def load(dst, src):
                nonlocal n
                act.dma_start(dst, src).then_inc(small_load, 16)
                n += 16
            for name, at, count in rows:
                t, r = divmod(at, P)
                if name in doubled:
                    load(table_in[r:r + 1, t, 0:64], dram[name])
                    load(table_in[r:r + 1, t, 64:128], dram[name])
                else:
                    load(table_in[r:r + count, t, :], row_views[name])
            load(lam_in[:, :, :], dram["diff_lambda"].to_broadcast([P, 4, 64]))
            load(gates_b[:, 0:4], dram["gdn_a_log"].to_broadcast([P, 4]))
            load(gates_b[:, 4:8], dram["gdn_dt_bias"].to_broadcast([P, 4]))
            load(gmlp_ws[:, :, :], dram["gmlp_ws"][0].rearrange("g t s -> t g s"))
            load(gmlp_bs[:, :, :], dram["gmlp_bs"].to_broadcast([P, 4, P]))
            with nc.allow_non_contiguous_dma(reason="eight columns of w_in_e"):
                load(gates_w[:, :, :], dram["w_in_e"][0].rearrange("(k p) n -> p k n", p=P)[:, :, 3072:3080])
            return n

        rows_in_table = [max(at + n - t * P for _, at, n in rows if at // P == t) for t in range(n_tables)]
        n_small = 16 * (len(rows) + 4 + 6)
        ADA_TURN = 8

        def ada_loads(sp):
            n = 0
            for layer, part in ada_parts:
                for k in range(ND):
                    if n >= 4:
                        sp.wait_ge(ada_read, n - 3)
                    sp.dma_start(ada_w[:, n % 4, :],
                                 dram["ada_w_2"][layer][k * P:(k + 1) * P, part * D:(part + 1) * D]
                                 ).then_inc(ada_load[n % 4], 16)
                    n += 1

        def setup_gpsimd(pool):
            nc.gpsimd.iota(idx[:, :], [[1, P]], base=0, channel_multiplier=-1,
                           allow_small_or_imprecise_dtypes=True).then_inc(iota_done, 1)
            nc.gpsimd.iota(s_idx, [[0, P]], base=0, channel_multiplier=1).then_inc(iota_done, 1)
            nc.gpsimd.iota(t_idx, [[1, P]], base=0, channel_multiplier=0).then_inc(iota_done, 1)
            pool.wait_ge(table_copied, 1)

        def setup_scalar(act):
            setup_loads(act)
            for n in range(8):
                act.wait_ge(x_turned, n + 1)
                nc.scalar.activation(h[:, n, :], ps[2 + n % 2][:, :], ACT.Copy).then_inc(x_copied, 1)
            act.wait_ge(small_load, n_small)
            nc.scalar.activation(neg_exp_a, gates_b[:, 0:4], ACT.Exp).then_inc(acted, 1)
            act.wait_ge(for_act, 1)
            nc.scalar.activation(small[:, 40:42], small[:, 38:40], ACT.Exp).then_inc(acted, 1)
            act.wait_ge(for_act, 2)
            nc.scalar.activation(small[:, 56:68], small[:, 44:56], ACT.Exp).then_inc(acted, 1)
            nc.scalar.activation(c_silu, vt[:, col["c_2"]:col["c_2"] + ND], ACT.Silu).then_inc(acted, 1)

        def setup_tensor(pe):
            pe.wait_ge(consts_ready, 1)
            pe.wait_ge(small_load, n_small)
            for t in range(n_tables):
                r = rows_in_table[t]
                last = nc.tensor.transpose(ps[4][:, t * P:t * P + r], table_in[0:r, t, :], ident[0:r, 0:r])
            last.then_inc(table_turned, 1)
            for g in range(4):
                last = nc.tensor.transpose(ps[5][:, g * P:(g + 1) * P], gmlp_ws[:, g, :], ident[:, :])
            last.then_inc(ws_turned, 1)
            pe.wait_ge(x_load, 16 * NT)
            for n in range(ND):
                if n >= 2:
                    pe.wait_ge(x_copied, n - 1)
                for b in range(NT):
                    last = nc.tensor.transpose(ps[2 + n % 2][:, b * P:(b + 1) * P], x_in[:, b, n * P:(n + 1) * P],
                                               ident[:, :])
                last.then_inc(x_turned, 1)
            for u in range(len(ada_parts)):
                pe.wait_ge(ada_summed, u + 1)
                for n in range(8):
                    last = nc.tensor.matmul(ps[6][:, u * 8 + n:u * 8 + n + 1], ada_acc[:, u % 2, n * P:(n + 1) * P],
                                            ones[:, 0:1], start=True, stop=True)
                last.then_inc(ada_turned, 1)

        def setup_vector(v):
            chain = [0]

            def link(ins):
                chain[0] += 1
                ins.then_inc(setup_dve, 1)
                v.wait_ge(setup_dve, chain[0])

            link(nc.vector.memset(ones[:, :], 1.0))
            link(nc.vector.memset(small[:, :], 0.0))
            link(nc.vector.memset(eps_col, EPS))
            v.wait_ge(iota_done, 3)
            link(nc.vector.tensor_scalar(ident[:, :], idx[:, :], 0.0, None, ALU.is_equal))
            link(nc.vector.tensor_scalar(upper[:, :], idx[:, :], 0.0, None, ALU.is_ge))
            link(nc.vector.tensor_scalar(upper_s[:, :], idx[:, :], 0.0, None, ALU.is_gt))
            link(nc.vector.tensor_scalar(lower_s[:, :], idx[:, :], 0.0, None, ALU.is_lt))
            link(nc.vector.tensor_tensor(t_idx, s_idx, t_idx, ALU.bitwise_xor))
            link(nc.vector.tensor_copy(s_xor_t, t_idx))
            link(nc.vector.tensor_scalar(ones64[:, :], s_xor_t, 64.0, None, ALU.is_lt))
            for lv in range(LEVELS):
                link(nc.vector.tensor_scalar(level[:, lv, :], s_xor_t, float(2 ** (lv + 1)), None, ALU.is_lt))
            for lv in range(LEVELS - 1, 0, -1):
                link(nc.vector.tensor_tensor(level[:, lv, :], level[:, lv, :], level[:, lv - 1, :], ALU.subtract))
            link(nc.vector.tensor_tensor(level0_low[:, :], level[:, 0, :], lower_s[:, :], ALU.mult))
            for lv in range(LEVELS):
                link(nc.vector.tensor_tensor(level[:, lv, :], level[:, lv, :], upper_s[:, :], ALU.mult))
            nc.vector.tensor_copy(small[:, 33:34], ones[:, 0:1]).then_inc(consts_ready, 1)

            v.wait_ge(table_turned, 1)
            for t in range(n_tables):
                s = slice(t * P, t * P + rows_in_table[t])
                last = nc.vector.tensor_copy(vt[:, s], ps[4][:, s])
            last.then_inc(table_copied, 1)
            v.wait_ge(table_copied, 1)
            v.wait_ge(ws_turned, 1)
            link(nc.vector.tensor_tensor(gmlp_wt[:, :, :], blocks(ps[5][:, :]), over_blocks(upper[:, :]), ALU.mult))

            for i in range(2):
                link(nc.vector.tensor_tensor(lam_in[:, 2 * i, :], lam_in[:, 2 * i, :], lam_in[:, 2 * i + 1, :], ALU.mult))
                link(nc.vector.tensor_reduce(small[:, 38 + i:39 + i], lam_in[:, 2 * i, :], AX_X, ALU.add))
            nc.vector.tensor_copy(small[:, 34:35], ones[:, 0:1]).then_inc(for_act, 1)
            lg = [vt[:, col["lb_logits_2"] + 4 * i:col["lb_logits_2"] + 4 * i + 4] for i in range(3)]
            link(nc.vector.tensor_tensor(small[:, 68:72], lg[0], lg[1], ALU.max))
            link(nc.vector.tensor_tensor(small[:, 68:72], small[:, 68:72], lg[2], ALU.max))
            for i in range(3):
                link(nc.vector.tensor_tensor(small[:, 44 + 4 * i:48 + 4 * i], lg[i], small[:, 68:72], ALU.subtract))
            nc.vector.tensor_copy(small[:, 35:36], ones[:, 0:1]).then_inc(for_act, 1)
            v.wait_ge(acted, 4)
            link(nc.vector.tensor_scalar(neg_exp_a, neg_exp_a, -1.0, None, ALU.mult))
            link(nc.vector.tensor_scalar(lam, small[:, 40:41], small[:, 41:42], LAM_INIT, ALU.subtract, ALU.add))
            link(nc.vector.tensor_scalar(neg_lam, lam, -1.0, None, ALU.mult))
            link(nc.vector.tensor_tensor(small[:, 68:72], small[:, 56:60], small[:, 60:64], ALU.add))
            link(nc.vector.tensor_tensor(small[:, 68:72], small[:, 68:72], small[:, 64:68], ALU.add))
            link(nc.vector.reciprocal(small[:, 72:76], small[:, 68:72]))
            link(nc.vector.tensor_tensor(lb, small[:, 56:60], small[:, 72:76], ALU.mult))
            link(nc.vector.tensor_scalar(one_minus_lb, lb, -1.0, 1.0, ALU.mult, ALU.add))
            link(nc.vector.tensor_scalar(q_gain_o, vt[:, col["attn_q_gain"]:col["attn_q_gain"] + 1], 0.125, None, ALU.mult))
            link(nc.vector.tensor_scalar(q_gain_s, vt[:, col["q_norm_2"]:col["q_norm_2"] + 1], 0.125, None, ALU.mult))
            link(nc.vector.tensor_scalar(sub_gain, vt[:, col["attn_sub_gain"]:col["attn_sub_gain"] + 1],
                                         1.0 - LAM_INIT, None, ALU.mult))

            n = 0
            for u, (layer, part) in enumerate(ada_parts):
                acc = ada_acc[:, u % 2, :]
                if u >= 2:
                    v.wait_ge(ada_turned, u - 1)
                for k in range(ND):
                    v.wait_ge(ada_load[n % 4], 16 * (n // 4 + 1))
                    if k:
                        v.wait_ge(ada_read, n)
                    w = ada_w[:, n % 4, :]
                    if k == 0:
                        ins = nc.vector.tensor_scalar(acc, w, c_silu[:, 0:1], None, ALU.mult)
                    else:
                        ins = nc.vector.scalar_tensor_tensor(out=acc, in0=w, scalar=c_silu[:, k:k + 1], in1=acc,
                                                             op0=ALU.mult, op1=ALU.add)
                    ins.then_inc(ada_read, 1)
                    n += 1
                v.wait_ge(ada_read, n)
                nc.vector.tensor_copy(small[:, 36:37], ones[:, 0:1]).then_inc(ada_summed, 1)
                v.wait_ge(ada_summed, u + 1)
            v.wait_ge(ada_turned, len(ada_parts))
            link(nc.vector.tensor_tensor(mod[:, :], ps[6][:, 0:96], vt[:, col["ada_b_2"]:col["ada_b_2"] + 96], ALU.add))
            for i, (name, layer, scale_at) in enumerate([("norm_mix_2", 0, 8), ("norm_mlp_2", 0, 32),
                                                         ("norm_mix_2", 1, 56), ("norm_mlp_2", 1, 80)]):
                g = vt[:, col[name] + 8 * layer:col[name] + 8 * layer + 8]
                link(nc.vector.scalar_tensor_tensor(out=mod_gain[:, 8 * i:8 * i + 8], in0=mod[:, scale_at:scale_at + 8],
                                                    scalar=1.0, in1=g, op0=ALU.add, op1=ALU.mult))

        norm_pe = Steps(sem("norm_pe"), [f"sum{k}" for k in range(ND)])
        norm_act = Steps(sem("norm_act"), [f"sq{k}" for k in range(ND)] + ["ln", "rstd"] + [f"hi{k}" for k in range(ND)])
        norm_dve = Steps(sem("norm_dve"), ["t0", "t1"] + sum(([f"lo{k}", f"t{k + 2}"] for k in range(6)), [])
                         + ["lo6", "lo7"])

        def norm_gain(i, k):
            if i < 6:
                name, base = [("ln_mix_e", 0), ("ln_mlp", 0), ("ln_ple", 0),
                              ("ln_mix_o", 0), ("ln_mlp", 8), ("ln_ple", 8)][i]
                c = col[name] + base + k
                return vt[:, c:c + 1], 0.0
            n = i - 6
            s = 24 * n + k
            return mod_gain[:, 8 * n + k:8 * n + k + 1], mod[:, s:s + 1]

        def norm_tensor(pe, i):
            for k in range(ND):
                pe.wait_ge(*norm_act.at(i, f"sq{k}"))
                nc.tensor.matmul(ps[2][:, :], ones[:, :], sq[:, k % 2, :], start=(k == 0),
                                 stop=(k == ND - 1)).then_inc(*norm_pe(f"sum{k}"))

        def norm_scalar(act, i):
            for k in range(ND):
                if k >= 2:
                    act.wait_ge(*norm_pe.at(i, f"sum{k - 2}"))
                nc.scalar.activation(sq[:, k % 2, :], h[:, k, :], ACT.Square).then_inc(*norm_act(f"sq{k}"))
            act.wait_ge(*norm_pe.at(i, "sum7"))
            nc.scalar.activation(rb[:, 1, :], ps[2][:, :], ACT.Ln, scale=1.0 / D, bias=eps_col).then_inc(*norm_act("ln"))
            act.wait_ge(*norm_act.at(i, "ln"))
            nc.scalar.activation(rb[:, 0, :], rb[:, 1, :], ACT.Exp, scale=-0.5).then_inc(*norm_act("rstd"))
            for k in range(ND):
                act.wait_ge(*norm_dve.at(i, f"t{k}"))
                nc.scalar.activation(x_hi[:, k, :], tt[:, k % 3, :], ACT.Identity,
                                     bias=norm_gain(i, k)[1]).then_inc(*norm_act(f"hi{k}"))

        def norm_vector(v, i):
            def full(k):
                gain, _ = norm_gain(i, k)
                if k >= 3:
                    v.wait_ge(*norm_dve.at(i, f"lo{k - 3}"))
                nc.vector.scalar_tensor_tensor(out=tt[:, k % 3, :], in0=h[:, k, :], scalar=gain, in1=rb[:, 0, :],
                                               op0=ALU.mult, op1=ALU.mult).then_inc(*norm_dve(f"t{k}"))
            v.wait_ge(*norm_act.at(i, "rstd"))
            full(0)
            full(1)
            for k in range(ND):
                v.wait_ge(*norm_act.at(i, f"hi{k}"))
                nc.vector.scalar_tensor_tensor(out=x_lo[:, k, :], in0=tt[:, k % 3, :], scalar=norm_gain(i, k)[1],
                                               in1=x_hi[:, k, :].bitcast(F32), op0=ALU.add,
                                               op1=ALU.subtract).then_inc(*norm_dve(f"lo{k}"))
                if k + 2 < ND:
                    full(k + 2)

        def gate_col(block2_layer, half, n):
            if block2_layer is None:
                return 1.0
            c = 48 * block2_layer + 24 * half + 16 + n
            return mod[:, c:c + 1]

        def add_chunk(v, q, j, n, gate):
            v.wait_ge(*done(q, j))
            nc.vector.scalar_tensor_tensor(out=h[:, n, :], in0=ps[j % 2][:, :], scalar=gate, in1=h[:, n, :],
                                           op0=ALU.mult, op1=ALU.add).then_inc(bank_free[j % 2], 1)

        def project_tensor(pe, name):
            for n in range(8):
                dense(pe, quads[name] + n // 4, n % 4, m_hi, m_lo)

        def project_vector(v, name, layer2):
            for n in range(8):
                add_chunk(v, quads[name] + n // 4, n % 4, n, gate_col(layer2, 0, n))

        mlp_act = Steps(sem("mlp_act"), [f"hi{n}" for n in range(8)])
        mlp_dve = Steps(sem("mlp_dve"), sum(([f"square{n}", f"lo{n}"] for n in range(8)), []))
        relu = sq

        def mlp_tensor(pe, i, layer):
            q, u = quads[f"mlp{i}"], 4 * i
            with pe.Fori(0, 4) as quarter:
                for n in range(8):
                    dense(pe, q + 4 * quarter + n // 4, n % 4, x_hi, x_lo)
                for n in range(8):
                    dense(pe, q + 4 * quarter + 2 + n // 4, n % 4, m_hi, m_lo,
                          rhs_ready=(lambda k: mlp_dve.at(u + quarter, f"lo{k}")) if n == 0 else None)

        def mlp_scalar(act, i):
            q, u = quads[f"mlp{i}"], 4 * i
            with act.Fori(0, 4) as quarter:
                for n in range(8):
                    qq, j = q + 4 * quarter + n // 4, n % 4
                    act.wait_ge(*done(qq, j))
                    if n >= 2:
                        act.wait_ge(*mlp_dve.at(u + quarter, f"square{n - 2}"))
                    nc.scalar.activation(relu[:, n % 2, :], ps[j % 2][:, :], ACT.Relu).then_inc(bank_free[j % 2], 1)
                    act.wait_ge(*mlp_dve.at(u + quarter, f"square{n}"))
                    nc.scalar.activation(m_hi[:, n, :], tt[:, n % 3, :], ACT.Copy).then_inc(*mlp_act(f"hi{n}"))

        def mlp_vector(v, i, layer2):
            q, u = quads[f"mlp{i}"], 4 * i
            with v.Fori(0, 4) as quarter:
                for n in range(8):
                    v.wait_ge(*freed(q + 4 * quarter + n // 4, n % 4))
                    if n >= 3:
                        v.wait_ge(*mlp_dve.at(u + quarter, f"lo{n - 3}"))
                    nc.vector.tensor_tensor(tt[:, n % 3, :], relu[:, n % 2, :], relu[:, n % 2, :],
                                            ALU.mult).then_inc(*mlp_dve(f"square{n}"))
                    v.wait_ge(*mlp_act.at(u + quarter, f"hi{n}"))
                    nc.vector.tensor_tensor(m_lo[:, n, :], tt[:, n % 3, :], m_hi[:, n, :].bitcast(F32),
                                            ALU.subtract).then_inc(*mlp_dve(f"lo{n}"))
                for n in range(8):
                    add_chunk(v, q + 4 * quarter + 2 + n // 4, n % 4, n, gate_col(layer2, 1, n))

        arena_at[0] = 0
        ple_w = take([2, D])
        p_in = take([NT, 256])
        p_t = take([2, T])
        ple_pe = Steps(sem("ple_pe"), ["p0", "p1"] + [f"proj{n}" for n in range(8)])
        ple_act = Steps(sem("ple_act"), ["p0", "p1"])
        ple_dve = Steps(sem("ple_dve"), [f"mul{n}" for n in range(8)] + ["add"])

        def ple_loads(act, i):
            act.dma_start(ple_w[:, :, :], dram["w_ple_proj"][i].rearrange("(k p) n -> p k n", p=P)).then_inc(ple_load, 16)
            act.dma_start(p_in[:, :, :], dram["p"][i][0].rearrange("(b p) n -> p b n", p=P)).then_inc(ple_load, 16)

        def ple_tensor(pe, i):
            q = quads[f"ple{i}"]
            pe.wait_ge(ple_load, 32 * i + 32)
            for k in range(2):
                for b in range(NT):
                    last = nc.tensor.transpose(ps[3 + k][:, b * P:(b + 1) * P], p_in[:, b, k * P:(k + 1) * P], ident[:, :])
                last.then_inc(*ple_pe(f"p{k}"))
            for n in range(8):
                dense(pe, q + n // 4, n % 4, x_hi, x_lo)
                if n < 2:
                    pe.wait_ge(*ple_act.at(i, "p1"))
                else:
                    pe.wait_ge(*ple_dve.at(i, f"mul{n - 2}"))
                for k in range(2):
                    last = nc.tensor.matmul(ps[3 + n % 2][:, :], ple_w[:, k, n * P:(n + 1) * P], p_t[:, k, :],
                                            start=(k == 0), stop=(k == 1))
                last.then_inc(*ple_pe(f"proj{n}"))

        def ple_scalar(act, i):
            q = quads[f"ple{i}"]
            for k in range(2):
                act.wait_ge(*ple_pe.at(i, f"p{k}"))
                nc.scalar.activation(p_t[:, k, :], ps[3 + k][:, :], ACT.Copy).then_inc(*ple_act(f"p{k}"))
            for n in range(8):
                act.wait_ge(*done(q + n // 4, n % 4))
                if n >= 2:
                    act.wait_ge(*ple_dve.at(i, f"mul{n - 2}"))
                nc.scalar.activation(sq[:, n % 2, :], ps[n % 2][:, :], ACT.Sigmoid).then_inc(bank_free[n % 2], 1)

        def ple_vector(v, i):
            q = quads[f"ple{i}"]
            for n in range(8):
                v.wait_ge(*freed(q + n // 4, n % 4))
                v.wait_ge(*ple_pe.at(i, f"proj{n}"))
                if n >= 3:
                    v.wait_ge(ple_add, 8 * i + n - 2)
                nc.vector.tensor_tensor(tt[:, n % 3, :], ps[3 + n % 2][:, :], sq[:, n % 2, :],
                                        ALU.mult).then_inc(*ple_dve(f"mul{n}"))
                v.wait_ge(*ple_dve.at(i, f"mul{n}"))
                nc.vector.tensor_tensor(h[:, n, :], h[:, n, :], tt[:, n % 3, :], ALU.add).then_inc(ple_add, 1)

        ple_dve.names.remove("add")
        ple_add = sem("ple_add")

        def rsqrt(act, steps, unit, name, src, dst, tmp, scale):
            nc.scalar.activation(tmp, src, ACT.Ln, scale=scale, bias=eps_col).then_inc(*steps(f"{name}_ln"))
            act.wait_ge(*steps.at(unit, f"{name}_ln"))
            nc.scalar.activation(dst, tmp, ACT.Exp, scale=-0.5).then_inc(*steps(f"{name}_rs"))

        arena_at[0] = 0
        gm_u, gm_v, gm_xc, gm_tmp = take([T]), take([T]), take([T]), take([T])
        gm_nat, gm_s = take([NT, P]), take([T])
        gmlp_pe = Steps(sem("gmlp_pe"), ["mean", "var", "turn", "mix"])
        gmlp_act = Steps(sem("gmlp_act"), ["sq", "v_ln", "v_rs", "nat", "hi"])
        gmlp_dve = Steps(sem("gmlp_dve"), ["xc", "vn", "s", "us", "lo"])

        def gmlp_chunks(g):
            c = 2 * g
            q = quads["gmlp"]
            return (q + c // 4, c % 4), (q + (c + 1) // 4, (c + 1) % 4)

        def gmlp_tensor(pe):
            for g in range(4):
                for q, j in gmlp_chunks(g):
                    dense(pe, q, j, x_hi, x_lo)
                pe.wait_ge(*freed(*gmlp_chunks(g)[1]))
                nc.tensor.matmul(ps[2][:, :], ones[:, :], gm_v, start=True, stop=True).then_inc(*gmlp_pe("mean"))
                pe.wait_ge(*gmlp_act.at(g, "sq"))
                nc.tensor.matmul(ps[3][:, :], ones[:, :], sq[:, 0, :], start=True, stop=True).then_inc(*gmlp_pe("var"))
                pe.wait_ge(*gmlp_dve.at(g, "vn"))
                for b in range(NT):
                    last = nc.tensor.transpose(ps[4][:, b * P:(b + 1) * P], gm_xc[:, b * P:(b + 1) * P], ident[:, :])
                last.then_inc(*gmlp_pe("turn"))
                pe.wait_ge(*gmlp_act.at(g, "nat"))
                for b in range(NT):
                    last = nc.tensor.matmul(ps[5][:, b * P:(b + 1) * P], gm_nat[:, b, :], gmlp_wt[:, g, :],
                                            start=True, stop=True)
                last.then_inc(*gmlp_pe("mix"))

        def gmlp_scalar(act):
            for g in range(4):
                (qu, ju), (qv, jv) = gmlp_chunks(g)
                act.wait_ge(*done(qu, ju))
                if g:
                    act.wait_ge(*gmlp_dve.at(g - 1, "us"))
                nc.scalar.activation(gm_u, ps[ju % 2][:, :], ACT.Gelu_apprx_tanh).then_inc(bank_free[ju % 2], 1)
                act.wait_ge(*done(qv, jv))
                nc.scalar.activation(gm_v, ps[jv % 2][:, :], ACT.Gelu_apprx_tanh).then_inc(bank_free[jv % 2], 1)
                act.wait_ge(*gmlp_dve.at(g, "xc"))
                nc.scalar.activation(sq[:, 0, :], gm_xc, ACT.Square).then_inc(*gmlp_act("sq"))
                act.wait_ge(*gmlp_pe.at(g, "var"))
                rsqrt(act, gmlp_act, g, "v", ps[3][:, :], rb[:, 0, :], rb[:, 1, :], 1.0 / P)
                act.wait_ge(*gmlp_pe.at(g, "turn"))
                nc.scalar.activation(gm_nat.rearrange("p b t -> p (b t)"), ps[4][:, :], ACT.Copy).then_inc(*gmlp_act("nat"))
                act.wait_ge(*gmlp_dve.at(g, "us"))
                nc.scalar.activation(m_hi[:, g, :], tt[:, 0, :], ACT.Copy).then_inc(*gmlp_act("hi"))

        def gmlp_vector(v):
            for g in range(4):
                v.wait_ge(*freed(*gmlp_chunks(g)[1]))
                v.wait_ge(*gmlp_pe.at(g, "mean"))
                nc.vector.scalar_tensor_tensor(out=gm_xc, in0=ps[2][:, :], scalar=-1.0 / P, in1=gm_v, op0=ALU.mult,
                                               op1=ALU.add).then_inc(*gmlp_dve("xc"))
                v.wait_ge(*gmlp_dve.at(g, "xc"))
                v.wait_ge(*gmlp_act.at(g, "v_rs"))
                nc.vector.tensor_tensor(gm_xc, gm_xc, rb[:, 0, :], ALU.mult).then_inc(*gmlp_dve("vn"))
                c = col["gmlp_v_gain"] + g
                v.wait_ge(*gmlp_pe.at(g, "mix"))
                nc.vector.scalar_tensor_tensor(out=blocks(gm_s), in0=blocks(ps[5][:, :]), scalar=vt[:, c:c + 1],
                                               in1=over_blocks(gmlp_bs[:, g, :]), op0=ALU.mult,
                                               op1=ALU.add).then_inc(*gmlp_dve("s"))
                v.wait_ge(*gmlp_dve.at(g, "s"))
                nc.vector.tensor_tensor(tt[:, 0, :], gm_u, gm_s, ALU.mult).then_inc(*gmlp_dve("us"))
                v.wait_ge(*gmlp_act.at(g, "hi"))
                nc.vector.tensor_tensor(m_lo[:, g, :], tt[:, 0, :], m_hi[:, g, :].bitcast(F32),
                                        ALU.subtract).then_inc(*gmlp_dve("lo"))

        gates_pe = Steps(sem("gates_pe"), ["logits", "cumsum"])
        gates_act = Steps(sem("gates_act"), ["beta", "abs", "exp", "ln"])
        gates_dve = Steps(sem("gates_dve"), ["x", "copy", "sp", "g", "gc"])
        ga_x, ga_e = take([NT, 4]), take([NT, 4])
        ga_w = take([ND, 8])

        def gates_tensor(pe):
            for b in range(NT):
                for k in range(ND):
                    for part, src in enumerate((x_hi, x_lo)):
                        last = nc.tensor.matmul(ps[6][:, b * 8:b * 8 + 8], src[:, k, b * P:(b + 1) * P].bitcast(F32),
                                                gates_w[:, k, :], start=(k == 0 and part == 0),
                                                stop=(k == ND - 1 and part == 1))
            last.then_inc(*gates_pe("logits"))
            pe.wait_ge(*gates_dve.at(0, "g"))
            nc.tensor.matmul(ps[7][:, 0:16], upper[:, :], g_nat[:, :, :].rearrange("p b h -> p (b h)"), start=True,
                             stop=True).then_inc(*gates_pe("cumsum"))

        def gates_scalar(act):
            act.wait_ge(*gates_dve.at(0, "x"))
            logits = ps[6][:, 0:32].rearrange("p (b e) -> p b e", e=8)
            nc.scalar.activation(beta_nat[:, :, :], logits[:, :, 0:4], ACT.Sigmoid).then_inc(*gates_act("beta"))
            act.wait_ge(*gates_dve.at(0, "x"))
            nc.scalar.activation(ga_e, ga_x, ACT.Abs).then_inc(*gates_act("abs"))
            act.wait_ge(*gates_act.at(0, "abs"))
            act.wait_ge(*gates_dve.at(0, "copy"))
            nc.scalar.activation(ga_e, ga_e, ACT.Exp, scale=-1.0).then_inc(*gates_act("exp"))
            act.wait_ge(*gates_act.at(0, "exp"))
            nc.scalar.activation(ga_e, ga_e, ACT.Ln, bias=1.0).then_inc(*gates_act("ln"))

        def gates_vector(v):
            v.wait_ge(*gates_pe.at(0, "logits"))
            logits = ps[6][:, 0:32].rearrange("p (b e) -> p b e", e=8)
            nc.vector.tensor_tensor(ga_x, logits[:, :, 4:8], gates_b[:, 4:8].unsqueeze(1).to_broadcast([P, NT, 4]),
                                    ALU.add).then_inc(*gates_dve("x"))
            nc.vector.tensor_copy(small[:, 37:38], ones[:, 0:1]).then_inc(*gates_dve("copy"))
            v.wait_ge(*gates_act.at(0, "ln"))
            nc.vector.scalar_tensor_tensor(out=ga_x, in0=ga_x, scalar=0.0, in1=ga_e, op0=ALU.max,
                                           op1=ALU.add).then_inc(*gates_dve("sp"))
            v.wait_ge(*gates_dve.at(0, "sp"))
            nc.vector.tensor_tensor(g_nat[:, :, :], ga_x, neg_exp_a.unsqueeze(1).to_broadcast([P, NT, 4]),
                                    ALU.mult).then_inc(*gates_dve("g"))
            v.wait_ge(*gates_pe.at(0, "cumsum"))
            nc.vector.tensor_copy(gc_nat[:, :, :].rearrange("p b h -> p (b h)"), ps[7][:, 0:16]).then_inc(*gates_dve("gc"))

        arena_at[0] = 0
        dl_z, dl_q, dl_k, dl_v = take([T]), take([T]), take([T]), take([T])
        dl_gtri, dl_bdiag, dl_eg, dl_dt = take([NT, P]), take([NT, P]), take([T]), take([T])
        dl_at, dl_pt, dl_kb, dl_kd, dl_vb = take([T]), take([T]), take([T]), take([T]), take([T])
        dl_x, dl_y, dl_p, dl_am = take([T]), take([T]), take([T]), take([T])
        dl_w, dl_u, dl_qd, dl_vn, dl_s, dl_o = take([T]), take([T]), take([T]), take([T]), take([P]), take([T])
        dl_cols = take([48])
        taps = dl_cols[:, 0:12]
        gcol, gccol, bcol = dl_cols[:, 12:16], dl_cols[:, 16:20], dl_cols[:, 20:24]
        egcol, kdcol, becol = dl_cols[:, 24:28], dl_cols[:, 28:32], dl_cols[:, 32:36]

        lv_pe = sum(([f"p{l}"] + ([f"x{l}"] if l < 6 else []) + [f"y{l}"] for l in range(1, LEVELS)), [])
        scan_pe = sum((([f"ws{b}"] if b else []) + [f"o{b}"] + ([f"ds{b}"] if b < 3 else []) for b in range(NT)), [])
        delta_pe = Steps(sem("delta_pe"), ["rows_g", "rows_b", "q_sum", "k_sum", "k_turn", "v_turn", "kk", "qk", "a_turn"]
                         + lv_pe + ["w", "u"] + scan_pe + ["o_sum"])
        delta_act = Steps(sem("delta_act"), ["q_s", "k_s", "v_s", "q_sq", "k_sq", "eg", "egc", "q_ln", "q_rs", "k_ln",
                                             "k_rs", "dt", "kd_col", "kb", "kd", "vb"]
                          + [f"p{l}" for l in range(1, LEVELS)] + ["w", "u", "o_raw", "o_sq", "o_ln", "o_rs", "o_hi"])
        lv_dve = sum(([f"am{l}"] + ([f"xm{l}"] if l < 6 else []) + [f"ym{l}"] for l in range(1, LEVELS)), [])
        scan_dve = ["vn0"] + sum(([f"s{b}", f"vn{b + 1}"] for b in range(3)), [])
        delta_dve = Steps(sem("delta_dve"), ["taps", "g_col", "gc_col", "b_col", "gtri", "bdiag"]
                          + [f"{x}_tap{i}" for x in "qkv" for i in range(4)]
                          + ["dt_arg", "dt_mask", "kd_arg", "be", "q_n", "k_n", "q_dec", "at0", "at", "pt",
                             "y_m", "y", "x_m", "x"] + lv_dve + scan_dve + ["o_t", "o_g", "o_lo"])

        def delta_tensor(pe):
            with pe.Fori(0, 4) as u:
                q = quads["delta"] + u
                for j in range(4):
                    dense(pe, q, j, x_hi, x_lo)
                pe.wait_ge(*delta_dve.at(u, "gtri"))
                nc.tensor.matmul(ps[2][:, :], ones[:, :], dl_gtri.rearrange("p b t -> p (b t)"), start=True,
                                 stop=True).then_inc(*delta_pe("rows_g"))
                pe.wait_ge(*delta_dve.at(u, "bdiag"))
                nc.tensor.matmul(ps[3][:, :], ones[:, :], dl_bdiag.rearrange("p b t -> p (b t)"), start=True,
                                 stop=True).then_inc(*delta_pe("rows_b"))
                pe.wait_ge(*delta_act.at(u, "q_sq"))
                nc.tensor.matmul(ps[4][:, :], ones[:, :], sq[:, 0, :], start=True, stop=True).then_inc(*delta_pe("q_sum"))
                pe.wait_ge(*delta_act.at(u, "k_sq"))
                nc.tensor.matmul(ps[5][:, :], ones[:, :], sq[:, 1, :], start=True, stop=True).then_inc(*delta_pe("k_sum"))

                def each(bank, lhs, rhs, step, turn=False):
                    for b in range(NT):
                        s = slice(b * P, (b + 1) * P)
                        if turn:
                            last = nc.tensor.transpose(ps[bank][:, s], lhs[:, s], ident[:, :])
                        else:
                            last = nc.tensor.matmul(ps[bank][:, s], lhs[:, s], rhs[:, s], start=True, stop=True)
                    last.then_inc(*delta_pe(step))

                pe.wait_ge(*delta_dve.at(u, "q_dec"))
                each(6, dl_k, None, "k_turn", True)
                each(7, dl_v, None, "v_turn", True)
                each(4, dl_k, dl_k, "kk")
                each(5, dl_k, dl_q, "qk")
                pe.wait_ge(*delta_dve.at(u, "at"))
                pe.wait_ge(*delta_act.at(u, "kd"))
                each(6, dl_at, None, "a_turn", True)
                pe.wait_ge(*delta_act.at(u, "vb"))
                pe.wait_ge(*delta_dve.at(u, "pt"))
                for l in range(1, LEVELS):
                    pe.wait_ge(*delta_dve.at(u, f"am{l}"))
                    pe.wait_ge(*delta_dve.at(u, "x" if l == 1 else f"xm{l - 1}"))
                    each(7, dl_am, dl_x, f"p{l}")
                    pe.wait_ge(*delta_act.at(u, f"p{l}"))
                    pe.wait_ge(*delta_dve.at(u, "y" if l == 1 else f"ym{l - 1}"))
                    if l < 6:
                        each(4, dl_y, dl_p, f"x{l}")
                    each(5, dl_p, dl_y, f"y{l}")
                pe.wait_ge(*delta_dve.at(u, "ym6"))
                each(6, dl_kb, dl_y, "w")
                each(7, dl_y, dl_vb, "u")
                for b in range(NT):
                    s = slice(b * P, (b + 1) * P)
                    if b:
                        pe.wait_ge(*delta_act.at(u, "w"))
                        pe.wait_ge(*delta_dve.at(u, f"s{b - 1}"))
                        nc.tensor.matmul(ps[4][:, s], dl_w[:, s], dl_s, start=True, stop=True).then_inc(*delta_pe(f"ws{b}"))
                        nc.tensor.matmul(ps[2][:, s], dl_s, dl_qd[:, s], start=True, stop=False)
                    pe.wait_ge(*delta_dve.at(u, f"vn{b}"))
                    nc.tensor.matmul(ps[2][:, s], dl_vn[:, s], dl_pt[:, s], start=(b == 0),
                                     stop=True).then_inc(*delta_pe(f"o{b}"))
                    if b < 3:
                        nc.tensor.matmul(ps[5][:, s], dl_kd[:, s], dl_vn[:, s], start=True,
                                         stop=True).then_inc(*delta_pe(f"ds{b}"))
                pe.wait_ge(*delta_act.at(u, "o_sq"))
                nc.tensor.matmul(ps[3][:, :], ones[:, :], sq[:, 0, :], start=True, stop=True).then_inc(*delta_pe("o_sum"))

        def delta_scalar(act):
            with act.Fori(0, 4) as u:
                q = quads["delta"] + u
                for x, buf in (("q", dl_q), ("k", dl_k), ("v", dl_v)):
                    act.wait_ge(*delta_dve.at(u, f"{x}_tap3"))
                    nc.scalar.activation(buf, buf, ACT.Silu).then_inc(*delta_act(f"{x}_s"))
                act.wait_ge(*done(q, 3))
                nc.scalar.activation(dl_z, ps[1][:, :], ACT.Silu).then_inc(bank_free[1], 1)
                act.wait_ge(*delta_act.at(u, "q_s"))
                nc.scalar.activation(sq[:, 0, :], dl_q, ACT.Square).then_inc(*delta_act("q_sq"))
                act.wait_ge(*delta_act.at(u, "k_s"))
                nc.scalar.activation(sq[:, 1, :], dl_k, ACT.Square).then_inc(*delta_act("k_sq"))
                act.wait_ge(*delta_pe.at(u, "rows_g"))
                nc.scalar.activation(dl_eg, ps[2][:, :], ACT.Exp).then_inc(*delta_act("eg"))
                act.wait_ge(*delta_dve.at(u, "gc_col"))
                nc.scalar.activation(egcol, gccol, ACT.Exp).then_inc(*delta_act("egc"))
                act.wait_ge(*delta_pe.at(u, "q_sum"))
                rsqrt(act, delta_act, u, "q", ps[4][:, :], rb[:, 0, :], tt[:, 1, :], 1.0)
                act.wait_ge(*delta_pe.at(u, "k_sum"))
                rsqrt(act, delta_act, u, "k", ps[5][:, :], rb[:, 1, :], tt[:, 2, :], 1.0)
                act.wait_ge(*delta_dve.at(u, "dt_arg"))
                nc.scalar.activation(dl_dt, dl_dt, ACT.Exp).then_inc(*delta_act("dt"))
                act.wait_ge(*delta_dve.at(u, "kd_arg"))
                nc.scalar.activation(kdcol, kdcol, ACT.Exp).then_inc(*delta_act("kd_col"))

                def scaled(dst, src, cols, step):
                    for b in range(NT):
                        s = slice(b * P, (b + 1) * P)
                        last = nc.scalar.activation(dst[:, s], src[:, s], ACT.Copy, scale=cols[:, b:b + 1])
                    last.then_inc(*delta_act(step))

                act.wait_ge(*delta_pe.at(u, "k_turn"))
                act.wait_ge(*delta_dve.at(u, "be"))
                scaled(dl_kb, ps[6], becol, "kb")
                act.wait_ge(*delta_act.at(u, "kd_col"))
                scaled(dl_kd, ps[6], kdcol, "kd")
                act.wait_ge(*delta_pe.at(u, "v_turn"))
                scaled(dl_vb, ps[7], bcol, "vb")
                for l in range(1, LEVELS):
                    act.wait_ge(*delta_pe.at(u, f"p{l}"))
                    nc.scalar.activation(dl_p, ps[7][:, :], ACT.Copy).then_inc(*delta_act(f"p{l}"))
                act.wait_ge(*delta_pe.at(u, "w"))
                nc.scalar.activation(dl_w, ps[6][:, :], ACT.Copy).then_inc(*delta_act("w"))
                act.wait_ge(*delta_pe.at(u, "u"))
                nc.scalar.activation(dl_u, ps[7][:, :], ACT.Copy).then_inc(*delta_act("u"))
                act.wait_ge(*delta_pe.at(u, "o3"))
                nc.scalar.activation(dl_o, ps[2][:, :], ACT.Copy).then_inc(*delta_act("o_raw"))
                act.wait_ge(*delta_act.at(u, "o_raw"))
                nc.scalar.activation(sq[:, 0, :], dl_o, ACT.Square).then_inc(*delta_act("o_sq"))
                act.wait_ge(*delta_pe.at(u, "o_sum"))
                rsqrt(act, delta_act, u, "o", ps[3][:, :], rb[:, 0, :], tt[:, 1, :], 1.0 / P)
                act.wait_ge(*delta_dve.at(u, "o_g"))
                nc.scalar.activation(m_hi[:, 4 + u, :], tt[:, 0, :], ACT.Copy).then_inc(*delta_act("o_hi"))

        def delta_vector(v):
            with v.Fori(0, 4) as u:
                q = quads["delta"] + u

                def own(name):
                    v.wait_ge(*delta_dve.at(u, name))

                c = col["gdn_conv"]
                nc.vector.tensor_copy(taps, vt[:, c:c + 48].rearrange("p (n h) -> p n h", h=4)[:, :, bass.ds(u, 1)]
                                      ).then_inc(*delta_dve("taps"))
                for name, dst, src in (("g_col", gcol, g_nat), ("gc_col", gccol, gc_nat), ("b_col", bcol, beta_nat)):
                    nc.vector.tensor_copy(dst, src[:, :, bass.ds(u, 1)]).then_inc(*delta_dve(name))
                own("b_col")
                for b in range(NT):
                    last = nc.vector.tensor_scalar(dl_gtri[:, b, :], upper[:, :], gcol[:, b:b + 1], None, ALU.mult)
                last.then_inc(*delta_dve("gtri"))
                for b in range(NT):
                    last = nc.vector.tensor_scalar(dl_bdiag[:, b, :], ident[:, :], bcol[:, b:b + 1], None, ALU.mult)
                last.then_inc(*delta_dve("bdiag"))
                for i, (x, buf) in enumerate((("q", dl_q), ("k", dl_k), ("v", dl_v))):
                    v.wait_ge(*done(q, i))
                    src = ps[i % 2]
                    nc.vector.tensor_scalar(buf, src[:, :], taps[:, 9 + i:10 + i], None, ALU.mult
                                            ).then_inc(*delta_dve(f"{x}_tap0"))
                    for n in range(1, 4):
                        own(f"{x}_tap{n - 1}")
                        t = taps[:, 3 * (3 - n) + i:3 * (3 - n) + i + 1]
                        nc.vector.scalar_tensor_tensor(out=buf[:, n:T], in0=src[:, 0:T - n], scalar=t, in1=buf[:, n:T],
                                                       op0=ALU.mult, op1=ALU.add).then_inc(*delta_dve(f"{x}_tap{n}"))
                    own(f"{x}_tap3")
                    nc.vector.tensor_copy(small[:, 76 + i:77 + i], ones[:, 0:1]).then_inc(bank_free[i % 2], 1)
                v.wait_ge(*delta_act.at(u, "eg"))
                for b in range(NT):
                    s = slice(b * P, (b + 1) * P)
                    last = nc.vector.tensor_scalar(dl_dt[:, s], ps[2][:, s], gccol[:, b:b + 1], 0.0, ALU.subtract, ALU.min)
                last.then_inc(*delta_dve("dt_arg"))
                v.wait_ge(*delta_act.at(u, "dt"))
                nc.vector.tensor_tensor(blocks(dl_dt), blocks(dl_dt), over_blocks(upper[:, :]), ALU.mult
                                        ).then_inc(*delta_dve("dt_mask"))
                nc.vector.tensor_tensor(kdcol, blocks(ps[2][:, :])[:, :, P - 1:P].rearrange("p b o -> p (b o)"), gccol,
                                        ALU.subtract).then_inc(*delta_dve("kd_arg"))
                v.wait_ge(*delta_act.at(u, "egc"))
                nc.vector.tensor_tensor(becol, bcol, egcol, ALU.mult).then_inc(*delta_dve("be"))
                v.wait_ge(*delta_act.at(u, "q_rs"))
                nc.vector.scalar_tensor_tensor(out=dl_q, in0=dl_q, scalar=float(P) ** -0.5, in1=rb[:, 0, :], op0=ALU.mult,
                                               op1=ALU.mult).then_inc(*delta_dve("q_n"))
                v.wait_ge(*delta_act.at(u, "k_rs"))
                nc.vector.tensor_tensor(dl_k, dl_k, rb[:, 1, :], ALU.mult).then_inc(*delta_dve("k_n"))
                own("q_n")
                v.wait_ge(*delta_act.at(u, "eg"))
                nc.vector.tensor_tensor(dl_qd, dl_q, dl_eg, ALU.mult).then_inc(*delta_dve("q_dec"))
                v.wait_ge(*delta_pe.at(u, "kk"))
                own("dt_mask")
                nc.vector.tensor_tensor(dl_at, ps[4][:, :], dl_dt, ALU.mult).then_inc(*delta_dve("at0"))
                own("at0")
                nc.vector.tensor_tensor(dl_at, ps[3][:, :], dl_at, ALU.mult).then_inc(*delta_dve("at"))
                v.wait_ge(*delta_pe.at(u, "qk"))
                nc.vector.tensor_tensor(dl_pt, ps[5][:, :], dl_dt, ALU.mult).then_inc(*delta_dve("pt"))
                own("at")
                nc.vector.tensor_tensor(blocks(dl_y), blocks(dl_at), over_blocks(level[:, 0, :]), ALU.mult
                                        ).then_inc(*delta_dve("y_m"))
                own("y_m")
                nc.vector.tensor_tensor(blocks(dl_y), over_blocks(ident[:, :]), blocks(dl_y), ALU.subtract
                                        ).then_inc(*delta_dve("y"))
                v.wait_ge(*delta_pe.at(u, "a_turn"))
                nc.vector.tensor_tensor(blocks(dl_x), blocks(ps[6][:, :]), over_blocks(level0_low[:, :]), ALU.mult
                                        ).then_inc(*delta_dve("x_m"))
                own("x_m")
                nc.vector.tensor_tensor(blocks(dl_x), over_blocks(ident[:, :]), blocks(dl_x), ALU.subtract
                                        ).then_inc(*delta_dve("x"))
                for l in range(1, LEVELS):
                    if l > 1:
                        v.wait_ge(*delta_pe.at(u, f"p{l - 1}"))
                    nc.vector.tensor_tensor(blocks(dl_am), blocks(dl_at), over_blocks(level[:, l, :]), ALU.mult
                                            ).then_inc(*delta_dve(f"am{l}"))
                    if l < 6:
                        v.wait_ge(*delta_pe.at(u, f"x{l}"))
                        own("x" if l == 1 else f"xm{l - 1}")
                        nc.vector.tensor_tensor(dl_x, dl_x, ps[4][:, :], ALU.subtract).then_inc(*delta_dve(f"xm{l}"))
                    v.wait_ge(*delta_pe.at(u, f"y{l}"))
                    own("y" if l == 1 else f"ym{l - 1}")
                    nc.vector.tensor_tensor(dl_y, dl_y, ps[5][:, :], ALU.subtract).then_inc(*delta_dve(f"ym{l}"))
                v.wait_ge(*delta_act.at(u, "u"))
                nc.vector.tensor_copy(dl_vn[:, 0:P], dl_u[:, 0:P]).then_inc(*delta_dve("vn0"))
                for b in range(3):
                    s, last_token = slice(b * P, (b + 1) * P), (b + 1) * P - 1
                    v.wait_ge(*delta_pe.at(u, f"ds{b}"))
                    if b == 0:
                        nc.vector.tensor_copy(dl_s, ps[5][:, s]).then_inc(*delta_dve("s0"))
                    else:
                        v.wait_ge(*delta_pe.at(u, f"o{b}"))
                        nc.vector.scalar_tensor_tensor(out=dl_s, in0=dl_s, scalar=dl_eg[:, last_token:last_token + 1],
                                                       in1=ps[5][:, s], op0=ALU.mult, op1=ALU.add
                                                       ).then_inc(*delta_dve(f"s{b}"))
                    s = slice((b + 1) * P, (b + 2) * P)
                    v.wait_ge(*delta_pe.at(u, f"ws{b + 1}"))
                    nc.vector.tensor_tensor(dl_vn[:, s], dl_u[:, s], ps[4][:, s], ALU.subtract
                                            ).then_inc(*delta_dve(f"vn{b + 1}"))
                v.wait_ge(*delta_act.at(u, "o_rs"))
                g = vt[:, col["gdn_out_gain"]:col["gdn_out_gain"] + 1]
                nc.vector.scalar_tensor_tensor(out=tt[:, 0, :], in0=dl_o, scalar=g, in1=rb[:, 0, :], op0=ALU.mult,
                                               op1=ALU.mult).then_inc(*delta_dve("o_t"))
                own("o_t")
                nc.vector.tensor_tensor(tt[:, 0, :], tt[:, 0, :], dl_z, ALU.mult).then_inc(*delta_dve("o_g"))
                v.wait_ge(*delta_act.at(u, "o_hi"))
                nc.vector.tensor_tensor(m_lo[:, 4 + u, :], tt[:, 0, :], m_hi[:, 4 + u, :].bitcast(F32),
                                        ALU.subtract).then_inc(*delta_dve("o_lo"))

        def qkv_tensor(pe, steps, act_steps, dve_steps, u, chunk, bufs, prev_done=None):
            for c in range(3):
                dense(pe, *chunk(c), x_hi, x_lo)
            for c, (x, bank) in enumerate((("q", 2), ("k", 3))):
                pe.wait_ge(*act_steps.at(u, f"{x}_sq"))
                nc.tensor.matmul(ps[bank][:, :], ones64[:, :], sq[:, c, :], start=True, stop=True).then_inc(*steps(f"{x}_sum"))
            pe.wait_ge(*freed(*chunk(2)))
            for b in range(NT):
                last = nc.tensor.transpose(ps[4][:, b * P:(b + 1) * P], bufs[2][:, b * P:(b + 1) * P], ident[:, :])
            last.then_inc(*steps("v_turn"))

        def qkv_scalar(act, steps, pe_steps, u, chunk, bufs, v_nat):
            for c, x in enumerate("qkv"):
                q, j = chunk(c)
                act.wait_ge(*done(q, j))
                nc.scalar.activation(bufs[c], ps[j % 2][:, :], ACT.Copy).then_inc(bank_free[j % 2], 1)
                if x != "v":
                    act.wait_ge(*freed(q, j))
                    nc.scalar.activation(sq[:, c, :], bufs[c], ACT.Square).then_inc(*steps(f"{x}_sq"))
            for c, x in enumerate("qk"):
                act.wait_ge(*pe_steps.at(u, f"{x}_sum"))
                rsqrt(act, steps, u, x, ps[2 + c][:, :], rb[:, c, :], tt[:, 1 + c, :], 1.0 / 64)
            act.wait_ge(*pe_steps.at(u, "v_turn"))
            nc.scalar.activation(v_nat, ps[4][:, :], ACT.Copy).then_inc(*steps("v_nat"))

        def qkv_vector(v, steps, act_steps, u, bufs, q_gain, k_gain):
            for c, (x, gain) in enumerate((("q", q_gain), ("k", k_gain))):
                v.wait_ge(*act_steps.at(u, f"{x}_rs"))
                nc.vector.scalar_tensor_tensor(out=bufs[c], in0=bufs[c], scalar=gain, in1=rb[:, c, :], op0=ALU.mult,
                                               op1=ALU.mult).then_inc(*steps(f"{x}_n"))

        arena_at[0] = 0
        at_qkv = [take([T]) for _ in range(3)]
        at_nat, at_bias, at_lg, at_pr = take([T]), take([T]), take([2, 2, T]), take([2, 2, T])
        at_p0, at_diff, at_turned, at_o = take([T]), take([T]), take([T]), take([T])
        at_small = take([64])

        def at_col(b, what, r, n=1):
            c = 16 * b + 2 * what + r
            return at_small[:, c:c + n]

        NEG_MAX, SUM, INV, MAX, LAM_INV = range(5)
        at_q, at_k, at_v = at_qkv
        attn_pe = Steps(sem("attn_pe"), ["q_sum", "k_sum", "v_turn", "lg0_0", "lg0_1"]
                        + sum(([f"lg{b + 1}_0", f"lg{b + 1}_1"] * (b < 3) + [f"turn{b}", f"pv{b}"] for b in range(NT)), [])
                        + ["o_sum"])
        attn_act = Steps(sem("attn_act"), ["q_sq", "k_sq", "q_ln", "q_rs", "k_ln", "k_rs", "v_nat", "e0_0", "e0_1"]
                         + sum(([f"e{b + 1}_0", f"e{b + 1}_1"] * (b < 3) + [f"turned{b}"] for b in range(NT)), [])
                         + ["o_raw", "o_sq", "o_ln", "o_rs", "o_hi"])

        def lg_steps(b):
            return [f"lg{b}_0", f"nm{b}_0", f"lg{b}_1", f"nm{b}_1"]
        attn_dve = Steps(sem("attn_dve"), ["q_n", "k_n"] + lg_steps(0)
                         + sum((lg_steps(b + 1) * (b < 3) + [f"inv{b}", f"lam{b}", f"p0_{b}", f"diff{b}"]
                                for b in range(NT)), []) + ["bias", "o_t", "o_lo"])
        bias_made = sem("bias_made")

        def attn_chunk(i, hh):
            def chunk(c):
                n = 3 * hh + c
                return quads["attn"] + 3 * i + n // 4, n % 4
            return chunk

        def attn_tensor(pe):
            with pe.Fori(0, 2) as i:
                for hh in range(4):
                    u = 4 * i + hh
                    qkv_tensor(pe, attn_pe, attn_act, attn_dve, u, attn_chunk(i, hh), at_qkv)

                    def logits(b):
                        for r in range(2):
                            half = slice(64 * r, 64 * r + 64)
                            if b == 0 and r == 0:
                                pe.wait_ge(*attn_dve.at(u, "k_n"))
                            if b:
                                pe.wait_ge(*attn_dve.at(u, f"lg{b - 1}_{r}"))
                            nc.tensor.matmul(ps[5 + r][:, 0:(b + 1) * P], at_q[half, b * P:(b + 1) * P],
                                             at_k[half, 0:(b + 1) * P], start=True, stop=True
                                             ).then_inc(*attn_pe(f"lg{b}_{r}"))
                    logits(0)
                    for b in range(NT):
                        if b < 3:
                            logits(b + 1)
                        pe.wait_ge(*attn_dve.at(u, f"diff{b}"))
                        if b:
                            pe.wait_ge(*attn_act.at(u, f"turned{b - 1}"))
                        for kb in range(b + 1):
                            s = slice(kb * P, (kb + 1) * P)
                            last = nc.tensor.transpose(ps[7][:, s], at_diff[:, s], ident[:, :])
                        last.then_inc(*attn_pe(f"turn{b}"))
                        pe.wait_ge(*attn_act.at(u, f"turned{b}"))
                        for kb in range(b + 1):
                            s = slice(kb * P, (kb + 1) * P)
                            last = nc.tensor.matmul(ps[3][:, b * P:(b + 1) * P], at_nat[:, s], at_turned[:, s],
                                                    start=(kb == 0), stop=(kb == b))
                        last.then_inc(*attn_pe(f"pv{b}"))
                    pe.wait_ge(*attn_act.at(u, "o_sq"))
                    nc.tensor.matmul(ps[2][:, :], ones[:, :], sq[:, 0, :], start=True, stop=True
                                     ).then_inc(*attn_pe("o_sum"))

        def attn_scalar(act):
            with act.Fori(0, 2) as i:
                for hh in range(4):
                    u = 4 * i + hh
                    if hh:
                        act.wait_ge(*attn_dve.at(u - 1, "o_lo"))
                    qkv_scalar(act, attn_act, attn_pe, u, attn_chunk(i, hh), at_qkv, at_nat)

                    def exps(b):
                        for r in range(2):
                            act.wait_ge(*attn_dve.at(u, f"nm{b}_{r}"))
                            if b >= 2:
                                act.wait_ge(*attn_dve.at(u, f"diff{b - 2}"))
                            n = (b + 1) * P
                            nc.scalar.activation(at_pr[:, b % 2, r, 0:n], at_lg[:, b % 2, r, 0:n], ACT.Exp,
                                                 bias=at_col(b, NEG_MAX, r), accum_out=at_col(b, SUM, r)
                                                 ).then_inc(*attn_act(f"e{b}_{r}"))
                    exps(0)
                    for b in range(NT):
                        if b < 3:
                            exps(b + 1)
                        n = (b + 1) * P
                        act.wait_ge(*attn_pe.at(u, f"turn{b}"))
                        if b:
                            act.wait_ge(*attn_pe.at(u, f"pv{b - 1}"))
                        nc.scalar.activation(at_turned[:, 0:n], ps[7][:, 0:n], ACT.Copy).then_inc(*attn_act(f"turned{b}"))
                    act.wait_ge(*attn_pe.at(u, "pv3"))
                    nc.scalar.activation(at_o, ps[3][:, :], ACT.Copy).then_inc(*attn_act("o_raw"))
                    act.wait_ge(*attn_act.at(u, "o_raw"))
                    nc.scalar.activation(sq[:, 0, :], at_o, ACT.Square).then_inc(*attn_act("o_sq"))
                    act.wait_ge(*attn_pe.at(u, "o_sum"))
                    rsqrt(act, attn_act, u, "o", ps[2][:, :], rb[:, 0, :], tt[:, 1, :], 1.0 / P)
                    act.wait_ge(*attn_dve.at(u, "o_t"))
                    nc.scalar.activation(m_hi[:, u, :], tt[:, 0, :], ACT.Copy).then_inc(*attn_act("o_hi"))

        def attn_vector(v):
            for c in range(NT):
                last = nc.vector.tensor_scalar(at_bias[:, c * P:(c + 1) * P], idx[:, :], -1.0, float(384 - c * P),
                                               ALU.mult, ALU.add)
            last.then_inc(bias_made, 1)
            v.wait_ge(bias_made, 1)
            nc.vector.tensor_scalar(at_o, at_bias, 0.0, BIG, ALU.is_lt, ALU.mult).then_inc(bias_made, 1)
            v.wait_ge(bias_made, 2)
            nc.vector.tensor_tensor(at_bias, at_bias, at_o, ALU.add).then_inc(bias_made, 1)
            v.wait_ge(bias_made, 3)
            nc.vector.tensor_scalar(at_bias, at_bias, -0.5, None, ALU.mult).then_inc(bias_made, 1)
            v.wait_ge(bias_made, 4)
            with v.Fori(0, 2) as i:
                for hh in range(4):
                    u = 4 * i + hh
                    qkv_vector(v, attn_dve, attn_act, u, at_qkv, q_gain_o,
                               vt[:, col["attn_k_gain"]:col["attn_k_gain"] + 1])

                    def logits(b):
                        n = (b + 1) * P
                        for r in range(2):
                            v.wait_ge(*attn_pe.at(u, f"lg{b}_{r}"))
                            if b >= 2:
                                v.wait_ge(*attn_act.at(u, f"e{b - 2}_{r}"))
                            nc.vector.tensor_tensor(at_lg[:, b % 2, r, 0:n], ps[5 + r][:, 0:n], at_bias[:, T - n:T],
                                                    ALU.add).then_inc(*attn_dve(f"lg{b}_{r}"))
                            v.wait_ge(*attn_dve.at(u, f"lg{b}_{r}"))
                            nc.vector.tensor_reduce(at_col(b, NEG_MAX, r), at_lg[:, b % 2, r, 0:n], AX_X, ALU.max,
                                                    negate=True).then_inc(*attn_dve(f"nm{b}_{r}"))
                    logits(0)
                    for b in range(NT):
                        if b < 3:
                            logits(b + 1)
                        n = (b + 1) * P
                        v.wait_ge(*attn_act.at(u, f"e{b}_1"))
                        nc.vector.reciprocal(at_col(b, INV, 0, 2), at_col(b, SUM, 0, 2)).then_inc(*attn_dve(f"inv{b}"))
                        v.wait_ge(*attn_dve.at(u, f"inv{b}"))
                        nc.vector.tensor_scalar(at_col(b, LAM_INV, 0), at_col(b, INV, 1), neg_lam, None, ALU.mult
                                                ).then_inc(*attn_dve(f"lam{b}"))
                        nc.vector.tensor_scalar(at_p0[:, 0:n], at_pr[:, b % 2, 0, 0:n], at_col(b, INV, 0), None, ALU.mult
                                                ).then_inc(*attn_dve(f"p0_{b}"))
                        v.wait_ge(*attn_dve.at(u, f"p0_{b}"))
                        if b:
                            v.wait_ge(*attn_pe.at(u, f"turn{b - 1}"))
                        nc.vector.scalar_tensor_tensor(out=at_diff[:, 0:n], in0=at_pr[:, b % 2, 1, 0:n],
                                                       scalar=at_col(b, LAM_INV, 0), in1=at_p0[:, 0:n], op0=ALU.mult,
                                                       op1=ALU.add).then_inc(*attn_dve(f"diff{b}"))
                    nc.vector.tensor_scalar(at_bias, at_bias, 0.5, None, ALU.mult).then_inc(*attn_dve("bias"))
                    v.wait_ge(*attn_act.at(u, "o_rs"))
                    nc.vector.scalar_tensor_tensor(out=tt[:, 0, :], in0=at_o, scalar=sub_gain, in1=rb[:, 0, :],
                                                   op0=ALU.mult, op1=ALU.mult).then_inc(*attn_dve("o_t"))
                    v.wait_ge(*attn_act.at(u, "o_hi"))
                    nc.vector.tensor_tensor(m_lo[:, u, :], tt[:, 0, :], m_hi[:, u, :].bitcast(F32), ALU.subtract
                                            ).then_inc(*attn_dve("o_lo"))

        arena_at[0] = 0
        st_qkv = [take([T]) for _ in range(3)]
        st_nat, st_abs, st_ln = take([T]), take([2, T]), take([2, T])
        st_sp, st_lb, st_w = take([NT, T]), take([2, T]), take([NT, T])
        st_q, st_k, st_v = st_qkv
        ITEMS = [(r, sb) for r in range(2) for sb in range(NT - 1, -1, -1)]

        def piped(first, second):
            return first(0) + sum(((first(n + 1) if n + 1 < len(ITEMS) else []) + second(n) for n in range(len(ITEMS))), [])

        stick_pe = Steps(sem("stick_pe"), ["q_sum", "k_sum", "v_turn"]
                         + piped(lambda n: [f"z{n}"], lambda n: [f"c{n}"] + [f"o{n // 4}"] * (n % 4 == 3)))
        stick_act = Steps(sem("stick_act"), ["q_sq", "k_sq", "q_ln", "q_rs", "k_ln", "k_rs", "v_nat"]
                          + piped(lambda n: [f"abs{n}", f"exp{n}", f"ln{n}"], lambda n: [f"w{n}"]) + ["o_hi"])
        stick_dve = Steps(sem("stick_dve"), ["q_n", "k_n"]
                          + piped(lambda n: [f"sp{n}", f"mask{n}", f"lb{n}"], lambda n: [f"lw{n}", f"wm{n}"]) + ["o_lo"])

        def stick_chunk(i, hh):
            def chunk(c):
                n = 3 * hh + c
                return quads["stick"] + 3 * i + n // 4, n % 4
            return chunk

        def stick_tensor(pe):
            with pe.Fori(0, 2) as i:
                for hh in range(4):
                    u = 4 * i + hh
                    qkv_tensor(pe, stick_pe, stick_act, stick_dve, u, stick_chunk(i, hh), st_qkv)

                    def scores(n):
                        r, sb = ITEMS[n]
                        half = slice(64 * r, 64 * r + 64)
                        if n == 0:
                            pe.wait_ge(*stick_dve.at(u, "k_n"))
                        if n >= 2:
                            pe.wait_ge(*stick_dve.at(u, f"lb{n - 2}"))
                        else:
                            pe.wait_ge(*stick_act.at(u, "v_nat"))
                        nc.tensor.matmul(ps[3 + n % 2][:, sb * P:T], st_k[half, sb * P:(sb + 1) * P],
                                         st_q[half, sb * P:T], start=True, stop=True).then_inc(*stick_pe(f"z{n}"))
                    scores(0)
                    for n, (r, sb) in enumerate(ITEMS):
                        if n + 1 < len(ITEMS):
                            scores(n + 1)
                        pe.wait_ge(*stick_dve.at(u, f"mask{n}"))
                        if n >= 2:
                            pe.wait_ge(*stick_dve.at(u, f"lw{n - 2}"))
                        bank = ps[5 + n % 2]
                        last = nc.tensor.matmul(bank[:, sb * P:T], lower_s[:, :], st_sp[:, sb, sb * P:T], start=True,
                                                stop=(sb == NT - 1))
                        for jb in range(sb + 1, NT):
                            last = nc.tensor.matmul(bank[:, jb * P:T], ones[:, :], st_sp[:, jb, jb * P:T], start=False,
                                                    stop=(jb == NT - 1))
                        last.then_inc(*stick_pe(f"c{n}"))
                        if sb == 0:
                            pe.wait_ge(*stick_dve.at(u, f"wm{n}"))
                            for kb in range(NT):
                                last = nc.tensor.matmul(ps[7][64 * r:64 * r + 64, kb * P:T],
                                                        st_nat[:, kb * P + 64 * r:kb * P + 64 * r + 64],
                                                        st_w[:, kb, kb * P:T], start=(kb == 0), stop=(kb == NT - 1))
                            last.then_inc(*stick_pe(f"o{r}"))

        def stick_scalar(act):
            with act.Fori(0, 2) as i:
                for hh in range(4):
                    u = 4 * i + hh
                    if hh:
                        act.wait_ge(*stick_dve.at(u - 1, "o_lo"))
                    qkv_scalar(act, stick_act, stick_pe, u, stick_chunk(i, hh), st_qkv, st_nat)

                    def first(n):
                        r, sb = ITEMS[n]
                        t = slice(sb * P, T)
                        act.wait_ge(*stick_pe.at(u, f"z{n}"))
                        nc.scalar.activation(st_abs[:, n % 2, t], ps[3 + n % 2][:, t], ACT.Abs).then_inc(*stick_act(f"abs{n}"))
                        act.wait_ge(*stick_act.at(u, f"abs{n}"))
                        nc.scalar.activation(st_abs[:, n % 2, t], st_abs[:, n % 2, t], ACT.Exp, scale=-1.0
                                             ).then_inc(*stick_act(f"exp{n}"))
                        act.wait_ge(*stick_act.at(u, f"exp{n}"))
                        if n >= 2:
                            act.wait_ge(*stick_dve.at(u, f"lb{n - 2}"))
                        nc.scalar.activation(st_ln[:, n % 2, t], st_abs[:, n % 2, t], ACT.Ln, bias=1.0
                                             ).then_inc(*stick_act(f"ln{n}"))
                    first(0)
                    for n, (r, sb) in enumerate(ITEMS):
                        if n + 1 < len(ITEMS):
                            first(n + 1)
                        act.wait_ge(*stick_dve.at(u, f"lw{n}"))
                        if n == 4:
                            act.wait_ge(*stick_pe.at(u, "o0"))
                        t = slice(sb * P, T)
                        nc.scalar.activation(st_w[:, sb, t], st_lb[:, n % 2, t], ACT.Exp).then_inc(*stick_act(f"w{n}"))
                    act.wait_ge(*stick_pe.at(u, "o1"))
                    nc.scalar.activation(m_hi[:, u, :], ps[7][:, :], ACT.Copy).then_inc(*stick_act("o_hi"))

        def stick_vector(v):
            with v.Fori(0, 2) as i:
                for hh in range(4):
                    u = 4 * i + hh
                    qkv_vector(v, stick_dve, stick_act, u, st_qkv, q_gain_s, vt[:, col["k_norm_2"]:col["k_norm_2"] + 1])

                    def first(n):
                        r, sb = ITEMS[n]
                        t, diag = slice(sb * P, T), slice(sb * P, (sb + 1) * P)
                        v.wait_ge(*stick_act.at(u, f"ln{n}"))
                        if n >= 4:
                            v.wait_ge(*stick_pe.at(u, "c3"))
                        nc.vector.scalar_tensor_tensor(out=st_sp[:, sb, t], in0=ps[3 + n % 2][:, t], scalar=0.0,
                                                       in1=st_ln[:, n % 2, t], op0=ALU.max, op1=ALU.add
                                                       ).then_inc(*stick_dve(f"sp{n}"))
                        v.wait_ge(*stick_dve.at(u, f"sp{n}"))
                        nc.vector.tensor_tensor(st_sp[:, sb, diag], st_sp[:, sb, diag], upper_s[:, :], ALU.mult
                                                ).then_inc(*stick_dve(f"mask{n}"))
                        if n >= 2:
                            v.wait_ge(*stick_act.at(u, f"w{n - 2}"))
                        nc.vector.scalar_tensor_tensor(out=st_lb[:, n % 2, t], in0=ps[3 + n % 2][:, t], scalar=0.0,
                                                       in1=st_ln[:, n % 2, t], op0=ALU.min, op1=ALU.subtract
                                                       ).then_inc(*stick_dve(f"lb{n}"))
                    first(0)
                    for n, (r, sb) in enumerate(ITEMS):
                        if n + 1 < len(ITEMS):
                            first(n + 1)
                        t, diag = slice(sb * P, T), slice(sb * P, (sb + 1) * P)
                        v.wait_ge(*stick_pe.at(u, f"c{n}"))
                        v.wait_ge(*stick_dve.at(u, f"lb{n}"))
                        nc.vector.tensor_tensor(st_lb[:, n % 2, t], st_lb[:, n % 2, t], ps[5 + n % 2][:, t], ALU.subtract
                                                ).then_inc(*stick_dve(f"lw{n}"))
                        v.wait_ge(*stick_act.at(u, f"w{n}"))
                        nc.vector.tensor_tensor(st_w[:, sb, diag], st_w[:, sb, diag], upper_s[:, :], ALU.mult
                                                ).then_inc(*stick_dve(f"wm{n}"))
                    v.wait_ge(*stick_act.at(u, "o_hi"))
                    nc.vector.tensor_tensor(m_lo[:, u, :], ps[7][:, :], m_hi[:, u, :].bitcast(F32), ALU.subtract
                                            ).then_inc(*stick_dve("o_lo"))

        arena_at[0] = 0
        cv_b, cv_c, cv_u, cv_y = take([T]), take([T]), take([T]), take([T])
        conv_act = Steps(sem("conv_act"), ["hi"])
        conv_dve = Steps(sem("conv_dve"), ["y0", "y1", "y2", "t", "lo"])

        def conv_chunk(n, c):
            g = 3 * n + c
            return quads["conv"] + g // 4, g % 4

        def conv_tensor(pe):
            for n in range(4):
                for c in range(3):
                    dense(pe, *conv_chunk(n, c), x_hi, x_lo)

        def conv_scalar(act):
            for n in range(4):
                if n:
                    act.wait_ge(*conv_dve.at(n - 1, "t"))
                for c, buf in enumerate((cv_b, cv_c)):
                    q, j = conv_chunk(n, c)
                    act.wait_ge(*done(q, j))
                    nc.scalar.activation(buf, ps[j % 2][:, :], ACT.Copy).then_inc(bank_free[j % 2], 1)
                act.wait_ge(*conv_dve.at(n, "t"))
                nc.scalar.activation(m_hi[:, n, :], tt[:, 0, :], ACT.Copy).then_inc(*conv_act("hi"))

        def conv_vector(v):
            for n in range(4):
                q, j = conv_chunk(n, 2)
                v.wait_ge(*done(q, j))
                v.wait_ge(*freed(*conv_chunk(n, 1)))
                nc.vector.tensor_tensor(cv_u, ps[j % 2][:, :], cv_c, ALU.mult).then_inc(bank_free[j % 2], 1)
                v.wait_ge(*freed(q, j))
                taps = [vt[:, col["conv_w_2"] + 4 * t + n:col["conv_w_2"] + 4 * t + n + 1] for t in range(3)]
                nc.vector.tensor_scalar(cv_y, cv_u, taps[2], None, ALU.mult).then_inc(*conv_dve("y0"))
                for s in (1, 2):
                    v.wait_ge(*conv_dve.at(n, f"y{s - 1}"))
                    nc.vector.scalar_tensor_tensor(out=cv_y[:, s:T], in0=cv_u[:, 0:T - s], scalar=taps[2 - s],
                                                   in1=cv_y[:, s:T], op0=ALU.mult, op1=ALU.add
                                                   ).then_inc(*conv_dve(f"y{s}"))
                v.wait_ge(*conv_dve.at(n, "y2"))
                v.wait_ge(*freed(*conv_chunk(n, 0)))
                nc.vector.tensor_tensor(tt[:, 0, :], cv_y, cv_b, ALU.mult).then_inc(*conv_dve("t"))
                v.wait_ge(*conv_act.at(n, "hi"))
                nc.vector.tensor_tensor(m_lo[:, n, :], tt[:, 0, :], m_hi[:, n, :].bitcast(F32), ALU.subtract
                                        ).then_inc(*conv_dve("lo"))

        arena_at[0] = 0
        hg_q, hg_f, hg_v, hg_g, hg_b = take([T]), take([T]), take([T]), take([T]), take([T])
        hg_reset, hg_e, hg_qe, hg_ke = take([T]), take([2, T]), take([2, T]), take([2, T])
        hg_sc, hg_eb, hg_qd, hg_kd, hg_kn, hg_vn = (take([T]) for _ in range(6))
        hg_lf, hg_s, hg_o, hg_cols = take([T]), take([P]), take([T]), take([8])
        hg_gain, hg_lb, hg_oml = hg_cols[:, 0:1], hg_cols[:, 1:2], hg_cols[:, 2:3]
        hg_reset_done = sem("hg_reset_done")

        def lv_piped(first, second):
            return first(0) + sum(((first(l + 1) if l + 1 < LEVELS else []) + second(l) for l in range(LEVELS)), [])

        hgrn_pe = Steps(sem("hgrn_pe"), ["diag"] + [f"lv{l}" for l in range(LEVELS)] + ["k_turn", "v_turn", "ds"]
                        + [f"o{b}" for b in range(NT)] + ["o_sum"])
        hgrn_act = Steps(sem("hgrn_act"), ["ln"] + [x for l in range(LEVELS) for x in (f"abs{l}", f"e{l}")]
                         + ["eb", "kd", "kn", "vn", "o_raw", "o_sq", "o_ln", "o_rs", "o_hi"])
        hgrn_dve = Steps(sem("hgrn_dve"), ["gain", "lb", "oml", "f", "k", "b", "diag"]
                         + lv_piped(lambda l: [f"d{l}"], lambda l: [f"qe{l}", f"ke{l}"] + [f"sc{l - 1}"] * (l > 0))
                         + ["kd_arg", "sc6", "qd", "kd", "s0", "s1", "s2", "o_t", "o_g", "o_lo"])

        def hgrn_tensor(pe):
            with pe.Fori(0, 4) as u:
                q = quads["hgrn"] + u
                for j in range(4):
                    dense(pe, q, j, x_hi, x_lo)

                def each(bank, lhs, rhs, step, turn=False):
                    for b in range(NT):
                        s = slice(b * P, (b + 1) * P)
                        if turn:
                            last = nc.tensor.transpose(ps[bank][:, s], lhs[:, s], ident[:, :])
                        else:
                            last = nc.tensor.matmul(ps[bank][:, s], lhs[:, s], rhs[:, s], start=True, stop=True)
                    last.then_inc(*hgrn_pe(step))

                pe.wait_ge(*hgrn_dve.at(u, "k"))
                each(2, hg_lf, hg_q, "diag")
                for l in range(LEVELS):
                    pe.wait_ge(*hgrn_dve.at(u, f"ke{l}"))
                    if l >= 2:
                        pe.wait_ge(*hgrn_dve.at(u, f"sc{l - 2}"))
                    each(3 + l % 2, hg_ke[:, l % 2], hg_qe[:, l % 2], f"lv{l}")
                pe.wait_ge(*hgrn_dve.at(u, "kd"))
                each(5, hg_kd, None, "k_turn", True)
                each(6, hg_v, None, "v_turn", True)
                pe.wait_ge(*hgrn_act.at(u, "vn"))
                for b in range(3):
                    s = slice(b * P, (b + 1) * P)
                    last = nc.tensor.matmul(ps[7][:, s], hg_kn[:, s], hg_vn[:, s], start=True, stop=True)
                last.then_inc(*hgrn_pe("ds"))
                for b in range(NT):
                    s = slice(b * P, (b + 1) * P)
                    if b:
                        pe.wait_ge(*hgrn_dve.at(u, f"s{b - 1}"))
                        nc.tensor.matmul(ps[2][:, s], hg_s, hg_qd[:, s], start=True, stop=False)
                    nc.tensor.matmul(ps[2][:, s], hg_vn[:, s], hg_sc[:, s], start=(b == 0), stop=True
                                     ).then_inc(*hgrn_pe(f"o{b}"))
                pe.wait_ge(*hgrn_act.at(u, "o_sq"))
                nc.tensor.matmul(ps[3][:, :], ones[:, :], sq[:, 0, :], start=True, stop=True).then_inc(*hgrn_pe("o_sum"))

        def hgrn_scalar(act):
            with act.Fori(0, 4) as u:
                q = quads["hgrn"] + u
                for j, (buf, func) in enumerate(((hg_q, ACT.Copy), (hg_f, ACT.Sigmoid), (hg_v, ACT.Copy), (hg_g, ACT.Silu))):
                    act.wait_ge(*done(q, j))
                    nc.scalar.activation(buf, ps[j % 2][:, :], func).then_inc(bank_free[j % 2], 1)
                act.wait_ge(*hgrn_dve.at(u, "k"))
                nc.scalar.activation(hg_f, hg_f, ACT.Ln).then_inc(*hgrn_act("ln"))
                for l in range(LEVELS):
                    act.wait_ge(*hgrn_dve.at(u, f"d{l}"))
                    e = hg_e[:, l % 2]
                    nc.scalar.activation(e, e, ACT.Abs).then_inc(*hgrn_act(f"abs{l}"))
                    act.wait_ge(*hgrn_act.at(u, f"abs{l}"))
                    nc.scalar.activation(e, e, ACT.Exp, scale=-1.0).then_inc(*hgrn_act(f"e{l}"))
                nc.scalar.activation(hg_eb, hg_b, ACT.Exp).then_inc(*hgrn_act("eb"))
                act.wait_ge(*hgrn_dve.at(u, "kd_arg"))
                nc.scalar.activation(hg_kd, hg_kd, ACT.Exp).then_inc(*hgrn_act("kd"))
                act.wait_ge(*hgrn_pe.at(u, "k_turn"))
                nc.scalar.activation(hg_kn, ps[5][:, :], ACT.Copy).then_inc(*hgrn_act("kn"))
                act.wait_ge(*hgrn_pe.at(u, "v_turn"))
                nc.scalar.activation(hg_vn, ps[6][:, :], ACT.Copy).then_inc(*hgrn_act("vn"))
                act.wait_ge(*hgrn_pe.at(u, "o3"))
                nc.scalar.activation(hg_o, ps[2][:, :], ACT.Copy).then_inc(*hgrn_act("o_raw"))
                act.wait_ge(*hgrn_act.at(u, "o_raw"))
                nc.scalar.activation(sq[:, 0, :], hg_o, ACT.Square).then_inc(*hgrn_act("o_sq"))
                act.wait_ge(*hgrn_pe.at(u, "o_sum"))
                rsqrt(act, hgrn_act, u, "o", ps[3][:, :], rb[:, 0, :], tt[:, 1, :], 1.0 / P)
                act.wait_ge(*hgrn_dve.at(u, "o_g"))
                nc.scalar.activation(m_hi[:, 4 + u, :], tt[:, 0, :], ACT.Copy).then_inc(*hgrn_act("o_hi"))

        def hgrn_vector(v):
            nc.vector.memset(hg_reset, 1.0).then_inc(hg_reset_done, 1)
            v.wait_ge(hg_reset_done, 1)
            nc.vector.memset(blocks(hg_reset)[:, :, 0:1], 0.0).then_inc(hg_reset_done, 1)
            v.wait_ge(hg_reset_done, 2)
            with v.Fori(0, 4) as u:
                q = quads["hgrn"] + u

                def own(name):
                    v.wait_ge(*hgrn_dve.at(u, name))

                c = col["hg_norm_2"]
                nc.vector.tensor_copy(hg_gain, vt[:, c:c + 4][:, bass.ds(u, 1)]).then_inc(*hgrn_dve("gain"))
                nc.vector.tensor_copy(hg_lb, lb[:, bass.ds(u, 1)]).then_inc(*hgrn_dve("lb"))
                nc.vector.tensor_copy(hg_oml, one_minus_lb[:, bass.ds(u, 1)]).then_inc(*hgrn_dve("oml"))
                own("oml")
                v.wait_ge(*freed(q, 3))
                nc.vector.tensor_scalar(hg_f, hg_f, hg_oml, hg_lb, ALU.mult, ALU.add).then_inc(*hgrn_dve("f"))
                own("f")
                nc.vector.tensor_scalar(hg_lf, hg_f, -1.0, 1.0, ALU.mult, ALU.add).then_inc(*hgrn_dve("k"))
                hg_k = hg_lf
                v.wait_ge(*hgrn_act.at(u, "ln"))
                nc.vector.tensor_tensor_scan(hg_b, hg_reset, hg_f, 0.0, ALU.mult, ALU.add).then_inc(*hgrn_dve("b"))
                v.wait_ge(*hgrn_pe.at(u, "diag"))
                nc.vector.tensor_tensor(blocks(hg_sc), blocks(ps[2][:, :]), over_blocks(ident[:, :]), ALU.mult
                                        ).then_inc(*hgrn_dve("diag"))

                def to_boundary(l):
                    n = 2 ** (l + 1)
                    b = hg_b.rearrange("p (m n) -> p m n", n=n)
                    nc.vector.tensor_tensor(hg_e[:, l % 2].rearrange("p (m n) -> p m n", n=n), b,
                                            b[:, :, n // 2 - 1:n // 2].to_broadcast([P, T // n, n]), ALU.subtract
                                            ).then_inc(*hgrn_dve(f"d{l}"))

                def level_ready(l):
                    v.wait_ge(*hgrn_pe.at(u, f"lv{l}"))
                    own("diag" if l == 0 else f"sc{l - 1}")

                def take_level(l):
                    nc.vector.copy_predicated(blocks(hg_sc), over_blocks(level[:, l, :]).bitcast(U32),
                                              blocks(ps[3 + l % 2][:, :])).then_inc(*hgrn_dve(f"sc{l}"))
                own("b")
                to_boundary(0)
                for l in range(LEVELS):
                    if l + 1 < LEVELS:
                        if l >= 1:
                            own(f"ke{l - 1}")
                        to_boundary(l + 1)
                    v.wait_ge(*hgrn_act.at(u, f"e{l}"))
                    if l >= 2:
                        v.wait_ge(*hgrn_pe.at(u, f"lv{l - 2}"))
                    nc.vector.tensor_tensor(hg_qe[:, l % 2], hg_q, hg_e[:, l % 2], ALU.mult).then_inc(*hgrn_dve(f"qe{l}"))
                    if l:
                        level_ready(l - 1)
                    nc.vector.tensor_tensor(hg_ke[:, l % 2], hg_k, hg_e[:, l % 2], ALU.mult).then_inc(*hgrn_dve(f"ke{l}"))
                    if l:
                        take_level(l - 1)
                level_ready(6)
                nc.vector.tensor_tensor(blocks(hg_kd), blocks(hg_b)[:, :, P - 1:P].to_broadcast([P, NT, P]), blocks(hg_b),
                                        ALU.subtract).then_inc(*hgrn_dve("kd_arg"))
                take_level(6)
                v.wait_ge(*hgrn_act.at(u, "eb"))
                nc.vector.tensor_tensor(hg_qd, hg_q, hg_eb, ALU.mult).then_inc(*hgrn_dve("qd"))
                v.wait_ge(*hgrn_act.at(u, "kd"))
                nc.vector.tensor_tensor(hg_kd, hg_kd, hg_k, ALU.mult).then_inc(*hgrn_dve("kd"))
                v.wait_ge(*hgrn_pe.at(u, "ds"))
                nc.vector.tensor_copy(hg_s, ps[7][:, 0:P]).then_inc(*hgrn_dve("s0"))
                for b in (1, 2):
                    s, last_token = slice(b * P, (b + 1) * P), (b + 1) * P - 1
                    own(f"s{b - 1}")
                    v.wait_ge(*hgrn_pe.at(u, f"o{b}"))
                    nc.vector.scalar_tensor_tensor(out=hg_s, in0=hg_s, scalar=hg_eb[:, last_token:last_token + 1],
                                                   in1=ps[7][:, s], op0=ALU.mult, op1=ALU.add).then_inc(*hgrn_dve(f"s{b}"))
                v.wait_ge(*hgrn_act.at(u, "o_rs"))
                nc.vector.scalar_tensor_tensor(out=tt[:, 0, :], in0=hg_o, scalar=hg_gain, in1=rb[:, 0, :], op0=ALU.mult,
                                               op1=ALU.mult).then_inc(*hgrn_dve("o_t"))
                own("o_t")
                nc.vector.tensor_tensor(tt[:, 0, :], tt[:, 0, :], hg_g, ALU.mult).then_inc(*hgrn_dve("o_g"))
                v.wait_ge(*hgrn_act.at(u, "o_hi"))
                nc.vector.tensor_tensor(m_lo[:, 4 + u, :], tt[:, 0, :], m_hi[:, 4 + u, :].bitcast(F32), ALU.subtract
                                        ).then_inc(*hgrn_dve("o_lo"))

        def norm(i):
            return (lambda e: norm_tensor(e, i), lambda e: norm_scalar(e, i), lambda e: norm_vector(e, i))

        def project(name, layer2=None):
            return (lambda e: project_tensor(e, name), None, lambda e: project_vector(e, name, layer2))

        def mlp(i, layer2=None):
            return (lambda e: mlp_tensor(e, i, layer2), lambda e: mlp_scalar(e, i), lambda e: mlp_vector(e, i, layer2))

        def ple(i):
            return (lambda e: ple_tensor(e, i), lambda e: (ple_loads(e, i), ple_scalar(e, i)), lambda e: ple_vector(e, i))

        plan = [(setup_tensor, setup_scalar, setup_vector)]
        if has("gmlp"):
            plan += [norm(0), (gmlp_tensor, gmlp_scalar, gmlp_vector)]
        if has("delta"):
            plan += [(gates_tensor, gates_scalar, gates_vector), (delta_tensor, delta_scalar, delta_vector)]
        if has("out_e"):
            plan += [project("out_e")]
        if has("mlp0"):
            plan += [norm(1), mlp(0)]
        if has("ple0"):
            plan += [norm(2), ple(0)]
        if has("attn"):
            plan += [norm(3), (attn_tensor, attn_scalar, attn_vector)]
        if has("out_o"):
            plan += [project("out_o")]
        if has("mlp1"):
            plan += [norm(4), mlp(1)]
        if has("ple1"):
            plan += [norm(5), ple(1)]
        if has("conv"):
            plan += [norm(6), (conv_tensor, conv_scalar, conv_vector)]
        if has("hgrn"):
            plan += [(hgrn_tensor, hgrn_scalar, hgrn_vector)]
        if has("out_ab"):
            plan += [project("out_ab", 0)]
        if has("mlp2"):
            plan += [norm(7), mlp(2, 0)]
        if has("stick"):
            plan += [norm(8), (stick_tensor, stick_scalar, stick_vector)]
        if has("out_c"):
            plan += [project("out_c", 1)]
        if has("mlp3"):
            plan += [norm(9), mlp(3, 1)]

        arena_at[0] = 0
        out_rows = take([NT, D])
        fin_pe = Steps(sem("fin_pe"), [f"b{i}" for i in range(8)])
        fin_act = Steps(sem("fin_act"), [f"b{i}" for i in range(8)])

        def finish_tensor(pe):
            for i in range(8):
                b, half = divmod(i, 2)
                if i >= 2:
                    pe.wait_ge(*fin_act.at(0, f"b{i - 2}"))
                for n in range(4):
                    last = nc.tensor.transpose(ps[2 + i % 2][:, n * P:(n + 1) * P],
                                               h[:, 4 * half + n, b * P:(b + 1) * P], ident[:, :])
                last.then_inc(*fin_pe(f"b{i}"))

        def finish_scalar(act):
            for i in range(8):
                b, half = divmod(i, 2)
                act.wait_ge(*fin_pe.at(0, f"b{i}"))
                nc.scalar.activation(out_rows[:, b, half * T:(half + 1) * T], ps[2 + i % 2][:, :],
                                     ACT.Copy).then_inc(*fin_act(f"b{i}"))

        def finish_sync(sp):
            for b in range(NT):
                sp.wait_ge(*fin_act.at(0, f"b{2 * b + 1}"))
                sp.dma_start(out[0][b * P:(b + 1) * P, :], out_rows[:, b, :]).then_inc(out_sent, 16)
            sp.wait_ge(out_sent, 16 * NT)

        plan += [(finish_tensor, finish_scalar, None)]
        block = ctx.enter_context(nc.Block())

        @block.sync
        def _(sp):
            setup_sync(sp)
            ada_loads(sp)
            stream(sp)
            finish_sync(sp)

        @block.gpsimd
        def _(pool):
            setup_gpsimd(pool)
            cut_stream(pool)

        @block.tensor
        def _(pe):
            ph = Phases(pe, "pe")
            for phase in plan:
                ph.enter()
                if phase[0] is not None:
                    phase[0](pe)
                ph.leave()

        @block.scalar
        def _(act):
            ph = Phases(act, "act")
            for phase in plan:
                ph.enter()
                if phase[1] is not None:
                    phase[1](act)
                ph.leave()

        @block.vector
        def _(v):
            ph = Phases(v, "dve")
            for phase in plan:
                ph.enter()
                if phase[2] is not None:
                    phase[2](v)
                ph.leave()


_INS = ['x', 'p', 'ln_mix_e', 'w_in_e', 'gmlp_v_gain', 'gmlp_ws', 'gmlp_bs', 'gdn_conv', 'gdn_a_log', 'gdn_dt_bias',
        'gdn_out_gain', 'w_out_e', 'ln_mix_o', 'w_qkv_o', 'attn_q_gain', 'attn_k_gain', 'diff_lambda',
        'attn_sub_gain', 'w_out_o', 'ln_mlp', 'w_mlp1', 'w_mlp2', 'ln_ple', 'w_ple_gate', 'w_ple_proj', 'c_2',
        'ada_w_2', 'ada_b_2', 'norm_mix_2', 'norm_mlp_2', 'w_in_ab_2', 'conv_w_2', 'hg_norm_2', 'lb_logits_2',
        'w_out_ab_2', 'w_qkv_2', 'q_norm_2', 'k_norm_2', 'w_out_c_2', 'mlp_w1_2', 'mlp_w2_2']


def kernel(**inputs):
    import numpy as _np
    import concourse.bacc as _bacc
    from concourse import mybir as _mybir
    from concourse.bass_utils import run_bass_kernel_spmd as _run

    nc = _bacc.Bacc("TRN2", target_bir_lowering=False, num_devices=1)
    arrays, dram = {}, {}
    for name in _INS:
        a = _np.ascontiguousarray(inputs[name])
        arrays[f"in_{name}_dram"] = a
        dram[name] = nc.dram_tensor(f"in_{name}_dram", a.shape, _mybir.dt.from_np(a.dtype), kind="ExternalInput").ap()
    out = nc.dram_tensor("out_0_dram", (1, T, D), _mybir.dt.float32, kind="ExternalOutput").ap()
    program(nc, dram, out)
    r = _run(nc, [arrays], core_ids=[0])
    return r.results[0]["out_0_dram"]
```

```python
import math
from contextlib import ExitStack

import concourse.bass as bass
from concourse import mybir

F32 = mybir.dt.float32
F32R = mybir.dt.float32r
I32 = mybir.dt.int32
U32 = mybir.dt.uint32
ALU = mybir.AluOpType
ACT = mybir.ActivationFunctionType
AX_X = mybir.AxisListType.X

P = 128
T = 512
NT = T // P
D = 1024
ND = D // P
DFF = 4096
EPS = 1e-6
BIG = 1e34
LAM_INIT = 0.8 - 0.6 * math.exp(-0.3)
LEVELS = 7


class Steps:

    def __init__(self, sem, names):
        self.sem, self.names, self.n = sem, list(names), 0
        assert len(set(self.names)) == len(self.names)

    def __call__(self, name):
        assert self.names[self.n % len(self.names)] == name, (self.names[self.n % len(self.names)], name)
        self.n += 1
        return self.sem, 1

    def at(self, unit, name):
        return self.sem, unit * len(self.names) + self.names.index(name) + 1

    def before(self, unit):
        return self.sem, unit * len(self.names)


def vector_rows():
    rows, at = [], 0
    index = {}
    for name, count in [("ln_mix_e", ND), ("ln_mix_o", ND), ("ln_mlp", 2 * ND), ("ln_ple", 2 * ND),
                        ("gmlp_v_gain", 4), ("gdn_out_gain", 1), ("gdn_conv", 48), ("attn_sub_gain", 1),
                        ("attn_q_gain", 1), ("attn_k_gain", 1),
                        ("norm_mix_2", 2 * ND), ("norm_mlp_2", 2 * ND), ("c_2", ND), ("hg_norm_2", 4),
                        ("conv_w_2", 12), ("lb_logits_2", 12), ("q_norm_2", 1), ("k_norm_2", 1),
                        ("ada_b_2", 96)]:
        if at % P + count > P:
            at += P - at % P
        index[name] = at
        rows.append((name, at, count))
        at += count
    return rows, index, -(-at // P)


def program(nc: bass.Bass, dram, out, upto="end"):
    rows, col, n_tables = vector_rows()
    ctx = ExitStack()
    with ctx:
        def sb(name, shape, dt=F32):
            return ctx.enter_context(nc.sbuf_tensor(name, shape, dt))

        def sem(name):
            return ctx.enter_context(nc.semaphore(name))

        h = sb("h", [P, ND, T])
        x_hi = sb("x_hi", [P, ND, T], F32R)
        x_lo = sb("x_lo", [P, ND, T], F32R)
        m_hi = sb("m_hi", [P, ND, T], F32R)
        m_lo = sb("m_lo", [P, ND, T], F32R)
        w_raw = sb("w_raw", [P, 4, ND, P])
        w_hi = sb("w_hi", [P, 4, ND, P], F32R)
        w_lo = sb("w_lo", [P, 4, ND, P], F32R)
        sq = sb("sq", [P, 2, T])
        rb = sb("rb", [P, 2, T])
        tt = sb("tt", [P, 3, T])
        ident = sb("ident", [P, P])
        ones = sb("ones", [P, P])
        ones64 = sb("ones64", [P, P])
        upper = sb("upper", [P, P])
        upper_s = sb("upper_s", [P, P])
        lower_s = sb("lower_s", [P, P])
        level = sb("level", [P, LEVELS, P])
        level0_low = sb("level0_low", [P, P])
        vt = sb("vt", [P, n_tables * P])
        idx = sb("idx", [P, P])
        small = sb("small", [P, 96])
        mod = sb("mod", [P, 96])
        mod_gain = sb("mod_gain", [P, 4 * ND])
        beta_nat = sb("beta_nat", [P, NT, 4])
        g_nat = sb("g_nat", [P, NT, 4])
        gc_nat = sb("gc_nat", [P, NT, 4])
        ps = [ctx.enter_context(nc.psum_tensor(f"ps{i}", [P, T], F32)) for i in range(8)]

        w_load = [sem(f"w_load{s}") for s in range(4)]
        w_cut_hi = sem("w_cut_hi")
        w_ready = sem("w_ready")
        mm_done = sem("mm_done")
        bank_free = [sem(f"bank_free{b}") for b in range(2)]
        phase_end = {e: sem(f"phase_end_{e}") for e in ("pe", "act", "dve")}

        def loaded(q, j):
            return w_load[j], 16 * q + 16

        def ready(q, j):
            return w_ready, 4 * q + j + 1

        def done(q, j):
            return mm_done, 4 * q + j + 1

        def freed(q, j):
            return bank_free[j % 2], 2 * q + j // 2 + 1

        def exp_and_ln():
            nc.scalar.preload_act_table_set("natural_log_exp_and_others")

        class Phases:

            def __init__(self, eng, me):
                self.eng, self.me, self.n = eng, me, 0

            def enter(self):
                if self.n:
                    for e, s in phase_end.items():
                        if e != self.me:
                            self.eng.wait_ge(s, self.n)

            def leave(self):
                self.n += 1
                self.eng.drain().then_inc(phase_end[self.me], 1)

        quads, n_quads = {}, 0
        for name, count in [("gmlp", 2), ("delta", 4), ("out_e", 2), ("mlp0", 16), ("ple0", 2),
                            ("attn", 6), ("out_o", 2), ("mlp1", 16), ("ple1", 2),
                            ("conv", 3), ("hgrn", 4), ("out_ab", 2), ("mlp2", 16),
                            ("stick", 6), ("out_c", 2), ("mlp3", 16)]:
            quads[name] = n_quads
            n_quads += count
            if name == upto:
                break
        names = list(quads)

        def has(name):
            return name in quads

        mlp_w = [(dram["w_mlp1"][0], dram["w_mlp2"][0]), (dram["w_mlp1"][1], dram["w_mlp2"][1]),
                 (dram["mlp_w1_2"][0], dram["mlp_w2_2"][0]), (dram["mlp_w1_2"][1], dram["mlp_w2_2"][1])]
        proj_w = {"out_e": dram["w_out_e"][0], "out_o": dram["w_out_o"][0], "out_ab": dram["w_out_ab_2"][0],
                  "out_c": dram["w_out_c_2"][0], "ple0": dram["w_ple_gate"][0], "ple1": dram["w_ple_gate"][1]}

        gates_w = sb("gates_w", [P, ND, 8])
        gates_hi = sb("gates_hi", [P, ND, 8], F32R)
        gates_lo = sb("gates_lo", [P, ND, 8], F32R)
        gates_b = sb("gates_b", [P, 8])
        x_load, small_load, iota_done = sem("x_load"), sem("small_load"), sem("iota_done")
        ple_load = sem("ple_load")
        ada_load = [sem(f"ada_load{i}") for i in range(6)]
        out_sent = sem("out_sent")

        lam = small[:, 0:1]
        neg_lam = small[:, 1:2]
        q_gain_o = small[:, 2:3]
        sub_gain = small[:, 3:4]
        q_gain_s = small[:, 4:5]
        lb = small[:, 8:12]
        one_minus_lb = small[:, 12:16]
        neg_exp_a = small[:, 16:20]
        c_silu = small[:, 24:32]
        eps_col = small[:, 32:33]

        scratch_size = 26 * T
        arena = sb("arena", [P, scratch_size])
        arena_at = [0]

        def take(shape):
            n = int(math.prod(shape))
            a = arena[:, arena_at[0]:arena_at[0] + n]
            arena_at[0] += n
            assert arena_at[0] <= scratch_size, arena_at
            if len(shape) == 2:
                a = a.rearrange("p (a b) -> p a b", b=shape[1])
            if len(shape) == 3:
                a = a.rearrange("p (a b c) -> p a b c", b=shape[1], c=shape[2])
            return a

        def blocks(a):
            return a.rearrange("p (b t) -> p b t", t=P)

        def over_blocks(mask):
            return mask.unsqueeze(1).to_broadcast([P, NT, P])

        x_in = take([NT, D])
        table_in = take([n_tables, P])
        lam_in = take([4, 64])
        s_idx = take([P]).bitcast(I32)
        t_idx = take([P]).bitcast(I32)
        s_xor_t = take([P])
        arena_at[0] = 10 * T
        ada_w = take([6, D])
        ada_acc = take([2, D])
        arena_at[0] = scratch_size - 3 * T
        gmlp_ws = take([4, P])
        gmlp_wt = take([4, P])
        gmlp_bs = take([4, P])

        def transposed_rows(name):
            return dram[name].rearrange("l (n p) -> (l n) p", p=P)

        row_views = {
            "ln_mix_e": transposed_rows("ln_mix_e"), "ln_mix_o": transposed_rows("ln_mix_o"),
            "ln_mlp": transposed_rows("ln_mlp"), "ln_ple": transposed_rows("ln_ple"),
            "gmlp_v_gain": transposed_rows("gmlp_v_gain"), "gdn_out_gain": dram["gdn_out_gain"],
            "gdn_conv": dram["gdn_conv"].rearrange("l t (n p) -> (l t n) p", p=P),
            "attn_sub_gain": dram["attn_sub_gain"],
            "norm_mix_2": transposed_rows("norm_mix_2"), "norm_mlp_2": transposed_rows("norm_mlp_2"),
            "c_2": transposed_rows("c_2"), "hg_norm_2": transposed_rows("hg_norm_2"),
            "conv_w_2": dram["conv_w_2"].rearrange("l t (n p) -> (l t n) p", p=P),
            "lb_logits_2": transposed_rows("lb_logits_2"),
            "ada_b_2": transposed_rows("ada_b_2"),
        }
        doubled = {"attn_q_gain": "attn_q_gain", "attn_k_gain": "attn_k_gain",
                   "q_norm_2": "q_norm_2", "k_norm_2": "k_norm_2"}

        def weight_chunk(sp, q, j, src):
            if not (isinstance(q, int) and q == 0):
                sp.wait_ge(*ready(q - 1, j))
            sp.dma_start(w_raw[:, j, :, :], src.rearrange("(k p) n -> p k n", p=P)).then_inc(w_load[j], 16)

        def stream(sp):
            sp_square(sp, "gmlp", lambda c: dram["w_in_e"][0][:, bass.ds((c % 2) * 512 + (c // 2) * P, P)], 8)
            if has("delta"):
                with sp.Fori(0, 4) as head:
                    for j in range(4):
                        weight_chunk(sp, quads["delta"] + head, j,
                                     dram["w_in_e"][0][:, bass.ds(head * P + (1024 + 512 * j), P)])
            for name in names:
                if name in proj_w:
                    with sp.Fori(0, 2) as i:
                        for j in range(4):
                            weight_chunk(sp, quads[name] + i, j, proj_w[name][:, bass.ds(i * 512 + j * P, P)])
                elif name in ("mlp0", "mlp1"):
                    layer = int(name[3])
                    w1, w2 = mlp_w[layer]
                    with sp.Fori(0, 2) as pair:
                        for half in range(2):
                            for n in range(16):
                                q = quads[name] + 8 * pair + 4 * half + n // 4
                                if n < 8:
                                    weight_chunk(sp, q, n % 4, w1[:, bass.ds(pair * 2048 + half * 1024 + n * P, P)])
                                else:
                                    weight_chunk(sp, q, n % 4,
                                                 w2[bass.ds(pair * 2048 + half * 1024, 1024), (n - 8) * P:(n - 7) * P])
                                for m in ada_loads_at(n):
                                    ada_load_one(sp, layer, pair, 12 * half + m)
                elif name.startswith("mlp"):
                    w1, w2 = mlp_w[int(name[3])]
                    with sp.Fori(0, 4) as i:
                        for n in range(8):
                            weight_chunk(sp, quads[name] + 4 * i + n // 4, n % 4,
                                         w1[:, bass.ds(i * 1024 + n * P, P)])
                        for n in range(8):
                            weight_chunk(sp, quads[name] + 4 * i + 2 + n // 4, n % 4,
                                         w2[bass.ds(i * 1024, 1024), n * P:(n + 1) * P])
                elif name in ("attn", "stick"):
                    w = dram["w_qkv_o"][0] if name == "attn" else dram["w_qkv_2"][0]
                    with sp.Fori(0, 2) as i:
                        for c in range(12):
                            weight_chunk(sp, quads[name] + 3 * i + c // 4, c % 4,
                                         w[:, bass.ds(i * 512 + (c // 3) * P + (c % 3) * 1024, P)])
                elif name == "conv":
                    sp_square(sp, "conv", lambda c: dram["w_in_ab_2"][0][:, bass.ds((c % 3) * 512 + (c // 3) * P, P)], 12)
                elif name == "hgrn":
                    with sp.Fori(0, 4) as head:
                        for j in range(4):
                            weight_chunk(sp, quads["hgrn"] + head, j,
                                         dram["w_in_ab_2"][0][:, bass.ds(head * P + (1536 + 512 * j), P)])

        def ada_loads_at(n):
            return range(12 * min(n, 14) // 14, 12 * min(n + 1, 14) // 14)

        def ada_load_one(sp, layer, pair, m):
            part, k = divmod(m, ND)
            sp.wait_ge(ada_read, 48 * layer + m + 1 + 24 * pair)
            src = dram["ada_w_2"][layer][k * P:(k + 1) * P, bass.ds(pair * 3 * D + part * D, D)]
            sp.dma_start(ada_w[:, m % 6, :], src).then_inc(ada_load[m % 6], 16)

        def sp_square(sp, name, src, count):
            for c in range(count):
                weight_chunk(sp, quads[name] + c // 4, c % 4, src(c))

        def cut_hi(q, j):
            nc.gpsimd.tensor_scalar(w_hi[:, j, :, :], w_raw[:, j, :, :], 1.0, 1.0, ALU.mult, ALU.mult
                                    ).then_inc(w_cut_hi, 1)

        def cut_lo(pool, q, j):
            pool.wait_ge(w_cut_hi, 4 * q + j + 1)
            nc.gpsimd.tensor_tensor(w_lo[:, j, :, :], w_raw[:, j, :, :], w_hi[:, j, :, :].bitcast(F32),
                                    ALU.subtract).then_inc(w_ready, 1)

        def cut_stream(pool):
            for j in range(4):
                pool.wait_ge(*loaded(0, j))
                if j:
                    cut_lo(pool, 0, j - 1)
                cut_hi(0, j)
            with pool.Fori(1, n_quads) as q:
                for j in range(4):
                    pool.wait_ge(*loaded(q, j))
                    pool.wait_ge(*done(q - 1, j))
                    if j:
                        cut_lo(pool, q, j - 1)
                    else:
                        cut_lo(pool, q - 1, 3)
                    cut_hi(q, j)
            cut_lo(pool, n_quads - 1, 3)

        def dense(pe, q, j, hi, lo, rhs_ready=None, ks=range(ND)):
            if ks[0] == 0:
                pe.wait_ge(*ready(q, j))
                if not (isinstance(q, int) and q == 0 and j < 2):
                    pe.wait_ge(bank_free[j % 2], 2 * q + j // 2)
            bank = ps[j % 2]
            for k in ks:
                if rhs_ready is not None:
                    pe.wait_ge(*rhs_ready(k))
                nc.tensor.matmul(bank[:, :], w_hi[:, j, k, :], hi[:, k, :], start=(k == 0), stop=False)
                nc.tensor.matmul(bank[:, :], w_hi[:, j, k, :], lo[:, k, :], start=False, stop=False)
                last = nc.tensor.matmul(bank[:, :], w_lo[:, j, k, :], hi[:, k, :], start=False, stop=(k == ND - 1))
            if ks[-1] == ND - 1:
                last.then_inc(mm_done, 1)

        setup_dve = sem("setup_dve")
        consts_ready = sem("consts_ready")
        x_turned, x_copied = sem("x_turned"), sem("x_copied")
        table_turned, table_copied = sem("table_turned"), sem("table_copied")
        ws_turned, ws_copied = sem("ws_turned"), sem("ws_copied")
        acted = sem("setup_acted")
        for_act = sem("setup_for_act")
        ada_summed, ada_turned = sem("ada_summed"), sem("ada_turned")
        ada_read = sem("ada_read")
        mod_ready = sem("mod_ready")

        def setup_sync(sp):
            for b in range(NT):
                sp.dma_start(x_in[:, b, :], dram["x"][0][b * P:(b + 1) * P, :]).then_inc(x_load, 16)

        def setup_loads(act):
            n = 0

            def load(dst, src):
                nonlocal n
                act.dma_start(dst, src).then_inc(small_load, 16)
                n += 16
            for name, at, count in rows:
                t, r = divmod(at, P)
                if name in doubled:
                    load(table_in[r:r + 1, t, 0:64], dram[name])
                    load(table_in[r:r + 1, t, 64:128], dram[name])
                else:
                    load(table_in[r:r + count, t, :], row_views[name])
            load(lam_in[:, :, :], dram["diff_lambda"].to_broadcast([P, 4, 64]))
            load(gates_b[:, 0:4], dram["gdn_a_log"].to_broadcast([P, 4]))
            load(gates_b[:, 4:8], dram["gdn_dt_bias"].to_broadcast([P, 4]))
            load(gmlp_ws[:, :, :], dram["gmlp_ws"][0].rearrange("g t s -> t g s"))
            load(gmlp_bs[:, :, :], dram["gmlp_bs"].to_broadcast([P, 4, P]))
            with nc.allow_non_contiguous_dma(reason="eight columns of w_in_e"):
                load(gates_w[:, :, :], dram["w_in_e"][0].rearrange("(k p) n -> p k n", p=P)[:, :, 3072:3080])
            return n

        rows_in_table = [max(at + n - t * P for _, at, n in rows if at // P == t) for t in range(n_tables)]
        n_small = 16 * (len(rows) + 4 + 6)

        def setup_gpsimd(pool):
            nc.gpsimd.iota(idx[:, :], [[1, P]], base=0, channel_multiplier=-1,
                           allow_small_or_imprecise_dtypes=True).then_inc(iota_done, 1)
            nc.gpsimd.iota(s_idx, [[0, P]], base=0, channel_multiplier=1).then_inc(iota_done, 1)
            nc.gpsimd.iota(t_idx, [[1, P]], base=0, channel_multiplier=0).then_inc(iota_done, 1)
            pool.wait_ge(table_copied, 1)

        def setup_scalar(act):
            setup_loads(act)
            for n in range(8):
                act.wait_ge(x_turned, n + 1)
                nc.scalar.activation(h[:, n, :], ps[2 + n % 2][:, :], ACT.Copy).then_inc(x_copied, 1)
            act.wait_ge(small_load, n_small)
            nc.scalar.activation(neg_exp_a, gates_b[:, 0:4], ACT.Exp).then_inc(acted, 1)
            act.wait_ge(for_act, 1)
            nc.scalar.activation(small[:, 40:42], small[:, 38:40], ACT.Exp).then_inc(acted, 1)
            act.wait_ge(for_act, 2)
            nc.scalar.activation(small[:, 56:68], small[:, 44:56], ACT.Exp).then_inc(acted, 1)
            nc.scalar.activation(c_silu, vt[:, col["c_2"]:col["c_2"] + ND], ACT.Silu).then_inc(acted, 1)
            exp_and_ln()

        def setup_tensor(pe):
            pe.wait_ge(consts_ready, 1)
            pe.wait_ge(small_load, n_small)
            for t in range(n_tables):
                r = rows_in_table[t]
                last = nc.tensor.transpose(ps[4][:, t * P:t * P + r], table_in[0:r, t, :], ident[0:r, 0:r])
            last.then_inc(table_turned, 1)
            for g in range(4):
                last = nc.tensor.transpose(ps[5][:, g * P:(g + 1) * P], gmlp_ws[:, g, :], ident[:, :])
            last.then_inc(ws_turned, 1)
            pe.wait_ge(x_load, 16 * NT)
            for n in range(ND):
                if n >= 2:
                    pe.wait_ge(x_copied, n - 1)
                for b in range(NT):
                    last = nc.tensor.transpose(ps[2 + n % 2][:, b * P:(b + 1) * P], x_in[:, b, n * P:(n + 1) * P],
                                               ident[:, :])
                last.then_inc(x_turned, 1)

        def ada_sum(pe, layer, pair, part):
            pe.wait_ge(ada_summed, 3 * pair + (6 * layer + part + 1))
            for n in range(8):
                c = part * 8 + n
                last = nc.tensor.matmul(ps[6][:, bass.ds(pair * 24 + c, 1)], ada_acc[:, part % 2, n * P:(n + 1) * P],
                                        ones[:, 0:1], start=True, stop=True)
            last.then_inc(ada_turned, 1)

        def ada_product(v, layer, pair, m):
            part, k = divmod(m, ND)
            acc, w = ada_acc[:, part % 2, :], ada_w[:, m % 6, :]
            v.wait_ge(ada_load[m % 6], 64 * pair + (128 * layer + 16 * (m // 6 + 1)))
            if k:
                v.wait_ge(ada_read, 24 * pair + (6 + 48 * layer + m))
                ins = nc.vector.scalar_tensor_tensor(out=acc, in0=w, scalar=c_silu[:, k:k + 1], in1=acc,
                                                     op0=ALU.mult, op1=ALU.add)
            else:
                v.wait_ge(ada_turned, 3 * pair + (6 * layer + (2 if part == 2 else 1)))
                ins = nc.vector.tensor_scalar(acc, w, c_silu[:, 0:1], None, ALU.mult)
            ins.then_inc(ada_read, 1)
            if k == ND - 1:
                v.wait_ge(ada_read, 24 * pair + (6 + 48 * layer + m + 1))
                nc.vector.tensor_copy(small[:, 36:37], ones[:, 0:1]).then_inc(ada_summed, 1)

        def ada_finish(v, layer):
            v.wait_ge(ada_turned, 6 * layer + 7)
            at = 48 * layer
            nc.vector.tensor_tensor(mod[:, at:at + 48], ps[6][:, 0:48], vt[:, col["ada_b_2"] + at:col["ada_b_2"] + at + 48],
                                    ALU.add).then_inc(mod_ready, 1)
            v.wait_ge(mod_ready, layer + 1)
            for i, name, scale_at in [(2 * layer, "norm_mix_2", at + 8), (2 * layer + 1, "norm_mlp_2", at + 32)]:
                g = vt[:, col[name] + 8 * layer:col[name] + 8 * layer + 8]
                nc.vector.scalar_tensor_tensor(out=mod_gain[:, 8 * i:8 * i + 8], in0=mod[:, scale_at:scale_at + 8],
                                               scalar=1.0, in1=g, op0=ALU.add, op1=ALU.mult)

        def setup_vector(v):
            chain = [0]

            def link(ins):
                chain[0] += 1
                ins.then_inc(setup_dve, 1)
                v.wait_ge(setup_dve, chain[0])

            link(nc.vector.memset(ones[:, :], 1.0))
            link(nc.vector.memset(small[:, :], 0.0))
            link(nc.vector.memset(eps_col, EPS))
            v.wait_ge(iota_done, 3)
            link(nc.vector.tensor_scalar(ident[:, :], idx[:, :], 0.0, None, ALU.is_equal))
            link(nc.vector.tensor_scalar(upper[:, :], idx[:, :], 0.0, None, ALU.is_ge))
            link(nc.vector.tensor_scalar(upper_s[:, :], idx[:, :], 0.0, None, ALU.is_gt))
            link(nc.vector.tensor_scalar(lower_s[:, :], idx[:, :], 0.0, None, ALU.is_lt))
            link(nc.vector.tensor_tensor(t_idx, s_idx, t_idx, ALU.bitwise_xor))
            link(nc.vector.tensor_copy(s_xor_t, t_idx))
            link(nc.vector.tensor_scalar(ones64[:, :], s_xor_t, 64.0, None, ALU.is_lt))
            for lv in range(LEVELS):
                link(nc.vector.tensor_scalar(level[:, lv, :], s_xor_t, float(2 ** (lv + 1)), None, ALU.is_lt))
            for lv in range(LEVELS - 1, 0, -1):
                link(nc.vector.tensor_tensor(level[:, lv, :], level[:, lv, :], level[:, lv - 1, :], ALU.subtract))
            link(nc.vector.tensor_tensor(level0_low[:, :], level[:, 0, :], lower_s[:, :], ALU.mult))
            for lv in range(LEVELS):
                link(nc.vector.tensor_tensor(level[:, lv, :], level[:, lv, :], upper_s[:, :], ALU.mult))
            nc.vector.tensor_copy(small[:, 33:34], ones[:, 0:1]).then_inc(consts_ready, 1)

            v.wait_ge(table_turned, 1)
            for t in range(n_tables):
                s = slice(t * P, t * P + rows_in_table[t])
                last = nc.vector.tensor_copy(vt[:, s], ps[4][:, s])
            last.then_inc(table_copied, 1)
            v.wait_ge(table_copied, 1)
            v.wait_ge(ws_turned, 1)
            link(nc.vector.tensor_tensor(gmlp_wt[:, :, :], blocks(ps[5][:, :]), over_blocks(upper[:, :]), ALU.mult))

            for i in range(2):
                link(nc.vector.tensor_tensor(lam_in[:, 2 * i, :], lam_in[:, 2 * i, :], lam_in[:, 2 * i + 1, :], ALU.mult))
                link(nc.vector.tensor_reduce(small[:, 38 + i:39 + i], lam_in[:, 2 * i, :], AX_X, ALU.add))
            nc.vector.tensor_copy(small[:, 34:35], ones[:, 0:1]).then_inc(for_act, 1)
            lg = [vt[:, col["lb_logits_2"] + 4 * i:col["lb_logits_2"] + 4 * i + 4] for i in range(3)]
            link(nc.vector.tensor_tensor(small[:, 68:72], lg[0], lg[1], ALU.max))
            link(nc.vector.tensor_tensor(small[:, 68:72], small[:, 68:72], lg[2], ALU.max))
            for i in range(3):
                link(nc.vector.tensor_tensor(small[:, 44 + 4 * i:48 + 4 * i], lg[i], small[:, 68:72], ALU.subtract))
            nc.vector.tensor_copy(small[:, 35:36], ones[:, 0:1]).then_inc(for_act, 1)
            v.wait_ge(acted, 4)
            link(nc.vector.tensor_scalar(neg_exp_a, neg_exp_a, -1.0, None, ALU.mult))
            link(nc.vector.tensor_scalar(lam, small[:, 40:41], small[:, 41:42], LAM_INIT, ALU.subtract, ALU.add))
            link(nc.vector.tensor_scalar(neg_lam, lam, -1.0, None, ALU.mult))
            link(nc.vector.tensor_tensor(small[:, 68:72], small[:, 56:60], small[:, 60:64], ALU.add))
            link(nc.vector.tensor_tensor(small[:, 68:72], small[:, 68:72], small[:, 64:68], ALU.add))
            link(nc.vector.reciprocal(small[:, 72:76], small[:, 68:72]))
            link(nc.vector.tensor_tensor(lb, small[:, 56:60], small[:, 72:76], ALU.mult))
            link(nc.vector.tensor_scalar(one_minus_lb, lb, -1.0, 1.0, ALU.mult, ALU.add))
            link(nc.vector.tensor_scalar(q_gain_o, vt[:, col["attn_q_gain"]:col["attn_q_gain"] + 1], 0.125, None, ALU.mult))
            link(nc.vector.tensor_scalar(q_gain_s, vt[:, col["q_norm_2"]:col["q_norm_2"] + 1], 0.125, None, ALU.mult))
            link(nc.vector.tensor_scalar(sub_gain, vt[:, col["attn_sub_gain"]:col["attn_sub_gain"] + 1],
                                         1.0 - LAM_INIT, None, ALU.mult))

            link(nc.vector.tensor_copy(gates_hi[:, :, :], gates_w[:, :, :]))
            link(nc.vector.tensor_tensor(gates_lo[:, :, :], gates_w[:, :, :], gates_hi[:, :, :].bitcast(F32), ALU.subtract))

        norm_pe = Steps(sem("norm_pe"), [f"sum{k}" for k in range(ND)])
        norm_act = Steps(sem("norm_act"), [f"sq{k}" for k in range(ND)] + ["ln", "rstd"] + [f"hi{k}" for k in range(ND)])
        norm_dve = Steps(sem("norm_dve"), ["t0", "t1"] + sum(([f"lo{k}", f"t{k + 2}"] for k in range(6)), [])
                         + ["lo6", "lo7"])

        def norm_gain(i, k):
            if i < 6:
                name, base = [("ln_mix_e", 0), ("ln_mlp", 0), ("ln_ple", 0),
                              ("ln_mix_o", 0), ("ln_mlp", 8), ("ln_ple", 8)][i]
                c = col[name] + base + k
                return vt[:, c:c + 1], 0.0
            n = i - 6
            s = 24 * n + k
            return mod_gain[:, 8 * n + k:8 * n + k + 1], mod[:, s:s + 1]

        def norm_tensor(pe, i):
            for k in range(ND):
                pe.wait_ge(*norm_act.at(i, f"sq{k}"))
                nc.tensor.matmul(ps[2][:, :], ones[:, :], sq[:, k % 2, :], start=(k == 0),
                                 stop=(k == ND - 1)).then_inc(*norm_pe(f"sum{k}"))

        def norm_scalar(act, i):
            for k in range(ND):
                if k >= 2:
                    act.wait_ge(*norm_pe.at(i, f"sum{k - 2}"))
                nc.scalar.activation(sq[:, k % 2, :], h[:, k, :], ACT.Square).then_inc(*norm_act(f"sq{k}"))
            act.wait_ge(*norm_pe.at(i, "sum7"))
            nc.scalar.activation(rb[:, 1, :], ps[2][:, :], ACT.Ln, scale=1.0 / D, bias=eps_col).then_inc(*norm_act("ln"))
            act.wait_ge(*norm_act.at(i, "ln"))
            nc.scalar.activation(rb[:, 0, :], rb[:, 1, :], ACT.Exp, scale=-0.5).then_inc(*norm_act("rstd"))
            for k in range(ND):
                act.wait_ge(*norm_dve.at(i, f"t{k}"))
                nc.scalar.activation(x_hi[:, k, :], tt[:, k % 3, :], ACT.Identity,
                                     bias=norm_gain(i, k)[1]).then_inc(*norm_act(f"hi{k}"))

        def norm_vector(v, i):
            def full(k):
                gain, _ = norm_gain(i, k)
                if k >= 3:
                    v.wait_ge(*norm_dve.at(i, f"lo{k - 3}"))
                nc.vector.scalar_tensor_tensor(out=tt[:, k % 3, :], in0=h[:, k, :], scalar=gain, in1=rb[:, 0, :],
                                               op0=ALU.mult, op1=ALU.mult).then_inc(*norm_dve(f"t{k}"))
            v.wait_ge(*norm_act.at(i, "rstd"))
            full(0)
            full(1)
            for k in range(ND):
                v.wait_ge(*norm_act.at(i, f"hi{k}"))
                nc.vector.scalar_tensor_tensor(out=x_lo[:, k, :], in0=tt[:, k % 3, :], scalar=norm_gain(i, k)[1],
                                               in1=x_hi[:, k, :].bitcast(F32), op0=ALU.add,
                                               op1=ALU.subtract).then_inc(*norm_dve(f"lo{k}"))
                if k + 2 < ND:
                    full(k + 2)

        def gate_col(block2_layer, half, n):
            if block2_layer is None:
                return 1.0
            c = 48 * block2_layer + 24 * half + 16 + n
            return mod[:, c:c + 1]

        def add_chunk(v, q, j, n, gate):
            v.wait_ge(*done(q, j))
            nc.vector.scalar_tensor_tensor(out=h[:, n, :], in0=ps[j % 2][:, :], scalar=gate, in1=h[:, n, :],
                                           op0=ALU.mult, op1=ALU.add).then_inc(bank_free[j % 2], 1)

        def project_tensor(pe, name):
            for n in range(8):
                dense(pe, quads[name] + n // 4, n % 4, m_hi, m_lo)

        def project_vector(v, name, layer2):
            for n in range(8):
                add_chunk(v, quads[name] + n // 4, n % 4, n, gate_col(layer2, 0, n))

        mlp_act = Steps(sem("mlp_act"), [f"hi{n}" for n in range(8)])
        mlp_dve = Steps(sem("mlp_dve"), sum(([f"square{n}", f"lo{n}"] for n in range(8)), []))
        relu = sq

        def mlp_quarters(eng, i):
            q, u = quads[f"mlp{i}"], 4 * i
            if i >= 2:
                with eng.Fori(0, 4) as quarter:
                    yield u + quarter, q + 4 * quarter, None, 0
            else:
                with eng.Fori(0, 2) as pair:
                    for half in range(2):
                        yield u + 2 * pair + half, q + 8 * pair + 4 * half, pair, half

        ADA_SUMS = [(0, 3), (1, 1), (1, 7)]

        def mlp_tensor(pe, i):
            for u, q, pair, half in mlp_quarters(pe, i):
                for n in range(8):
                    dense(pe, q + n // 4, n % 4, x_hi, x_lo)
                for n in range(8):
                    dense(pe, q + 2 + n // 4, n % 4, m_hi, m_lo,
                          rhs_ready=(lambda k: mlp_dve.at(u, f"lo{k}")) if n == 0 else None)
                    if pair is not None and (half, n) in ADA_SUMS:
                        ada_sum(pe, i, pair, ADA_SUMS.index((half, n)))

        def mlp_scalar(act, i):
            for u, q, pair, half in mlp_quarters(act, i):
                for n in range(8):
                    qq, j = q + n // 4, n % 4
                    act.wait_ge(*done(qq, j))
                    if n >= 2:
                        act.wait_ge(*mlp_dve.at(u, f"square{n - 2}"))
                    nc.scalar.activation(relu[:, n % 2, :], ps[j % 2][:, :], ACT.Relu).then_inc(bank_free[j % 2], 1)
                    act.wait_ge(*mlp_dve.at(u, f"square{n}"))
                    nc.scalar.activation(m_hi[:, n, :], tt[:, n % 3, :], ACT.Copy).then_inc(*mlp_act(f"hi{n}"))

        def mlp_vector(v, i, layer2):
            if i == 0:
                for slot in range(6):
                    nc.vector.tensor_copy(small[:, 35:36], ones[:, 0:1]).then_inc(ada_read, 1)
                    v.wait_ge(ada_read, slot + 1)
                nc.vector.tensor_copy(small[:, 35:36], ones[:, 0:1]).then_inc(ada_turned, 1)
                v.wait_ge(ada_turned, 1)
            for u, q, pair, half in mlp_quarters(v, i):
                for n in range(8):
                    v.wait_ge(*freed(q + n // 4, n % 4))
                    if n >= 3:
                        v.wait_ge(*mlp_dve.at(u, f"lo{n - 3}"))
                    nc.vector.tensor_tensor(tt[:, n % 3, :], relu[:, n % 2, :], relu[:, n % 2, :],
                                            ALU.mult).then_inc(*mlp_dve(f"square{n}"))
                    v.wait_ge(*mlp_act.at(u, f"hi{n}"))
                    nc.vector.tensor_tensor(m_lo[:, n, :], tt[:, n % 3, :], m_hi[:, n, :].bitcast(F32),
                                            ALU.subtract).then_inc(*mlp_dve(f"lo{n}"))
                    if pair is not None:
                        for m in ada_loads_at(n):
                            ada_product(v, i, pair, 12 * half + m)
                for n in range(8):
                    add_chunk(v, q + 2 + n // 4, n % 4, n, gate_col(layer2, 1, n))
                    if pair is not None:
                        for m in ada_loads_at(8 + n):
                            ada_product(v, i, pair, 12 * half + m)
            if i < 2:
                ada_finish(v, i)

        arena_at[0] = 0
        ple_w = take([2, D])
        p_in = take([NT, 256])
        p_t = take([2, T])
        ple_pe = Steps(sem("ple_pe"), ["p0", "p1"] + [f"proj{n}" for n in range(8)])
        ple_act = Steps(sem("ple_act"), ["p0", "p1"])
        ple_dve = Steps(sem("ple_dve"), [f"mul{n}" for n in range(8)] + ["add"])

        def ple_loads(act, i):
            act.dma_start(ple_w[:, :, :], dram["w_ple_proj"][i].rearrange("(k p) n -> p k n", p=P)).then_inc(ple_load, 16)
            act.dma_start(p_in[:, :, :], dram["p"][i][0].rearrange("(b p) n -> p b n", p=P)).then_inc(ple_load, 16)

        def ple_tensor(pe, i):
            q = quads[f"ple{i}"]
            pe.wait_ge(ple_load, 32 * i + 32)
            for k in range(2):
                for b in range(NT):
                    last = nc.tensor.transpose(ps[3 + k][:, b * P:(b + 1) * P], p_in[:, b, k * P:(k + 1) * P], ident[:, :])
                last.then_inc(*ple_pe(f"p{k}"))
            for n in range(8):
                dense(pe, q + n // 4, n % 4, x_hi, x_lo)
                if n < 2:
                    pe.wait_ge(*ple_act.at(i, "p1"))
                else:
                    pe.wait_ge(*ple_dve.at(i, f"mul{n - 2}"))
                for k in range(2):
                    last = nc.tensor.matmul(ps[3 + n % 2][:, :], ple_w[:, k, n * P:(n + 1) * P], p_t[:, k, :],
                                            start=(k == 0), stop=(k == 1))
                last.then_inc(*ple_pe(f"proj{n}"))

        def ple_scalar(act, i):
            q = quads[f"ple{i}"]
            for k in range(2):
                act.wait_ge(*ple_pe.at(i, f"p{k}"))
                nc.scalar.activation(p_t[:, k, :], ps[3 + k][:, :], ACT.Copy).then_inc(*ple_act(f"p{k}"))
            for n in range(8):
                act.wait_ge(*done(q + n // 4, n % 4))
                if n >= 2:
                    act.wait_ge(*ple_dve.at(i, f"mul{n - 2}"))
                nc.scalar.activation(sq[:, n % 2, :], ps[n % 2][:, :], ACT.Sigmoid).then_inc(bank_free[n % 2], 1)
            exp_and_ln()

        def ple_vector(v, i):
            q = quads[f"ple{i}"]
            for n in range(8):
                v.wait_ge(*freed(q + n // 4, n % 4))
                v.wait_ge(*ple_pe.at(i, f"proj{n}"))
                if n >= 3:
                    v.wait_ge(ple_add, 8 * i + n - 2)
                nc.vector.tensor_tensor(tt[:, n % 3, :], ps[3 + n % 2][:, :], sq[:, n % 2, :],
                                        ALU.mult).then_inc(*ple_dve(f"mul{n}"))
                v.wait_ge(*ple_dve.at(i, f"mul{n}"))
                nc.vector.tensor_tensor(h[:, n, :], h[:, n, :], tt[:, n % 3, :], ALU.add).then_inc(ple_add, 1)

        ple_dve.names.remove("add")
        ple_add = sem("ple_add")

        def rsqrt(act, steps, unit, name, src, dst, tmp, scale):
            nc.scalar.activation(tmp, src, ACT.Ln, scale=scale, bias=eps_col).then_inc(*steps(f"{name}_ln"))
            act.wait_ge(*steps.at(unit, f"{name}_ln"))
            nc.scalar.activation(dst, tmp, ACT.Exp, scale=-0.5).then_inc(*steps(f"{name}_rs"))

        arena_at[0] = 0
        gm_u, gm_v, gm_xc, gm_tmp = take([T]), take([T]), take([T]), take([T])
        gm_nat, gm_s = take([NT, P]), take([T])
        gmlp_pe = Steps(sem("gmlp_pe"), ["mean", "var", "turn", "mix"])
        gmlp_act = Steps(sem("gmlp_act"), ["sq", "v_ln", "v_rs", "nat", "hi"])
        gmlp_dve = Steps(sem("gmlp_dve"), ["xc", "vn", "s", "us", "lo"])

        def gmlp_chunks(g):
            c = 2 * g
            q = quads["gmlp"]
            return (q + c // 4, c % 4), (q + (c + 1) // 4, (c + 1) % 4)

        def gmlp_tensor(pe):
            for g in range(4):
                for q, j in gmlp_chunks(g):
                    dense(pe, q, j, x_hi, x_lo)
                pe.wait_ge(*freed(*gmlp_chunks(g)[1]))
                nc.tensor.matmul(ps[2][:, :], ones[:, :], gm_v, start=True, stop=True).then_inc(*gmlp_pe("mean"))
                pe.wait_ge(*gmlp_act.at(g, "sq"))
                nc.tensor.matmul(ps[3][:, :], ones[:, :], sq[:, 0, :], start=True, stop=True).then_inc(*gmlp_pe("var"))
                pe.wait_ge(*gmlp_dve.at(g, "vn"))
                for b in range(NT):
                    last = nc.tensor.transpose(ps[4][:, b * P:(b + 1) * P], gm_xc[:, b * P:(b + 1) * P], ident[:, :])
                last.then_inc(*gmlp_pe("turn"))
                pe.wait_ge(*gmlp_act.at(g, "nat"))
                for b in range(NT):
                    last = nc.tensor.matmul(ps[5][:, b * P:(b + 1) * P], gm_nat[:, b, :], gmlp_wt[:, g, :],
                                            start=True, stop=True)
                last.then_inc(*gmlp_pe("mix"))

        def gmlp_scalar(act):
            for g in range(4):
                (qu, ju), (qv, jv) = gmlp_chunks(g)
                act.wait_ge(*done(qu, ju))
                if g:
                    act.wait_ge(*gmlp_dve.at(g - 1, "us"))
                nc.scalar.activation(gm_u, ps[ju % 2][:, :], ACT.Gelu_apprx_tanh).then_inc(bank_free[ju % 2], 1)
                act.wait_ge(*done(qv, jv))
                nc.scalar.activation(gm_v, ps[jv % 2][:, :], ACT.Gelu_apprx_tanh).then_inc(bank_free[jv % 2], 1)
                exp_and_ln()
                act.wait_ge(*gmlp_dve.at(g, "xc"))
                nc.scalar.activation(sq[:, 0, :], gm_xc, ACT.Square).then_inc(*gmlp_act("sq"))
                act.wait_ge(*gmlp_pe.at(g, "var"))
                rsqrt(act, gmlp_act, g, "v", ps[3][:, :], rb[:, 0, :], rb[:, 1, :], 1.0 / P)
                act.wait_ge(*gmlp_pe.at(g, "turn"))
                nc.scalar.activation(gm_nat.rearrange("p b t -> p (b t)"), ps[4][:, :], ACT.Copy).then_inc(*gmlp_act("nat"))
                act.wait_ge(*gmlp_dve.at(g, "us"))
                nc.scalar.activation(m_hi[:, g, :], tt[:, 0, :], ACT.Copy).then_inc(*gmlp_act("hi"))

        def gmlp_vector(v):
            for g in range(4):
                v.wait_ge(*freed(*gmlp_chunks(g)[1]))
                v.wait_ge(*gmlp_pe.at(g, "mean"))
                nc.vector.scalar_tensor_tensor(out=gm_xc, in0=ps[2][:, :], scalar=-1.0 / P, in1=gm_v, op0=ALU.mult,
                                               op1=ALU.add).then_inc(*gmlp_dve("xc"))
                v.wait_ge(*gmlp_dve.at(g, "xc"))
                v.wait_ge(*gmlp_act.at(g, "v_rs"))
                nc.vector.tensor_tensor(gm_xc, gm_xc, rb[:, 0, :], ALU.mult).then_inc(*gmlp_dve("vn"))
                c = col["gmlp_v_gain"] + g
                v.wait_ge(*gmlp_pe.at(g, "mix"))
                nc.vector.scalar_tensor_tensor(out=blocks(gm_s), in0=blocks(ps[5][:, :]), scalar=vt[:, c:c + 1],
                                               in1=over_blocks(gmlp_bs[:, g, :]), op0=ALU.mult,
                                               op1=ALU.add).then_inc(*gmlp_dve("s"))
                v.wait_ge(*gmlp_dve.at(g, "s"))
                nc.vector.tensor_tensor(tt[:, 0, :], gm_u, gm_s, ALU.mult).then_inc(*gmlp_dve("us"))
                v.wait_ge(*gmlp_act.at(g, "hi"))
                nc.vector.tensor_tensor(m_lo[:, g, :], tt[:, 0, :], m_hi[:, g, :].bitcast(F32),
                                        ALU.subtract).then_inc(*gmlp_dve("lo"))

        gates_pe = Steps(sem("gates_pe"), ["logits", "cumsum"])
        gates_act = Steps(sem("gates_act"), ["beta", "abs", "exp", "ln"])
        gates_dve = Steps(sem("gates_dve"), ["x", "copy", "sp", "g", "gc"])
        ga_x, ga_e = take([NT, 4]), take([NT, 4])
        ga_w = take([ND, 8])

        def gates_tensor(pe):
            for b in range(NT):
                t = slice(b * P, (b + 1) * P)
                for k in range(ND):
                    out_b = ps[6][:, b * 8:b * 8 + 8]
                    nc.tensor.matmul(out_b, x_hi[:, k, t], gates_hi[:, k, :], start=(k == 0), stop=False)
                    nc.tensor.matmul(out_b, x_lo[:, k, t], gates_hi[:, k, :], start=False, stop=False)
                    last = nc.tensor.matmul(out_b, x_hi[:, k, t], gates_lo[:, k, :], start=False, stop=(k == ND - 1))
            last.then_inc(*gates_pe("logits"))
            pe.wait_ge(*gates_dve.at(0, "g"))
            nc.tensor.matmul(ps[7][:, 0:16], upper[:, :], g_nat[:, :, :].rearrange("p b h -> p (b h)"), start=True,
                             stop=True).then_inc(*gates_pe("cumsum"))

        def gates_scalar(act):
            act.wait_ge(*gates_dve.at(0, "x"))
            logits = ps[6][:, 0:32].rearrange("p (b e) -> p b e", e=8)
            nc.scalar.activation(beta_nat[:, :, :], logits[:, :, 0:4], ACT.Sigmoid).then_inc(*gates_act("beta"))
            exp_and_ln()
            act.wait_ge(*gates_dve.at(0, "x"))
            nc.scalar.activation(ga_e, ga_x, ACT.Abs).then_inc(*gates_act("abs"))
            act.wait_ge(*gates_act.at(0, "abs"))
            act.wait_ge(*gates_dve.at(0, "copy"))
            nc.scalar.activation(ga_e, ga_e, ACT.Exp, scale=-1.0).then_inc(*gates_act("exp"))
            act.wait_ge(*gates_act.at(0, "exp"))
            nc.scalar.activation(ga_e, ga_e, ACT.Ln, bias=1.0).then_inc(*gates_act("ln"))

        def gates_vector(v):
            v.wait_ge(*gates_pe.at(0, "logits"))
            logits = ps[6][:, 0:32].rearrange("p (b e) -> p b e", e=8)
            nc.vector.tensor_tensor(ga_x, logits[:, :, 4:8], gates_b[:, 4:8].unsqueeze(1).to_broadcast([P, NT, 4]),
                                    ALU.add).then_inc(*gates_dve("x"))
            nc.vector.tensor_copy(small[:, 37:38], ones[:, 0:1]).then_inc(*gates_dve("copy"))
            v.wait_ge(*gates_act.at(0, "ln"))
            nc.vector.scalar_tensor_tensor(out=ga_x, in0=ga_x, scalar=0.0, in1=ga_e, op0=ALU.max,
                                           op1=ALU.add).then_inc(*gates_dve("sp"))
            v.wait_ge(*gates_dve.at(0, "sp"))
            nc.vector.tensor_tensor(g_nat[:, :, :], ga_x, neg_exp_a.unsqueeze(1).to_broadcast([P, NT, 4]),
                                    ALU.mult).then_inc(*gates_dve("g"))
            v.wait_ge(*gates_pe.at(0, "cumsum"))
            nc.vector.tensor_copy(gc_nat[:, :, :].rearrange("p b h -> p (b h)"), ps[7][:, 0:16]).then_inc(*gates_dve("gc"))

        arena_at[0] = 0
        dl_z, dl_q, dl_k, dl_v = take([T]), take([T]), take([T]), take([T])
        dl_gtri, dl_bdiag, dl_eg, dl_dt = take([NT, P]), take([NT, P]), take([T]), take([T])
        dl_at, dl_pt, dl_kb, dl_kd, dl_vb = take([T]), take([T]), take([T]), take([T]), take([T])
        dl_x, dl_y, dl_p, dl_am = take([T]), take([T]), take([T]), take([T])
        dl_w, dl_u, dl_qd, dl_vn, dl_s, dl_o = take([T]), take([T]), take([T]), take([T]), take([P]), take([T])
        dl_cols = take([48])
        taps = dl_cols[:, 0:12]
        gcol, gccol, bcol = dl_cols[:, 12:16], dl_cols[:, 16:20], dl_cols[:, 20:24]
        egcol, kdcol, becol = dl_cols[:, 24:28], dl_cols[:, 28:32], dl_cols[:, 32:36]

        lv_pe = sum(([f"p{l}"] + ([f"x{l}"] if l < 6 else []) + [f"y{l}"] for l in range(1, LEVELS)), [])
        scan_pe = sum((([f"ws{b}"] if b else []) + [f"o{b}"] + ([f"ds{b}"] if b < 3 else []) for b in range(NT)), [])
        delta_pe = Steps(sem("delta_pe"), ["rows_g", "rows_b", "q_sum", "k_sum", "k_turn", "v_turn", "kk", "qk", "a_turn"]
                         + lv_pe + ["w", "u"] + scan_pe + ["o_sum"])
        delta_act = Steps(sem("delta_act"), ["q_s", "k_s", "v_s", "q_sq", "k_sq", "eg", "egc", "q_ln", "q_rs", "k_ln",
                                             "k_rs", "dt", "kd_col", "kb", "kd", "vb"]
                          + [f"p{l}" for l in range(1, LEVELS)] + ["w", "u", "o_raw", "o_sq", "o_ln", "o_rs", "o_hi"])
        lv_dve = sum(([f"am{l}"] + ([f"xm{l}"] if l < 6 else []) + [f"ym{l}"] for l in range(1, LEVELS)), [])
        scan_dve = ["vn0"] + sum(([f"s{b}", f"vn{b + 1}"] for b in range(3)), [])
        delta_dve = Steps(sem("delta_dve"), ["taps", "g_col", "gc_col", "b_col", "gtri", "bdiag"]
                          + [f"{x}_tap{i}" for x in "qkv" for i in range(4)]
                          + ["dt_arg", "dt_mask", "kd_arg", "be", "q_n", "k_n", "q_dec", "at0", "at", "pt",
                             "y_m", "y", "x_m", "x"] + lv_dve + scan_dve + ["o_t", "o_g", "o_lo"])

        def delta_tensor(pe):
            with pe.Fori(0, 4) as u:
                q = quads["delta"] + u
                for j in range(4):
                    dense(pe, q, j, x_hi, x_lo)
                pe.wait_ge(*delta_dve.at(u, "gtri"))
                nc.tensor.matmul(ps[2][:, :], ones[:, :], dl_gtri.rearrange("p b t -> p (b t)"), start=True,
                                 stop=True).then_inc(*delta_pe("rows_g"))
                pe.wait_ge(*delta_dve.at(u, "bdiag"))
                nc.tensor.matmul(ps[3][:, :], ones[:, :], dl_bdiag.rearrange("p b t -> p (b t)"), start=True,
                                 stop=True).then_inc(*delta_pe("rows_b"))
                pe.wait_ge(*delta_act.at(u, "q_sq"))
                nc.tensor.matmul(ps[4][:, :], ones[:, :], sq[:, 0, :], start=True, stop=True).then_inc(*delta_pe("q_sum"))
                pe.wait_ge(*delta_act.at(u, "k_sq"))
                nc.tensor.matmul(ps[5][:, :], ones[:, :], sq[:, 1, :], start=True, stop=True).then_inc(*delta_pe("k_sum"))

                def each(bank, lhs, rhs, step, turn=False):
                    for b in range(NT):
                        s = slice(b * P, (b + 1) * P)
                        if turn:
                            last = nc.tensor.transpose(ps[bank][:, s], lhs[:, s], ident[:, :])
                        else:
                            last = nc.tensor.matmul(ps[bank][:, s], lhs[:, s], rhs[:, s], start=True, stop=True)
                    last.then_inc(*delta_pe(step))

                pe.wait_ge(*delta_dve.at(u, "q_dec"))
                each(6, dl_k, None, "k_turn", True)
                each(7, dl_v, None, "v_turn", True)
                each(4, dl_k, dl_k, "kk")
                each(5, dl_k, dl_q, "qk")
                pe.wait_ge(*delta_dve.at(u, "at"))
                pe.wait_ge(*delta_act.at(u, "kd"))
                each(6, dl_at, None, "a_turn", True)
                pe.wait_ge(*delta_act.at(u, "vb"))
                pe.wait_ge(*delta_dve.at(u, "pt"))
                for l in range(1, LEVELS):
                    pe.wait_ge(*delta_dve.at(u, f"am{l}"))
                    pe.wait_ge(*delta_dve.at(u, "x" if l == 1 else f"xm{l - 1}"))
                    each(7, dl_am, dl_x, f"p{l}")
                    pe.wait_ge(*delta_act.at(u, f"p{l}"))
                    pe.wait_ge(*delta_dve.at(u, "y" if l == 1 else f"ym{l - 1}"))
                    if l < 6:
                        each(4, dl_y, dl_p, f"x{l}")
                    each(5, dl_p, dl_y, f"y{l}")
                pe.wait_ge(*delta_dve.at(u, "ym6"))
                each(6, dl_kb, dl_y, "w")
                each(7, dl_y, dl_vb, "u")
                for b in range(NT):
                    s = slice(b * P, (b + 1) * P)
                    if b:
                        pe.wait_ge(*delta_act.at(u, "w"))
                        pe.wait_ge(*delta_dve.at(u, f"s{b - 1}"))
                        nc.tensor.matmul(ps[4][:, s], dl_w[:, s], dl_s, start=True, stop=True).then_inc(*delta_pe(f"ws{b}"))
                        nc.tensor.matmul(ps[2][:, s], dl_s, dl_qd[:, s], start=True, stop=False)
                    pe.wait_ge(*delta_dve.at(u, f"vn{b}"))
                    nc.tensor.matmul(ps[2][:, s], dl_vn[:, s], dl_pt[:, s], start=(b == 0),
                                     stop=True).then_inc(*delta_pe(f"o{b}"))
                    if b < 3:
                        nc.tensor.matmul(ps[5][:, s], dl_kd[:, s], dl_vn[:, s], start=True,
                                         stop=True).then_inc(*delta_pe(f"ds{b}"))
                pe.wait_ge(*delta_act.at(u, "o_sq"))
                nc.tensor.matmul(ps[3][:, :], ones[:, :], sq[:, 0, :], start=True, stop=True).then_inc(*delta_pe("o_sum"))

        def delta_scalar(act):
            with act.Fori(0, 4) as u:
                q = quads["delta"] + u
                for x, buf in (("q", dl_q), ("k", dl_k), ("v", dl_v)):
                    act.wait_ge(*delta_dve.at(u, f"{x}_tap3"))
                    nc.scalar.activation(buf, buf, ACT.Silu).then_inc(*delta_act(f"{x}_s"))
                act.wait_ge(*done(q, 3))
                nc.scalar.activation(dl_z, ps[1][:, :], ACT.Silu).then_inc(bank_free[1], 1)
                exp_and_ln()
                act.wait_ge(*delta_act.at(u, "q_s"))
                nc.scalar.activation(sq[:, 0, :], dl_q, ACT.Square).then_inc(*delta_act("q_sq"))
                act.wait_ge(*delta_act.at(u, "k_s"))
                nc.scalar.activation(sq[:, 1, :], dl_k, ACT.Square).then_inc(*delta_act("k_sq"))
                act.wait_ge(*delta_pe.at(u, "rows_g"))
                nc.scalar.activation(dl_eg, ps[2][:, :], ACT.Exp).then_inc(*delta_act("eg"))
                act.wait_ge(*delta_dve.at(u, "gc_col"))
                nc.scalar.activation(egcol, gccol, ACT.Exp).then_inc(*delta_act("egc"))
                act.wait_ge(*delta_pe.at(u, "q_sum"))
                rsqrt(act, delta_act, u, "q", ps[4][:, :], rb[:, 0, :], tt[:, 1, :], 1.0)
                act.wait_ge(*delta_pe.at(u, "k_sum"))
                rsqrt(act, delta_act, u, "k", ps[5][:, :], rb[:, 1, :], tt[:, 2, :], 1.0)
                act.wait_ge(*delta_dve.at(u, "dt_arg"))
                nc.scalar.activation(dl_dt, dl_dt, ACT.Exp).then_inc(*delta_act("dt"))
                act.wait_ge(*delta_dve.at(u, "kd_arg"))
                nc.scalar.activation(kdcol, kdcol, ACT.Exp).then_inc(*delta_act("kd_col"))

                def scaled(dst, src, cols, step):
                    for b in range(NT):
                        s = slice(b * P, (b + 1) * P)
                        last = nc.scalar.activation(dst[:, s], src[:, s], ACT.Copy, scale=cols[:, b:b + 1])
                    last.then_inc(*delta_act(step))

                act.wait_ge(*delta_pe.at(u, "k_turn"))
                act.wait_ge(*delta_dve.at(u, "be"))
                scaled(dl_kb, ps[6], becol, "kb")
                act.wait_ge(*delta_act.at(u, "kd_col"))
                scaled(dl_kd, ps[6], kdcol, "kd")
                act.wait_ge(*delta_pe.at(u, "v_turn"))
                scaled(dl_vb, ps[7], bcol, "vb")
                for l in range(1, LEVELS):
                    act.wait_ge(*delta_pe.at(u, f"p{l}"))
                    nc.scalar.activation(dl_p, ps[7][:, :], ACT.Copy).then_inc(*delta_act(f"p{l}"))
                act.wait_ge(*delta_pe.at(u, "w"))
                nc.scalar.activation(dl_w, ps[6][:, :], ACT.Copy).then_inc(*delta_act("w"))
                act.wait_ge(*delta_pe.at(u, "u"))
                nc.scalar.activation(dl_u, ps[7][:, :], ACT.Copy).then_inc(*delta_act("u"))
                act.wait_ge(*delta_pe.at(u, "o3"))
                nc.scalar.activation(dl_o, ps[2][:, :], ACT.Copy).then_inc(*delta_act("o_raw"))
                act.wait_ge(*delta_act.at(u, "o_raw"))
                nc.scalar.activation(sq[:, 0, :], dl_o, ACT.Square).then_inc(*delta_act("o_sq"))
                act.wait_ge(*delta_pe.at(u, "o_sum"))
                rsqrt(act, delta_act, u, "o", ps[3][:, :], rb[:, 0, :], tt[:, 1, :], 1.0 / P)
                act.wait_ge(*delta_dve.at(u, "o_g"))
                nc.scalar.activation(m_hi[:, 4 + u, :], tt[:, 0, :], ACT.Copy).then_inc(*delta_act("o_hi"))

        def delta_vector(v):
            with v.Fori(0, 4) as u:
                q = quads["delta"] + u

                def own(name):
                    v.wait_ge(*delta_dve.at(u, name))

                c = col["gdn_conv"]
                nc.vector.tensor_copy(taps, vt[:, c:c + 48].rearrange("p (n h) -> p n h", h=4)[:, :, bass.ds(u, 1)]
                                      ).then_inc(*delta_dve("taps"))
                for name, dst, src in (("g_col", gcol, g_nat), ("gc_col", gccol, gc_nat), ("b_col", bcol, beta_nat)):
                    nc.vector.tensor_copy(dst, src[:, :, bass.ds(u, 1)]).then_inc(*delta_dve(name))
                own("b_col")
                for b in range(NT):
                    last = nc.vector.tensor_scalar(dl_gtri[:, b, :], upper[:, :], gcol[:, b:b + 1], None, ALU.mult)
                last.then_inc(*delta_dve("gtri"))
                for b in range(NT):
                    last = nc.vector.tensor_scalar(dl_bdiag[:, b, :], ident[:, :], bcol[:, b:b + 1], None, ALU.mult)
                last.then_inc(*delta_dve("bdiag"))
                for i, (x, buf) in enumerate((("q", dl_q), ("k", dl_k), ("v", dl_v))):
                    v.wait_ge(*done(q, i))
                    src = ps[i % 2]
                    nc.vector.tensor_scalar(buf, src[:, :], taps[:, 9 + i:10 + i], None, ALU.mult
                                            ).then_inc(*delta_dve(f"{x}_tap0"))
                    for n in range(1, 4):
                        own(f"{x}_tap{n - 1}")
                        t = taps[:, 3 * (3 - n) + i:3 * (3 - n) + i + 1]
                        nc.vector.scalar_tensor_tensor(out=buf[:, n:T], in0=src[:, 0:T - n], scalar=t, in1=buf[:, n:T],
                                                       op0=ALU.mult, op1=ALU.add).then_inc(*delta_dve(f"{x}_tap{n}"))
                    own(f"{x}_tap3")
                    nc.vector.tensor_copy(small[:, 76 + i:77 + i], ones[:, 0:1]).then_inc(bank_free[i % 2], 1)
                v.wait_ge(*delta_act.at(u, "eg"))
                for b in range(NT):
                    s = slice(b * P, (b + 1) * P)
                    last = nc.vector.tensor_scalar(dl_dt[:, s], ps[2][:, s], gccol[:, b:b + 1], 0.0, ALU.subtract, ALU.min)
                last.then_inc(*delta_dve("dt_arg"))
                v.wait_ge(*delta_act.at(u, "dt"))
                nc.vector.tensor_tensor(blocks(dl_dt), blocks(dl_dt), over_blocks(upper[:, :]), ALU.mult
                                        ).then_inc(*delta_dve("dt_mask"))
                nc.vector.tensor_tensor(kdcol, blocks(ps[2][:, :])[:, :, P - 1:P].rearrange("p b o -> p (b o)"), gccol,
                                        ALU.subtract).then_inc(*delta_dve("kd_arg"))
                v.wait_ge(*delta_act.at(u, "egc"))
                nc.vector.tensor_tensor(becol, bcol, egcol, ALU.mult).then_inc(*delta_dve("be"))
                v.wait_ge(*delta_act.at(u, "q_rs"))
                nc.vector.scalar_tensor_tensor(out=dl_q, in0=dl_q, scalar=float(P) ** -0.5, in1=rb[:, 0, :], op0=ALU.mult,
                                               op1=ALU.mult).then_inc(*delta_dve("q_n"))
                v.wait_ge(*delta_act.at(u, "k_rs"))
                nc.vector.tensor_tensor(dl_k, dl_k, rb[:, 1, :], ALU.mult).then_inc(*delta_dve("k_n"))
                own("q_n")
                v.wait_ge(*delta_act.at(u, "eg"))
                nc.vector.tensor_tensor(dl_qd, dl_q, dl_eg, ALU.mult).then_inc(*delta_dve("q_dec"))
                v.wait_ge(*delta_pe.at(u, "kk"))
                own("dt_mask")
                nc.vector.tensor_tensor(dl_at, ps[4][:, :], dl_dt, ALU.mult).then_inc(*delta_dve("at0"))
                own("at0")
                nc.vector.tensor_tensor(dl_at, ps[3][:, :], dl_at, ALU.mult).then_inc(*delta_dve("at"))
                v.wait_ge(*delta_pe.at(u, "qk"))
                nc.vector.tensor_tensor(dl_pt, ps[5][:, :], dl_dt, ALU.mult).then_inc(*delta_dve("pt"))
                own("at")
                nc.vector.tensor_tensor(blocks(dl_y), blocks(dl_at), over_blocks(level[:, 0, :]), ALU.mult
                                        ).then_inc(*delta_dve("y_m"))
                own("y_m")
                nc.vector.tensor_tensor(blocks(dl_y), over_blocks(ident[:, :]), blocks(dl_y), ALU.subtract
                                        ).then_inc(*delta_dve("y"))
                v.wait_ge(*delta_pe.at(u, "a_turn"))
                nc.vector.tensor_tensor(blocks(dl_x), blocks(ps[6][:, :]), over_blocks(level0_low[:, :]), ALU.mult
                                        ).then_inc(*delta_dve("x_m"))
                own("x_m")
                nc.vector.tensor_tensor(blocks(dl_x), over_blocks(ident[:, :]), blocks(dl_x), ALU.subtract
                                        ).then_inc(*delta_dve("x"))
                for l in range(1, LEVELS):
                    if l > 1:
                        v.wait_ge(*delta_pe.at(u, f"p{l - 1}"))
                    nc.vector.tensor_tensor(blocks(dl_am), blocks(dl_at), over_blocks(level[:, l, :]), ALU.mult
                                            ).then_inc(*delta_dve(f"am{l}"))
                    if l < 6:
                        v.wait_ge(*delta_pe.at(u, f"x{l}"))
                        own("x" if l == 1 else f"xm{l - 1}")
                        nc.vector.tensor_tensor(dl_x, dl_x, ps[4][:, :], ALU.subtract).then_inc(*delta_dve(f"xm{l}"))
                    v.wait_ge(*delta_pe.at(u, f"y{l}"))
                    own("y" if l == 1 else f"ym{l - 1}")
                    nc.vector.tensor_tensor(dl_y, dl_y, ps[5][:, :], ALU.subtract).then_inc(*delta_dve(f"ym{l}"))
                v.wait_ge(*delta_act.at(u, "u"))
                nc.vector.tensor_copy(dl_vn[:, 0:P], dl_u[:, 0:P]).then_inc(*delta_dve("vn0"))
                for b in range(3):
                    s, last_token = slice(b * P, (b + 1) * P), (b + 1) * P - 1
                    v.wait_ge(*delta_pe.at(u, f"ds{b}"))
                    if b == 0:
                        nc.vector.tensor_copy(dl_s, ps[5][:, s]).then_inc(*delta_dve("s0"))
                    else:
                        v.wait_ge(*delta_pe.at(u, f"o{b}"))
                        nc.vector.scalar_tensor_tensor(out=dl_s, in0=dl_s, scalar=dl_eg[:, last_token:last_token + 1],
                                                       in1=ps[5][:, s], op0=ALU.mult, op1=ALU.add
                                                       ).then_inc(*delta_dve(f"s{b}"))
                    s = slice((b + 1) * P, (b + 2) * P)
                    v.wait_ge(*delta_pe.at(u, f"ws{b + 1}"))
                    nc.vector.tensor_tensor(dl_vn[:, s], dl_u[:, s], ps[4][:, s], ALU.subtract
                                            ).then_inc(*delta_dve(f"vn{b + 1}"))
                v.wait_ge(*delta_act.at(u, "o_rs"))
                g = vt[:, col["gdn_out_gain"]:col["gdn_out_gain"] + 1]
                nc.vector.scalar_tensor_tensor(out=tt[:, 0, :], in0=dl_o, scalar=g, in1=rb[:, 0, :], op0=ALU.mult,
                                               op1=ALU.mult).then_inc(*delta_dve("o_t"))
                own("o_t")
                nc.vector.tensor_tensor(tt[:, 0, :], tt[:, 0, :], dl_z, ALU.mult).then_inc(*delta_dve("o_g"))
                v.wait_ge(*delta_act.at(u, "o_hi"))
                nc.vector.tensor_tensor(m_lo[:, 4 + u, :], tt[:, 0, :], m_hi[:, 4 + u, :].bitcast(F32),
                                        ALU.subtract).then_inc(*delta_dve("o_lo"))

        FRONT_PE = ["q_sum", "k_sum", "v_turn"]
        FRONT_ACT = ["q_sq", "k_sq", "q_ln", "q_rs", "k_ln", "k_rs", "v_nat"]
        FRONT_DVE = ["q_n", "k_n"]

        def front_tensor(pe, p, pe_steps, act_steps, u, chunk, bufs):
            if p < 6:
                dense(pe, *chunk(p // 2), x_hi, x_lo, ks=range(4 * (p % 2), 4 * (p % 2) + 4))
            if p == 3:
                pe.wait_ge(*act_steps.at(u, "q_sq"))
                nc.tensor.matmul(ps[2][:, :], ones64[:, :], sq[:, 0, :], start=True, stop=True).then_inc(*pe_steps("q_sum"))
            if p == 5:
                pe.wait_ge(*act_steps.at(u, "q_ln"))
                nc.tensor.matmul(ps[2][:, :], ones64[:, :], sq[:, 1, :], start=True, stop=True).then_inc(*pe_steps("k_sum"))
            if p == 7:
                pe.wait_ge(*act_steps.at(u, "k_ln"))
                pe.wait_ge(*freed(*chunk(2)))
                for b in range(NT):
                    last = nc.tensor.transpose(ps[2][:, b * P:(b + 1) * P], bufs[2][:, b * P:(b + 1) * P], ident[:, :])
                last.then_inc(*pe_steps("v_turn"))

        def front_scalar(act, p, pe_steps, act_steps, u, chunk, bufs):
            if p < 3:
                x, (q, j) = "qkv"[p], chunk(p)
                act.wait_ge(*done(q, j))
                nc.scalar.activation(bufs[p], ps[j % 2][:, :], ACT.Copy).then_inc(bank_free[j % 2], 1)
                if x != "v":
                    act.wait_ge(*freed(q, j))
                    nc.scalar.activation(sq[:, p, :], bufs[p], ACT.Square).then_inc(*act_steps(f"{x}_sq"))
            if p in (1, 2):
                x = "qk"[p - 1]
                act.wait_ge(*pe_steps.at(u, f"{x}_sum"))
                rsqrt(act, act_steps, u, x, ps[2][:, :], rb[:, p - 1, :], tt[:, p, :], 1.0 / 64)
            if p == 3:
                act.wait_ge(*pe_steps.at(u, "v_turn"))
                nc.scalar.activation(bufs[3], ps[2][:, :], ACT.Copy).then_inc(*act_steps("v_nat"))

        def front_vector(v, act_steps, dve_steps, u, bufs, q_gain, k_gain):
            for c, (x, gain) in enumerate((("q", q_gain), ("k", k_gain))):
                v.wait_ge(*act_steps.at(u, f"{x}_rs"))
                nc.vector.scalar_tensor_tensor(out=bufs[c], in0=bufs[c], scalar=gain, in1=rb[:, c, :], op0=ALU.mult,
                                               op1=ALU.mult).then_inc(*dve_steps(f"{x}_n"))

        arena_at[0] = 0
        at_bufs = [[take([T]) for _ in range(4)] for _ in range(2)]
        at_bias, at_lg, at_pr = take([T]), take([2, 2, T]), take([2, 2, T])
        at_p0, at_diff, at_turned, at_o = take([T]), take([T]), take([T]), take([T])
        at_sq, at_rb, at_ln = take([T]), take([T]), take([T])
        at_small = take([64])

        def at_col(b, what, r, n=1):
            c = 16 * b + 2 * what + r
            return at_small[:, c:c + n]

        NEG_MAX, SUM, INV, MAX, LAM_INV = range(5)
        attn_front_pe = Steps(sem("attn_front_pe"), FRONT_PE)
        attn_front_act = Steps(sem("attn_front_act"), FRONT_ACT)
        attn_front_dve = Steps(sem("attn_front_dve"), FRONT_DVE)
        attn_pe = Steps(sem("attn_pe"), ["lg0_0", "lg0_1"]
                        + sum(([f"lg{b + 1}_0", f"lg{b + 1}_1"] * (b < 3) + [f"turn{b}", f"pv{b}"] for b in range(NT)), [])
                        + ["o_sum"])
        attn_act = Steps(sem("attn_act"), ["e0_0", "e0_1"]
                         + sum(([f"e{b + 1}_0", f"e{b + 1}_1"] * (b < 3) + [f"turned{b}"] for b in range(NT)), [])
                         + ["o_raw", "o_sq", "o_ln", "o_rs", "o_hi"])

        def lg_steps(b):
            return [f"lg{b}_0", f"nm{b}_0", f"lg{b}_1", f"nm{b}_1"]
        attn_dve = Steps(sem("attn_dve"), lg_steps(0)
                         + sum((lg_steps(b + 1) * (b < 3) + [f"inv{b}", f"lam{b}", f"p0_{b}", f"diff{b}"]
                                for b in range(NT)), []) + ["bias", "o_t", "o_lo"])
        bias_made = sem("bias_made")

        def attn_chunk(i, hh):
            def chunk(c):
                n = 3 * hh + c
                return quads["attn"] + 3 * i + n // 4, n % 4
            return chunk

        def attn_tensor(pe):
            with pe.Fori(0, 2) as i:
                for hh in range(4):
                    u = 4 * i + hh
                    at_q, at_k, _, at_nat = at_bufs[hh % 2]

                    def front(of, p):
                        if of < 4:
                            front_tensor(pe, p, attn_front_pe, attn_front_act, 4 * i + of, attn_chunk(i, of),
                                         at_bufs[of % 2])
                    if hh == 0:
                        for p in range(8):
                            front(0, p)

                    def logits(b):
                        for r in range(2):
                            half = slice(64 * r, 64 * r + 64)
                            if b == 0 and r == 0:
                                pe.wait_ge(*attn_front_dve.at(u, "k_n"))
                                pe.wait_ge(*attn_front_act.at(u, "v_nat"))
                            if b:
                                pe.wait_ge(*attn_dve.at(u, f"lg{b - 1}_{r}"))
                            nc.tensor.matmul(ps[5 + r][:, 0:(b + 1) * P], at_q[half, b * P:(b + 1) * P],
                                             at_k[half, 0:(b + 1) * P], start=True, stop=True
                                             ).then_inc(*attn_pe(f"lg{b}_{r}"))
                    logits(0)
                    for b in range(NT):
                        if b < 3:
                            logits(b + 1)
                        front(hh + 1, 2 * b)
                        pe.wait_ge(*attn_dve.at(u, f"diff{b}"))
                        if b:
                            pe.wait_ge(*attn_act.at(u, f"turned{b - 1}"))
                        for kb in range(b + 1):
                            s = slice(kb * P, (kb + 1) * P)
                            last = nc.tensor.transpose(ps[7][:, s], at_diff[:, s], ident[:, :])
                        last.then_inc(*attn_pe(f"turn{b}"))
                        front(hh + 1, 2 * b + 1)
                        pe.wait_ge(*attn_act.at(u, f"turned{b}"))
                        for kb in range(b + 1):
                            s = slice(kb * P, (kb + 1) * P)
                            last = nc.tensor.matmul(ps[3][:, b * P:(b + 1) * P], at_nat[:, s], at_turned[:, s],
                                                    start=(kb == 0), stop=(kb == b))
                        last.then_inc(*attn_pe(f"pv{b}"))
                    pe.wait_ge(*attn_act.at(u, "o_sq"))
                    nc.tensor.matmul(ps[7][:, :], ones[:, :], at_sq, start=True, stop=True
                                     ).then_inc(*attn_pe("o_sum"))

        def attn_scalar(act):
            with act.Fori(0, 2) as i:
                for hh in range(4):
                    u = 4 * i + hh

                    def front(of, p):
                        if of < 4:
                            front_scalar(act, p, attn_front_pe, attn_front_act, 4 * i + of, attn_chunk(i, of),
                                         at_bufs[of % 2])
                    if hh == 0:
                        for p in range(4):
                            front(0, p)

                    def exps(b):
                        for r in range(2):
                            act.wait_ge(*attn_dve.at(u, f"nm{b}_{r}"))
                            if b >= 2:
                                act.wait_ge(*attn_dve.at(u, f"diff{b - 2}"))
                            n = (b + 1) * P
                            nc.scalar.activation(at_pr[:, b % 2, r, 0:n], at_lg[:, b % 2, r, 0:n], ACT.Exp,
                                                 bias=at_col(b, NEG_MAX, r), accum_out=at_col(b, SUM, r)
                                                 ).then_inc(*attn_act(f"e{b}_{r}"))
                    exps(0)
                    for b in range(NT):
                        if b < 3:
                            exps(b + 1)
                        n = (b + 1) * P
                        act.wait_ge(*attn_pe.at(u, f"turn{b}"))
                        if b:
                            act.wait_ge(*attn_pe.at(u, f"pv{b - 1}"))
                        nc.scalar.activation(at_turned[:, 0:n], ps[7][:, 0:n], ACT.Copy).then_inc(*attn_act(f"turned{b}"))
                        front(hh + 1, b)
                    act.wait_ge(*attn_pe.at(u, "pv3"))
                    nc.scalar.activation(at_o, ps[3][:, :], ACT.Copy).then_inc(*attn_act("o_raw"))
                    act.wait_ge(*attn_act.at(u, "o_raw"))
                    nc.scalar.activation(at_sq, at_o, ACT.Square).then_inc(*attn_act("o_sq"))
                    act.wait_ge(*attn_pe.at(u, "o_sum"))
                    rsqrt(act, attn_act, u, "o", ps[7][:, :], at_rb, at_ln, 1.0 / P)
                    act.wait_ge(*attn_dve.at(u, "o_t"))
                    nc.scalar.activation(m_hi[:, u, :], tt[:, 0, :], ACT.Copy).then_inc(*attn_act("o_hi"))

        def attn_vector(v):
            for c in range(NT):
                last = nc.vector.tensor_scalar(at_bias[:, c * P:(c + 1) * P], idx[:, :], -1.0, float(384 - c * P),
                                               ALU.mult, ALU.add)
            last.then_inc(bias_made, 1)
            v.wait_ge(bias_made, 1)
            nc.vector.tensor_scalar(at_o, at_bias, 0.0, BIG, ALU.is_lt, ALU.mult).then_inc(bias_made, 1)
            v.wait_ge(bias_made, 2)
            nc.vector.tensor_tensor(at_bias, at_bias, at_o, ALU.add).then_inc(bias_made, 1)
            v.wait_ge(bias_made, 3)
            nc.vector.tensor_scalar(at_bias, at_bias, -0.5, None, ALU.mult).then_inc(bias_made, 1)
            v.wait_ge(bias_made, 4)
            with v.Fori(0, 2) as i:
                for hh in range(4):
                    u = 4 * i + hh

                    def front(of):
                        if of < 4:
                            front_vector(v, attn_front_act, attn_front_dve, 4 * i + of, at_bufs[of % 2], q_gain_o,
                                         vt[:, col["attn_k_gain"]:col["attn_k_gain"] + 1])
                    if hh == 0:
                        front(0)

                    def logits(b):
                        n = (b + 1) * P
                        for r in range(2):
                            v.wait_ge(*attn_pe.at(u, f"lg{b}_{r}"))
                            if b >= 2:
                                v.wait_ge(*attn_act.at(u, f"e{b - 2}_{r}"))
                            nc.vector.tensor_tensor(at_lg[:, b % 2, r, 0:n], ps[5 + r][:, 0:n], at_bias[:, T - n:T],
                                                    ALU.add).then_inc(*attn_dve(f"lg{b}_{r}"))
                            v.wait_ge(*attn_dve.at(u, f"lg{b}_{r}"))
                            nc.vector.tensor_reduce(at_col(b, NEG_MAX, r), at_lg[:, b % 2, r, 0:n], AX_X, ALU.max,
                                                    negate=True).then_inc(*attn_dve(f"nm{b}_{r}"))
                    logits(0)
                    for b in range(NT):
                        if b < 3:
                            logits(b + 1)
                        n = (b + 1) * P
                        v.wait_ge(*attn_act.at(u, f"e{b}_1"))
                        nc.vector.reciprocal(at_col(b, INV, 0, 2), at_col(b, SUM, 0, 2)).then_inc(*attn_dve(f"inv{b}"))
                        v.wait_ge(*attn_dve.at(u, f"inv{b}"))
                        nc.vector.tensor_scalar(at_col(b, LAM_INV, 0), at_col(b, INV, 1), neg_lam, None, ALU.mult
                                                ).then_inc(*attn_dve(f"lam{b}"))
                        nc.vector.tensor_scalar(at_p0[:, 0:n], at_pr[:, b % 2, 0, 0:n], at_col(b, INV, 0), None, ALU.mult
                                                ).then_inc(*attn_dve(f"p0_{b}"))
                        v.wait_ge(*attn_dve.at(u, f"p0_{b}"))
                        if b:
                            v.wait_ge(*attn_pe.at(u, f"turn{b - 1}"))
                        nc.vector.scalar_tensor_tensor(out=at_diff[:, 0:n], in0=at_pr[:, b % 2, 1, 0:n],
                                                       scalar=at_col(b, LAM_INV, 0), in1=at_p0[:, 0:n], op0=ALU.mult,
                                                       op1=ALU.add).then_inc(*attn_dve(f"diff{b}"))
                    nc.vector.tensor_scalar(at_bias, at_bias, 0.5, None, ALU.mult).then_inc(*attn_dve("bias"))
                    front(hh + 1)
                    v.wait_ge(*attn_dve.at(u, "bias"))
                    v.wait_ge(*attn_act.at(u, "o_rs"))
                    nc.vector.scalar_tensor_tensor(out=tt[:, 0, :], in0=at_o, scalar=sub_gain, in1=at_rb,
                                                   op0=ALU.mult, op1=ALU.mult).then_inc(*attn_dve("o_t"))
                    v.wait_ge(*attn_act.at(u, "o_hi"))
                    nc.vector.tensor_tensor(m_lo[:, u, :], tt[:, 0, :], m_hi[:, u, :].bitcast(F32), ALU.subtract
                                            ).then_inc(*attn_dve("o_lo"))

        arena_at[0] = 0
        st_bufs = [[take([T]) for _ in range(4)] for _ in range(2)]
        st_abs, st_ln = take([2, T]), take([2, T])
        st_sp, st_lb, st_w = take([NT, T]), take([2, T]), take([NT, T])
        ITEMS = [(r, sb) for r in range(2) for sb in range(NT - 1, -1, -1)]

        def piped(first, second):
            return first(0) + sum(((first(n + 1) if n + 1 < len(ITEMS) else []) + second(n) for n in range(len(ITEMS))), [])

        stick_front_pe = Steps(sem("stick_front_pe"), FRONT_PE)
        stick_front_act = Steps(sem("stick_front_act"), FRONT_ACT)
        stick_front_dve = Steps(sem("stick_front_dve"), FRONT_DVE)
        stick_pe = Steps(sem("stick_pe"), piped(
            lambda n: [f"z{n}"], lambda n: [f"c{n}"] + [f"o{n // 4}"] * (n % 4 == 3)))
        stick_act = Steps(sem("stick_act"), piped(
            lambda n: [f"abs{n}", f"exp{n}", f"ln{n}"], lambda n: [f"w{n}"]) + ["o_hi"])
        stick_dve = Steps(sem("stick_dve"), piped(
            lambda n: [f"sp{n}", f"mask{n}", f"lb{n}"], lambda n: [f"lw{n}", f"wm{n}"]) + ["o_lo"])

        def stick_chunk(i, hh):
            def chunk(c):
                n = 3 * hh + c
                return quads["stick"] + 3 * i + n // 4, n % 4
            return chunk

        def stick_tensor(pe):
            with pe.Fori(0, 2) as i:
                for hh in range(4):
                    u = 4 * i + hh
                    st_q, st_k, _, st_nat = st_bufs[hh % 2]

                    def front(of, p):
                        if of < 4:
                            front_tensor(pe, p, stick_front_pe, stick_front_act, 4 * i + of, stick_chunk(i, of),
                                         st_bufs[of % 2])
                    if hh == 0:
                        for p in range(8):
                            front(0, p)

                    def scores(n):
                        r, sb = ITEMS[n]
                        half = slice(64 * r, 64 * r + 64)
                        if n == 0:
                            pe.wait_ge(*stick_front_dve.at(u, "k_n"))
                        if n >= 2:
                            pe.wait_ge(*stick_dve.at(u, f"lb{n - 2}"))
                        else:
                            pe.wait_ge(*stick_front_act.at(u, "v_nat"))
                        nc.tensor.matmul(ps[3 + n % 2][:, sb * P:T], st_k[half, sb * P:(sb + 1) * P],
                                         st_q[half, sb * P:T], start=True, stop=True).then_inc(*stick_pe(f"z{n}"))
                    scores(0)
                    for n, (r, sb) in enumerate(ITEMS):
                        if n + 1 < len(ITEMS):
                            scores(n + 1)
                        front(hh + 1, n)
                        pe.wait_ge(*stick_dve.at(u, f"mask{n}"))
                        if n >= 2:
                            pe.wait_ge(*stick_dve.at(u, f"lw{n - 2}"))
                        bank = ps[5 + n % 2]
                        last = nc.tensor.matmul(bank[:, sb * P:T], lower_s[:, :], st_sp[:, sb, sb * P:T], start=True,
                                                stop=(sb == NT - 1))
                        for jb in range(sb + 1, NT):
                            last = nc.tensor.matmul(bank[:, jb * P:T], ones[:, :], st_sp[:, jb, jb * P:T], start=False,
                                                    stop=(jb == NT - 1))
                        last.then_inc(*stick_pe(f"c{n}"))
                        if sb == 0:
                            pe.wait_ge(*stick_dve.at(u, f"wm{n}"))
                            for kb in range(NT):
                                last = nc.tensor.matmul(ps[7][64 * r:64 * r + 64, kb * P:T],
                                                        st_nat[:, kb * P + 64 * r:kb * P + 64 * r + 64],
                                                        st_w[:, kb, kb * P:T], start=(kb == 0), stop=(kb == NT - 1))
                            last.then_inc(*stick_pe(f"o{r}"))

        def stick_scalar(act):
            with act.Fori(0, 2) as i:
                for hh in range(4):
                    u = 4 * i + hh

                    def front(of, p):
                        if of < 4:
                            front_scalar(act, p, stick_front_pe, stick_front_act, 4 * i + of, stick_chunk(i, of),
                                         st_bufs[of % 2])
                    if hh == 0:
                        for p in range(4):
                            front(0, p)

                    def first(n):
                        r, sb = ITEMS[n]
                        t = slice(sb * P, T)
                        act.wait_ge(*stick_pe.at(u, f"z{n}"))
                        nc.scalar.activation(st_abs[:, n % 2, t], ps[3 + n % 2][:, t], ACT.Abs).then_inc(*stick_act(f"abs{n}"))
                        act.wait_ge(*stick_act.at(u, f"abs{n}"))
                        nc.scalar.activation(st_abs[:, n % 2, t], st_abs[:, n % 2, t], ACT.Exp, scale=-1.0
                                             ).then_inc(*stick_act(f"exp{n}"))
                        act.wait_ge(*stick_act.at(u, f"exp{n}"))
                        if n >= 2:
                            act.wait_ge(*stick_dve.at(u, f"lb{n - 2}"))
                        nc.scalar.activation(st_ln[:, n % 2, t], st_abs[:, n % 2, t], ACT.Ln, bias=1.0
                                             ).then_inc(*stick_act(f"ln{n}"))
                    first(0)
                    for n, (r, sb) in enumerate(ITEMS):
                        if n + 1 < len(ITEMS):
                            first(n + 1)
                        if n in (2, 4, 6):
                            front(hh + 1, n // 2 - 1)
                        act.wait_ge(*stick_dve.at(u, f"lw{n}"))
                        if n == 4:
                            act.wait_ge(*stick_pe.at(u, "o0"))
                        t = slice(sb * P, T)
                        nc.scalar.activation(st_w[:, sb, t], st_lb[:, n % 2, t], ACT.Exp).then_inc(*stick_act(f"w{n}"))
                    front(hh + 1, 3)
                    act.wait_ge(*stick_pe.at(u, "o1"))
                    nc.scalar.activation(m_hi[:, u, :], ps[7][:, :], ACT.Copy).then_inc(*stick_act("o_hi"))

        def stick_vector(v):
            with v.Fori(0, 2) as i:
                for hh in range(4):
                    u = 4 * i + hh

                    def front(of):
                        if of < 4:
                            front_vector(v, stick_front_act, stick_front_dve, 4 * i + of, st_bufs[of % 2], q_gain_s,
                                         vt[:, col["k_norm_2"]:col["k_norm_2"] + 1])
                    if hh == 0:
                        front(0)

                    def first(n):
                        r, sb = ITEMS[n]
                        t, diag = slice(sb * P, T), slice(sb * P, (sb + 1) * P)
                        v.wait_ge(*stick_act.at(u, f"ln{n}"))
                        if n >= 4:
                            v.wait_ge(*stick_pe.at(u, "c3"))
                        nc.vector.scalar_tensor_tensor(out=st_sp[:, sb, t], in0=ps[3 + n % 2][:, t], scalar=0.0,
                                                       in1=st_ln[:, n % 2, t], op0=ALU.max, op1=ALU.add
                                                       ).then_inc(*stick_dve(f"sp{n}"))
                        v.wait_ge(*stick_dve.at(u, f"sp{n}"))
                        nc.vector.tensor_tensor(st_sp[:, sb, diag], st_sp[:, sb, diag], upper_s[:, :], ALU.mult
                                                ).then_inc(*stick_dve(f"mask{n}"))
                        if n >= 2:
                            v.wait_ge(*stick_act.at(u, f"w{n - 2}"))
                        nc.vector.scalar_tensor_tensor(out=st_lb[:, n % 2, t], in0=ps[3 + n % 2][:, t], scalar=0.0,
                                                       in1=st_ln[:, n % 2, t], op0=ALU.min, op1=ALU.subtract
                                                       ).then_inc(*stick_dve(f"lb{n}"))
                    first(0)
                    for n, (r, sb) in enumerate(ITEMS):
                        if n + 1 < len(ITEMS):
                            first(n + 1)
                        t, diag = slice(sb * P, T), slice(sb * P, (sb + 1) * P)
                        v.wait_ge(*stick_pe.at(u, f"c{n}"))
                        v.wait_ge(*stick_dve.at(u, f"lb{n}"))
                        nc.vector.tensor_tensor(st_lb[:, n % 2, t], st_lb[:, n % 2, t], ps[5 + n % 2][:, t], ALU.subtract
                                                ).then_inc(*stick_dve(f"lw{n}"))
                        v.wait_ge(*stick_act.at(u, f"w{n}"))
                        nc.vector.tensor_tensor(st_w[:, sb, diag], st_w[:, sb, diag], upper_s[:, :], ALU.mult
                                                ).then_inc(*stick_dve(f"wm{n}"))
                    front(hh + 1)
                    v.wait_ge(*stick_act.at(u, "o_hi"))
                    nc.vector.tensor_tensor(m_lo[:, u, :], ps[7][:, :], m_hi[:, u, :].bitcast(F32), ALU.subtract
                                            ).then_inc(*stick_dve("o_lo"))

        arena_at[0] = 0
        cv_b, cv_c, cv_u, cv_y = take([T]), take([T]), take([T]), take([T])
        conv_act = Steps(sem("conv_act"), ["hi"])
        conv_dve = Steps(sem("conv_dve"), ["y0", "y1", "y2", "t", "lo"])

        def conv_chunk(n, c):
            g = 3 * n + c
            return quads["conv"] + g // 4, g % 4

        def conv_tensor(pe):
            for n in range(4):
                for c in range(3):
                    dense(pe, *conv_chunk(n, c), x_hi, x_lo)

        def conv_scalar(act):
            for n in range(4):
                if n:
                    act.wait_ge(*conv_dve.at(n - 1, "t"))
                for c, buf in enumerate((cv_b, cv_c)):
                    q, j = conv_chunk(n, c)
                    act.wait_ge(*done(q, j))
                    nc.scalar.activation(buf, ps[j % 2][:, :], ACT.Copy).then_inc(bank_free[j % 2], 1)
                act.wait_ge(*conv_dve.at(n, "t"))
                nc.scalar.activation(m_hi[:, n, :], tt[:, 0, :], ACT.Copy).then_inc(*conv_act("hi"))

        def conv_vector(v):
            for n in range(4):
                q, j = conv_chunk(n, 2)
                v.wait_ge(*done(q, j))
                v.wait_ge(*freed(*conv_chunk(n, 1)))
                nc.vector.tensor_tensor(cv_u, ps[j % 2][:, :], cv_c, ALU.mult).then_inc(bank_free[j % 2], 1)
                v.wait_ge(*freed(q, j))
                taps = [vt[:, col["conv_w_2"] + 4 * t + n:col["conv_w_2"] + 4 * t + n + 1] for t in range(3)]
                nc.vector.tensor_scalar(cv_y, cv_u, taps[2], None, ALU.mult).then_inc(*conv_dve("y0"))
                for s in (1, 2):
                    v.wait_ge(*conv_dve.at(n, f"y{s - 1}"))
                    nc.vector.scalar_tensor_tensor(out=cv_y[:, s:T], in0=cv_u[:, 0:T - s], scalar=taps[2 - s],
                                                   in1=cv_y[:, s:T], op0=ALU.mult, op1=ALU.add
                                                   ).then_inc(*conv_dve(f"y{s}"))
                v.wait_ge(*conv_dve.at(n, "y2"))
                v.wait_ge(*freed(*conv_chunk(n, 0)))
                nc.vector.tensor_tensor(tt[:, 0, :], cv_y, cv_b, ALU.mult).then_inc(*conv_dve("t"))
                v.wait_ge(*conv_act.at(n, "hi"))
                nc.vector.tensor_tensor(m_lo[:, n, :], tt[:, 0, :], m_hi[:, n, :].bitcast(F32), ALU.subtract
                                        ).then_inc(*conv_dve("lo"))

        arena_at[0] = 0
        hg_q, hg_f, hg_v, hg_g, hg_b = take([T]), take([T]), take([T]), take([T]), take([T])
        hg_reset, hg_e, hg_qe, hg_ke = take([T]), take([2, T]), take([2, T]), take([2, T])
        hg_sc, hg_eb, hg_qd, hg_kd, hg_kn, hg_vn = (take([T]) for _ in range(6))
        hg_lf, hg_s, hg_o, hg_cols = take([T]), take([P]), take([T]), take([8])
        hg_gain, hg_lb, hg_oml = hg_cols[:, 0:1], hg_cols[:, 1:2], hg_cols[:, 2:3]
        hg_reset_done = sem("hg_reset_done")

        def lv_piped(first, second):
            return first(0) + sum(((first(l + 1) if l + 1 < LEVELS else []) + second(l) for l in range(LEVELS)), [])

        hgrn_pe = Steps(sem("hgrn_pe"), ["diag"] + [f"lv{l}" for l in range(LEVELS)] + ["k_turn", "v_turn", "ds"]
                        + [f"o{b}" for b in range(NT)] + ["o_sum"])
        hgrn_act = Steps(sem("hgrn_act"), ["ln"] + [x for l in range(LEVELS) for x in (f"abs{l}", f"e{l}")]
                         + ["eb", "kd", "kn", "vn", "o_raw", "o_sq", "o_ln", "o_rs", "o_hi"])
        hgrn_dve = Steps(sem("hgrn_dve"), ["gain", "lb", "oml", "f", "k", "b", "diag"]
                         + lv_piped(lambda l: [f"d{l}"], lambda l: [f"qe{l}", f"ke{l}"] + [f"sc{l - 1}"] * (l > 0))
                         + ["kd_arg", "sc6", "qd", "kd", "s0", "s1", "s2", "o_t", "o_g", "o_lo"])

        def hgrn_tensor(pe):
            with pe.Fori(0, 4) as u:
                q = quads["hgrn"] + u
                for j in range(4):
                    dense(pe, q, j, x_hi, x_lo)

                def each(bank, lhs, rhs, step, turn=False):
                    for b in range(NT):
                        s = slice(b * P, (b + 1) * P)
                        if turn:
                            last = nc.tensor.transpose(ps[bank][:, s], lhs[:, s], ident[:, :])
                        else:
                            last = nc.tensor.matmul(ps[bank][:, s], lhs[:, s], rhs[:, s], start=True, stop=True)
                    last.then_inc(*hgrn_pe(step))

                pe.wait_ge(*hgrn_dve.at(u, "k"))
                each(2, hg_lf, hg_q, "diag")
                for l in range(LEVELS):
                    pe.wait_ge(*hgrn_dve.at(u, f"ke{l}"))
                    if l >= 2:
                        pe.wait_ge(*hgrn_dve.at(u, f"sc{l - 2}"))
                    each(3 + l % 2, hg_ke[:, l % 2], hg_qe[:, l % 2], f"lv{l}")
                pe.wait_ge(*hgrn_dve.at(u, "kd"))
                each(5, hg_kd, None, "k_turn", True)
                each(6, hg_v, None, "v_turn", True)
                pe.wait_ge(*hgrn_act.at(u, "vn"))
                for b in range(3):
                    s = slice(b * P, (b + 1) * P)
                    last = nc.tensor.matmul(ps[7][:, s], hg_kn[:, s], hg_vn[:, s], start=True, stop=True)
                last.then_inc(*hgrn_pe("ds"))
                for b in range(NT):
                    s = slice(b * P, (b + 1) * P)
                    if b:
                        pe.wait_ge(*hgrn_dve.at(u, f"s{b - 1}"))
                        nc.tensor.matmul(ps[2][:, s], hg_s, hg_qd[:, s], start=True, stop=False)
                    nc.tensor.matmul(ps[2][:, s], hg_vn[:, s], hg_sc[:, s], start=(b == 0), stop=True
                                     ).then_inc(*hgrn_pe(f"o{b}"))
                pe.wait_ge(*hgrn_act.at(u, "o_sq"))
                nc.tensor.matmul(ps[3][:, :], ones[:, :], sq[:, 0, :], start=True, stop=True).then_inc(*hgrn_pe("o_sum"))

        def hgrn_scalar(act):
            with act.Fori(0, 4) as u:
                q = quads["hgrn"] + u
                for j, (buf, func) in enumerate(((hg_q, ACT.Copy), (hg_f, ACT.Sigmoid), (hg_v, ACT.Copy), (hg_g, ACT.Silu))):
                    act.wait_ge(*done(q, j))
                    nc.scalar.activation(buf, ps[j % 2][:, :], func).then_inc(bank_free[j % 2], 1)
                exp_and_ln()
                act.wait_ge(*hgrn_dve.at(u, "k"))
                nc.scalar.activation(hg_f, hg_f, ACT.Ln).then_inc(*hgrn_act("ln"))
                for l in range(LEVELS):
                    act.wait_ge(*hgrn_dve.at(u, f"d{l}"))
                    e = hg_e[:, l % 2]
                    nc.scalar.activation(e, e, ACT.Abs).then_inc(*hgrn_act(f"abs{l}"))
                    act.wait_ge(*hgrn_act.at(u, f"abs{l}"))
                    nc.scalar.activation(e, e, ACT.Exp, scale=-1.0).then_inc(*hgrn_act(f"e{l}"))
                nc.scalar.activation(hg_eb, hg_b, ACT.Exp).then_inc(*hgrn_act("eb"))
                act.wait_ge(*hgrn_dve.at(u, "kd_arg"))
                nc.scalar.activation(hg_kd, hg_kd, ACT.Exp).then_inc(*hgrn_act("kd"))
                act.wait_ge(*hgrn_pe.at(u, "k_turn"))
                nc.scalar.activation(hg_kn, ps[5][:, :], ACT.Copy).then_inc(*hgrn_act("kn"))
                act.wait_ge(*hgrn_pe.at(u, "v_turn"))
                nc.scalar.activation(hg_vn, ps[6][:, :], ACT.Copy).then_inc(*hgrn_act("vn"))
                act.wait_ge(*hgrn_pe.at(u, "o3"))
                nc.scalar.activation(hg_o, ps[2][:, :], ACT.Copy).then_inc(*hgrn_act("o_raw"))
                act.wait_ge(*hgrn_act.at(u, "o_raw"))
                nc.scalar.activation(sq[:, 0, :], hg_o, ACT.Square).then_inc(*hgrn_act("o_sq"))
                act.wait_ge(*hgrn_pe.at(u, "o_sum"))
                rsqrt(act, hgrn_act, u, "o", ps[3][:, :], rb[:, 0, :], tt[:, 1, :], 1.0 / P)
                act.wait_ge(*hgrn_dve.at(u, "o_g"))
                nc.scalar.activation(m_hi[:, 4 + u, :], tt[:, 0, :], ACT.Copy).then_inc(*hgrn_act("o_hi"))

        def hgrn_vector(v):
            nc.vector.memset(hg_reset, 1.0).then_inc(hg_reset_done, 1)
            v.wait_ge(hg_reset_done, 1)
            nc.vector.memset(blocks(hg_reset)[:, :, 0:1], 0.0).then_inc(hg_reset_done, 1)
            v.wait_ge(hg_reset_done, 2)
            with v.Fori(0, 4) as u:
                q = quads["hgrn"] + u

                def own(name):
                    v.wait_ge(*hgrn_dve.at(u, name))

                c = col["hg_norm_2"]
                nc.vector.tensor_copy(hg_gain, vt[:, c:c + 4][:, bass.ds(u, 1)]).then_inc(*hgrn_dve("gain"))
                nc.vector.tensor_copy(hg_lb, lb[:, bass.ds(u, 1)]).then_inc(*hgrn_dve("lb"))
                nc.vector.tensor_copy(hg_oml, one_minus_lb[:, bass.ds(u, 1)]).then_inc(*hgrn_dve("oml"))
                own("oml")
                v.wait_ge(*freed(q, 3))
                nc.vector.tensor_scalar(hg_f, hg_f, hg_oml, hg_lb, ALU.mult, ALU.add).then_inc(*hgrn_dve("f"))
                own("f")
                nc.vector.tensor_scalar(hg_lf, hg_f, -1.0, 1.0, ALU.mult, ALU.add).then_inc(*hgrn_dve("k"))
                hg_k = hg_lf
                v.wait_ge(*hgrn_act.at(u, "ln"))
                nc.vector.tensor_tensor_scan(hg_b, hg_reset, hg_f, 0.0, ALU.mult, ALU.add).then_inc(*hgrn_dve("b"))
                v.wait_ge(*hgrn_pe.at(u, "diag"))
                nc.vector.tensor_tensor(blocks(hg_sc), blocks(ps[2][:, :]), over_blocks(ident[:, :]), ALU.mult
                                        ).then_inc(*hgrn_dve("diag"))

                def to_boundary(l):
                    n = 2 ** (l + 1)
                    b = hg_b.rearrange("p (m n) -> p m n", n=n)
                    nc.vector.tensor_tensor(hg_e[:, l % 2].rearrange("p (m n) -> p m n", n=n), b,
                                            b[:, :, n // 2 - 1:n // 2].to_broadcast([P, T // n, n]), ALU.subtract
                                            ).then_inc(*hgrn_dve(f"d{l}"))

                def level_ready(l):
                    v.wait_ge(*hgrn_pe.at(u, f"lv{l}"))
                    own("diag" if l == 0 else f"sc{l - 1}")

                def take_level(l):
                    nc.vector.copy_predicated(blocks(hg_sc), over_blocks(level[:, l, :]).bitcast(U32),
                                              blocks(ps[3 + l % 2][:, :])).then_inc(*hgrn_dve(f"sc{l}"))
                own("b")
                to_boundary(0)
                for l in range(LEVELS):
                    if l + 1 < LEVELS:
                        if l >= 1:
                            own(f"ke{l - 1}")
                        to_boundary(l + 1)
                    v.wait_ge(*hgrn_act.at(u, f"e{l}"))
                    if l >= 2:
                        v.wait_ge(*hgrn_pe.at(u, f"lv{l - 2}"))
                    nc.vector.tensor_tensor(hg_qe[:, l % 2], hg_q, hg_e[:, l % 2], ALU.mult).then_inc(*hgrn_dve(f"qe{l}"))
                    if l:
                        level_ready(l - 1)
                    nc.vector.tensor_tensor(hg_ke[:, l % 2], hg_k, hg_e[:, l % 2], ALU.mult).then_inc(*hgrn_dve(f"ke{l}"))
                    if l:
                        take_level(l - 1)
                level_ready(6)
                nc.vector.tensor_tensor(blocks(hg_kd), blocks(hg_b)[:, :, P - 1:P].to_broadcast([P, NT, P]), blocks(hg_b),
                                        ALU.subtract).then_inc(*hgrn_dve("kd_arg"))
                take_level(6)
                v.wait_ge(*hgrn_act.at(u, "eb"))
                nc.vector.tensor_tensor(hg_qd, hg_q, hg_eb, ALU.mult).then_inc(*hgrn_dve("qd"))
                v.wait_ge(*hgrn_act.at(u, "kd"))
                nc.vector.tensor_tensor(hg_kd, hg_kd, hg_k, ALU.mult).then_inc(*hgrn_dve("kd"))
                v.wait_ge(*hgrn_pe.at(u, "ds"))
                nc.vector.tensor_copy(hg_s, ps[7][:, 0:P]).then_inc(*hgrn_dve("s0"))
                for b in (1, 2):
                    s, last_token = slice(b * P, (b + 1) * P), (b + 1) * P - 1
                    own(f"s{b - 1}")
                    v.wait_ge(*hgrn_pe.at(u, f"o{b}"))
                    nc.vector.scalar_tensor_tensor(out=hg_s, in0=hg_s, scalar=hg_eb[:, last_token:last_token + 1],
                                                   in1=ps[7][:, s], op0=ALU.mult, op1=ALU.add).then_inc(*hgrn_dve(f"s{b}"))
                v.wait_ge(*hgrn_act.at(u, "o_rs"))
                nc.vector.scalar_tensor_tensor(out=tt[:, 0, :], in0=hg_o, scalar=hg_gain, in1=rb[:, 0, :], op0=ALU.mult,
                                               op1=ALU.mult).then_inc(*hgrn_dve("o_t"))
                own("o_t")
                nc.vector.tensor_tensor(tt[:, 0, :], tt[:, 0, :], hg_g, ALU.mult).then_inc(*hgrn_dve("o_g"))
                v.wait_ge(*hgrn_act.at(u, "o_hi"))
                nc.vector.tensor_tensor(m_lo[:, 4 + u, :], tt[:, 0, :], m_hi[:, 4 + u, :].bitcast(F32), ALU.subtract
                                        ).then_inc(*hgrn_dve("o_lo"))

        def norm(i):
            return (lambda e: norm_tensor(e, i), lambda e: norm_scalar(e, i), lambda e: norm_vector(e, i))

        def project(name, layer2=None):
            return (lambda e: project_tensor(e, name), None, lambda e: project_vector(e, name, layer2))

        def mlp(i, layer2=None):
            return (lambda e: mlp_tensor(e, i), lambda e: mlp_scalar(e, i), lambda e: mlp_vector(e, i, layer2))

        def ple(i):
            return (lambda e: ple_tensor(e, i), lambda e: (ple_loads(e, i), ple_scalar(e, i)), lambda e: ple_vector(e, i))

        plan = [(setup_tensor, setup_scalar, setup_vector)]
        if has("gmlp"):
            plan += [norm(0), (gmlp_tensor, gmlp_scalar, gmlp_vector)]
        if has("delta"):
            plan += [(gates_tensor, gates_scalar, gates_vector), (delta_tensor, delta_scalar, delta_vector)]
        if has("out_e"):
            plan += [project("out_e")]
        if has("mlp0"):
            plan += [norm(1), mlp(0)]
        if has("ple0"):
            plan += [norm(2), ple(0)]
        if has("attn"):
            plan += [norm(3), (attn_tensor, attn_scalar, attn_vector)]
        if has("out_o"):
            plan += [project("out_o")]
        if has("mlp1"):
            plan += [norm(4), mlp(1)]
        if has("ple1"):
            plan += [norm(5), ple(1)]
        if has("conv"):
            plan += [norm(6), (conv_tensor, conv_scalar, conv_vector)]
        if has("hgrn"):
            plan += [(hgrn_tensor, hgrn_scalar, hgrn_vector)]
        if has("out_ab"):
            plan += [project("out_ab", 0)]
        if has("mlp2"):
            plan += [norm(7), mlp(2, 0)]
        if has("stick"):
            plan += [norm(8), (stick_tensor, stick_scalar, stick_vector)]
        if has("out_c"):
            plan += [project("out_c", 1)]
        if has("mlp3"):
            plan += [norm(9), mlp(3, 1)]

        arena_at[0] = 0
        out_rows = take([NT, D])
        fin_pe = Steps(sem("fin_pe"), [f"b{i}" for i in range(8)])
        fin_act = Steps(sem("fin_act"), [f"b{i}" for i in range(8)])

        def finish_tensor(pe):
            for i in range(8):
                b, half = divmod(i, 2)
                if i >= 2:
                    pe.wait_ge(*fin_act.at(0, f"b{i - 2}"))
                for n in range(4):
                    last = nc.tensor.transpose(ps[2 + i % 2][:, n * P:(n + 1) * P],
                                               h[:, 4 * half + n, b * P:(b + 1) * P], ident[:, :])
                last.then_inc(*fin_pe(f"b{i}"))

        def finish_scalar(act):
            for i in range(8):
                b, half = divmod(i, 2)
                act.wait_ge(*fin_pe.at(0, f"b{i}"))
                nc.scalar.activation(out_rows[:, b, half * T:(half + 1) * T], ps[2 + i % 2][:, :],
                                     ACT.Copy).then_inc(*fin_act(f"b{i}"))

        def finish_sync(sp):
            for b in range(NT):
                sp.wait_ge(*fin_act.at(0, f"b{2 * b + 1}"))
                sp.dma_start(out[0][b * P:(b + 1) * P, :], out_rows[:, b, :]).then_inc(out_sent, 16)
            sp.wait_ge(out_sent, 16 * NT)

        plan += [(finish_tensor, finish_scalar, None)]
        block = ctx.enter_context(nc.Block())

        @block.sync
        def _(sp):
            setup_sync(sp)
            stream(sp)
            finish_sync(sp)

        @block.gpsimd
        def _(pool):
            setup_gpsimd(pool)
            cut_stream(pool)

        @block.tensor
        def _(pe):
            ph = Phases(pe, "pe")
            for phase in plan:
                ph.enter()
                if phase[0] is not None:
                    phase[0](pe)
                ph.leave()

        @block.scalar
        def _(act):
            ph = Phases(act, "act")
            for phase in plan:
                ph.enter()
                if phase[1] is not None:
                    phase[1](act)
                ph.leave()

        @block.vector
        def _(v):
            ph = Phases(v, "dve")
            for phase in plan:
                ph.enter()
                if phase[2] is not None:
                    phase[2](v)
                ph.leave()


_INS = ['x', 'p', 'ln_mix_e', 'w_in_e', 'gmlp_v_gain', 'gmlp_ws', 'gmlp_bs', 'gdn_conv', 'gdn_a_log', 'gdn_dt_bias',
        'gdn_out_gain', 'w_out_e', 'ln_mix_o', 'w_qkv_o', 'attn_q_gain', 'attn_k_gain', 'diff_lambda',
        'attn_sub_gain', 'w_out_o', 'ln_mlp', 'w_mlp1', 'w_mlp2', 'ln_ple', 'w_ple_gate', 'w_ple_proj', 'c_2',
        'ada_w_2', 'ada_b_2', 'norm_mix_2', 'norm_mlp_2', 'w_in_ab_2', 'conv_w_2', 'hg_norm_2', 'lb_logits_2',
        'w_out_ab_2', 'w_qkv_2', 'q_norm_2', 'k_norm_2', 'w_out_c_2', 'mlp_w1_2', 'mlp_w2_2']


def kernel(**inputs):
    import numpy as _np
    import concourse.bacc as _bacc
    from concourse import mybir as _mybir
    from concourse.bass_utils import run_bass_kernel_spmd as _run

    nc = _bacc.Bacc("TRN2", target_bir_lowering=False, num_devices=1)
    arrays, dram = {}, {}
    for name in _INS:
        a = _np.ascontiguousarray(inputs[name])
        arrays[f"in_{name}_dram"] = a
        dram[name] = nc.dram_tensor(f"in_{name}_dram", a.shape, _mybir.dt.from_np(a.dtype), kind="ExternalInput").ap()
    out = nc.dram_tensor("out_0_dram", (1, T, D), _mybir.dt.float32, kind="ExternalOutput").ap()
    program(nc, dram, out)
    r = _run(nc, [arrays], core_ids=[0])
    return r.results[0]["out_0_dram"]
```
